# Optimizing a Trainium2 kernel written in Bass

```python
import jax
import jax.numpy as jnp
from jax import lax
import numpy as np

D_MODEL = 1024
BATCH = 1
SEQ = 2048
DEPTH = 1

SWA_HEAD_DIM = 64
SWA_Q_HEADS = 8
SWA_KV_HEADS = 2
SWA_GROUP = SWA_Q_HEADS // SWA_KV_HEADS
WINDOW = 128
BAND_BLOCK = 128
RET_HEADS = 4
RET_QK_DIM = 128
RET_V_DIM = 256
RET_CHUNK = 128
ROPE_BASE = 10000.0
MEM_LEN = 256
MEM_HEADS = 4
MEM_HEAD_DIM = 128
N_BRANCH = 3
N_EXPERTS = 32
TOP_K = 4
D_FF = 1024
SWIGLU_LIMIT = 7.0
SWIGLU_ALPHA = 1.702
EPS = 1e-6
NEG_INF = -1e30

SWA_Q_W = SWA_Q_HEADS * SWA_HEAD_DIM
SWA_KV_W = SWA_KV_HEADS * SWA_HEAD_DIM
RET_QK_W = RET_HEADS * RET_QK_DIM
RET_V_W = RET_HEADS * RET_V_DIM
MEM_W = MEM_HEADS * MEM_HEAD_DIM
IN_SIZES = (SWA_Q_W, SWA_KV_W, SWA_KV_W, RET_QK_W, RET_QK_W, RET_V_W, RET_V_W, MEM_W, N_BRANCH * D_MODEL)
IN_WIDTH = sum(IN_SIZES)

kernel_name = "hybrid_swa_retention_memory_moe_block"

def rms_norm(x, w):
    xf = x.astype(jnp.float32)
    y = xf * lax.rsqrt(jnp.mean(xf * xf, axis=-1, keepdims=True) + EPS)
    return (y * w.astype(jnp.float32)).astype(x.dtype)

def head_layer_norm(t, w):
    mu = jnp.mean(t, axis=-1, keepdims=True)
    tc = t - mu
    var = jnp.mean(tc * tc, axis=-1, keepdims=True)
    return tc * lax.rsqrt(var + EPS) * w.astype(jnp.float32)

def split_cols(z, sizes):
    outs = []
    off = 0
    for s in sizes:
        outs.append(z[..., off:off + s])
        off += s
    return outs

def rotary(t):
    S, d = t.shape[1], t.shape[-1]
    half = d // 2
    inv = 1.0 / (ROPE_BASE ** (jnp.arange(0, half, dtype=jnp.float32) / half))
    ang = jnp.arange(S, dtype=jnp.float32)[:, None] * inv[None, :]
    cos = jnp.cos(ang)[None, :, None, :]
    sin = jnp.sin(ang)[None, :, None, :]
    tf = t.astype(jnp.float32)
    t1, t2 = tf[..., :half], tf[..., half:]
    return jnp.concatenate([t1 * cos - t2 * sin, t1 * sin + t2 * cos], axis=-1).astype(t.dtype)

def sliding_window_attention(q, k, v, sinks):
    B, S = q.shape[0], q.shape[1]
    nb = S // BAND_BLOCK
    qb = q.reshape(B, nb, BAND_BLOCK, SWA_KV_HEADS, SWA_GROUP, SWA_HEAD_DIM)

    def band(t):
        tp = jnp.pad(t, ((0, 0), (BAND_BLOCK, 0), (0, 0), (0, 0)))
        tb = tp.reshape(B, nb + 1, BAND_BLOCK, SWA_KV_HEADS, SWA_HEAD_DIM)
        return jnp.concatenate([tb[:, :-1], tb[:, 1:]], axis=2)

    kb, vb = band(k), band(v)
    scores = jnp.einsum('bnqhgd,bnkhd->bnhgqk', qb, kb,
                        preferred_element_type=jnp.float32) * (SWA_HEAD_DIM ** -0.5)
    qi = jnp.arange(BAND_BLOCK)[:, None]
    kj = jnp.arange(2 * BAND_BLOCK)[None, :]
    diff = BAND_BLOCK + qi - kj
    in_win = (diff >= 0) & (diff < WINDOW)
    not_pad = (jnp.arange(nb) > 0)[:, None, None] | (kj >= BAND_BLOCK)[None]
    mask = in_win[None] & not_pad
    scores = jnp.where(mask[None, :, None, None], scores, NEG_INF)
    sink = jnp.broadcast_to(sinks.astype(jnp.float32).reshape(1, 1, SWA_KV_HEADS, SWA_GROUP, 1, 1),
                            scores.shape[:-1] + (1,))
    probs = jax.nn.softmax(jnp.concatenate([scores, sink], axis=-1), axis=-1)[..., :-1]
    out = jnp.einsum('bnhgqk,bnkhd->bnqhgd', probs.astype(v.dtype), vb)
    return out.reshape(B, S, SWA_Q_HEADS * SWA_HEAD_DIM)

def retention(q, k, v):
    B, S = q.shape[0], q.shape[1]
    L = RET_CHUNK
    nc = S // L
    log_g = jnp.log1p(-(2.0 ** (-5.0 - jnp.arange(RET_HEADS, dtype=jnp.float32))))
    pos = jnp.arange(L, dtype=jnp.float32)
    diff = pos[:, None] - pos[None, :]
    decay_mask = jnp.where(diff[None] >= 0,
                           jnp.exp(jnp.maximum(diff, 0.0)[None] * log_g[:, None, None]), 0.0)
    q_decay = jnp.exp((pos[None, :] + 1.0) * log_g[:, None])[..., None]
    k_decay = jnp.exp((L - 1.0 - pos[None, :]) * log_g[:, None])[..., None]
    chunk_decay = jnp.exp(L * log_g)[:, None, None]

    def chunks(t):
        d = t.shape[-1]
        return t.astype(jnp.float32).reshape(B, nc, L, RET_HEADS, d).transpose(1, 0, 3, 2, 4)

    qc, kc, vc = chunks(q), chunks(k), chunks(v)

    def step(state, inp):
        qi, ki, vi = inp
        inner = jnp.einsum('bhld,bhmd->bhlm', qi, ki) * decay_mask[None]
        o = jnp.einsum('bhlm,bhme->bhle', inner, vi) + \
            jnp.einsum('bhld,bhde->bhle', qi * q_decay[None], state)
        state = state * chunk_decay[None] + jnp.einsum('bhld,bhle->bhde', ki * k_decay[None], vi)
        return state, o

    state0 = jnp.zeros((B, RET_HEADS, RET_QK_DIM, RET_V_DIM), jnp.float32)
    _, o = lax.scan(step, state0, (qc, kc, vc))
    return o.transpose(1, 0, 3, 2, 4).reshape(B, S, RET_HEADS, RET_V_DIM)

def memory_attention(q, mk, mv):
    B, S = q.shape[0], q.shape[1]
    s = jnp.einsum('bshd,bmhd->bhsm', q, mk, preferred_element_type=jnp.float32) * (MEM_HEAD_DIM ** -0.5)
    p = jax.nn.softmax(s, axis=-1)
    o = jnp.einsum('bhsm,bmhd->bshd', p.astype(mv.dtype), mv)
    return o.reshape(B, S, MEM_W)

def routed_experts(h, w_router, b_router, w_up, b_up, w_down, b_down):
    B, S, D = h.shape
    T = B * S
    ht = h.reshape(T, D)
    logits = (ht @ w_router + b_router).astype(jnp.float32)
    top_vals, top_idx = lax.top_k(logits, TOP_K)
    gate = jax.nn.softmax(top_vals, axis=-1)
    flat_e = top_idx.reshape(-1)
    order = jnp.argsort(flat_e)
    e_sorted = flat_e[order]
    tok = order // TOP_K
    xs = ht[tok]
    group_sizes = jnp.bincount(flat_e, length=N_EXPERTS).astype(jnp.int32)
    hid = lax.ragged_dot(xs, w_up, group_sizes) + b_up[e_sorted]
    x_glu = jnp.minimum(hid[:, 0::2], SWIGLU_LIMIT)
    x_lin = jnp.clip(hid[:, 1::2], -SWIGLU_LIMIT, SWIGLU_LIMIT)
    act = x_glu * jax.nn.sigmoid(SWIGLU_ALPHA * x_glu) * (x_lin + 1.0)
    out = lax.ragged_dot(act, w_down, group_sizes) + b_down[e_sorted]
    out = out * gate.reshape(-1)[order][:, None].astype(out.dtype)
    y = jnp.zeros_like(ht).at[tok].add(out)
    return y.reshape(B, S, D)

def setup_inputs(seed: int = 0) -> dict:
    key = jax.random.key(seed)
    ks = jax.random.split(key, 23)
    f32 = jnp.float32
    L, D = DEPTH, D_MODEL

    def nrm(k, shape, scale):
        return jax.random.normal(k, shape, f32) * scale

    def gain(k, shape):
        return 1.0 + 0.05 * jax.random.normal(k, shape, f32)

    return {
        'x': nrm(ks[0], (BATCH, SEQ, D), 1.0),
        'mem': nrm(ks[1], (BATCH, MEM_LEN, D), 1.0),
        'mix_norm_w': gain(ks[2], (L, D)),
        'mem_norm_w': gain(ks[3], (L, D)),
        'w_in': nrm(ks[4], (L, D, IN_WIDTH), D ** -0.5),
        'swa_q_norm_w': gain(ks[5], (L, SWA_HEAD_DIM)),
        'swa_k_norm_w': gain(ks[6], (L, SWA_HEAD_DIM)),
        'swa_sinks': nrm(ks[7], (L, SWA_Q_HEADS), 0.5),
        'ret_norm_w': gain(ks[8], (L, RET_V_W)),
        'w_mem_kv': nrm(ks[9], (L, D, 2 * MEM_W), D ** -0.5),
        'mem_q_norm_w': gain(ks[10], (L, MEM_HEAD_DIM)),
        'mem_k_norm_w': gain(ks[11], (L, MEM_HEAD_DIM)),
        'w_br_swa': nrm(ks[12], (L, SWA_Q_W, D), SWA_Q_W ** -0.5),
        'w_br_ret': nrm(ks[13], (L, RET_V_W, D), RET_V_W ** -0.5),
        'w_br_mem': nrm(ks[14], (L, MEM_W, D), MEM_W ** -0.5),
        'w_out': nrm(ks[15], (L, D, D), D ** -0.5),
        'ffn_norm_w': gain(ks[16], (L, D)),
        'w_router': nrm(ks[17], (L, D, N_EXPERTS), D ** -0.5),
        'b_router': nrm(ks[18], (L, N_EXPERTS), 0.01),
        'w_up': nrm(ks[19], (L, N_EXPERTS, D, 2 * D_FF), D ** -0.5),
        'b_up': nrm(ks[20], (L, N_EXPERTS, 2 * D_FF), 0.01),
        'w_down': nrm(ks[21], (L, N_EXPERTS, D_FF, D), D_FF ** -0.5),
        'b_down': nrm(ks[22], (L, N_EXPERTS, D), 0.01),
    }

def reference(x, mem, mix_norm_w, mem_norm_w, w_in, swa_q_norm_w, swa_k_norm_w, swa_sinks,
              ret_norm_w, w_mem_kv, mem_q_norm_w, mem_k_norm_w, w_br_swa, w_br_ret, w_br_mem,
              w_out, ffn_norm_w, w_router, b_router, w_up, b_up, w_down, b_down):
    B, S, D = x.shape
    for l in range(DEPTH):
        h = rms_norm(x, mix_norm_w[l])
        z = h @ w_in[l]
        sq, sk, sv, rq, rk, rv, rg, mq, zg = split_cols(z, IN_SIZES)

        sq = rms_norm(sq.reshape(B, S, SWA_Q_HEADS, SWA_HEAD_DIM), swa_q_norm_w[l])
        sk = rms_norm(sk.reshape(B, S, SWA_KV_HEADS, SWA_HEAD_DIM), swa_k_norm_w[l])
        sv = sv.reshape(B, S, SWA_KV_HEADS, SWA_HEAD_DIM)
        o_swa = sliding_window_attention(sq, sk, sv, swa_sinks[l])

        rq = rotary(rq.reshape(B, S, RET_HEADS, RET_QK_DIM))
        rk = rotary(rk.reshape(B, S, RET_HEADS, RET_QK_DIM)) * (RET_QK_DIM ** -0.5)
        rv = rv.reshape(B, S, RET_HEADS, RET_V_DIM)
        o_ret = head_layer_norm(retention(rq, rk, rv), ret_norm_w[l].reshape(RET_HEADS, RET_V_DIM))
        o_ret = jax.nn.silu(rg) * o_ret.reshape(B, S, RET_V_W).astype(x.dtype)

        m = rms_norm(mem, mem_norm_w[l])
        mk, mv = split_cols(m @ w_mem_kv[l], (MEM_W, MEM_W))
        M = mem.shape[1]
        mq = rms_norm(mq.reshape(B, S, MEM_HEADS, MEM_HEAD_DIM), mem_q_norm_w[l])
        mk = rms_norm(mk.reshape(B, M, MEM_HEADS, MEM_HEAD_DIM), mem_k_norm_w[l])
        mv = mv.reshape(B, M, MEM_HEADS, MEM_HEAD_DIM)
        o_mem = memory_attention(mq, mk, mv)

        gates = jax.nn.sigmoid(zg).reshape(B, S, N_BRANCH, D)
        merged = (gates[:, :, 0] * (o_swa @ w_br_swa[l])
                  + gates[:, :, 1] * (o_ret @ w_br_ret[l])
                  + gates[:, :, 2] * (o_mem @ w_br_mem[l]))
        x = x + merged @ w_out[l]

        h2 = rms_norm(x, ffn_norm_w[l])
        x = x + routed_experts(h2, w_router[l], b_router[l], w_up[l], b_up[l], w_down[l], b_down[l])
    return x


_drawn_inputs = setup_inputs


def setup_inputs(seed=0):
    import zlib

    import numpy as np

    out = dict(_drawn_inputs(seed))
    spreads = {}
    factors = {'mem_norm_w': 3.348,
     'swa_sinks': 200.0,
     'mem_q_norm_w': 3.152,
     'mem_k_norm_w': 3.4,
     'b_up': 8.0,
     'b_down': 23.331,
     'swa_q_norm_w': 5.868,
     'swa_k_norm_w': 6.235,
     'ret_norm_w': 3.172,
     'b_router': 2.689}
    for name, (base, spread) in spreads.items():
        noise = np.random.default_rng([zlib.crc32(name.encode()), seed]).standard_normal(out[name].shape)
        drawn = base * np.exp(spread * noise) if base else spread * noise
        out[name] = jnp.asarray(drawn.astype(out[name].dtype))
    for name, factor in factors.items():
        out[name] = (out[name] * factor).astype(out[name].dtype)
    return out
```

```python
from contextlib import ExitStack

import numpy as np

import concourse.bass as bass
from concourse import mybir

F32 = mybir.dt.float32
F32R = mybir.dt.float32r
I32 = mybir.dt.int32
U32 = mybir.dt.uint32
ALU = mybir.AluOpType
ACT = mybir.ActivationFunctionType
AX = mybir.AxisListType.X

P = 128
D = 1024
S = 2048
KD = D // P
TILES = S // P
EPS = 1e-6
NEG = -1e30

SWA_H, SWA_KV, SWA_D = 8, 2, 64
RET_H, RET_DK, RET_DV = 4, 128, 256
MEM_H, MEM_D, MEM_LEN = 4, 128, 256
E, TOPK, FF = 32, 4, 1024
LIMIT, ALPHA = 7.0, 1.702

SQ0 = 0
SK0 = SQ0 + SWA_H * SWA_D
SV0 = SK0 + SWA_KV * SWA_D
RQ0 = SV0 + SWA_KV * SWA_D
RK0 = RQ0 + RET_H * RET_DK
RV0 = RK0 + RET_H * RET_DK
RG0 = RV0 + RET_H * RET_DV
MQ0 = RG0 + RET_H * RET_DV
ZG0 = MQ0 + MEM_H * MEM_D
ZW = ZG0 + 3 * D

PAD = P


class Signal:

    def __init__(self, sems, nc, name, per=1, ahead=0):
        self.sem = nc.alloc_semaphore(name=name)
        sems.append(self.sem)
        self.per, self.ahead = per, ahead

    def open(self, eng):
        eng.sem_inc(self.sem, self.ahead * self.per)

    def after(self, t, j=None):
        return (t + self.ahead) * self.per + (self.per if j is None else j)


def stand(eng, idle):
    eng.sem_inc(idle.sem, 1)


def end_stage(nc, sems):
    nc.clear_and_free_semaphores(sems)
    sems.clear()
    nc.all_engine_barrier()


def at_first(p):
    return isinstance(p, int)


def peeled(eng, n):
    yield 0
    with eng.Fori(1, n) as p:
        yield p


def ds(start, size):
    return bass.ds(start, size)


def below(nc, value, end):
    return nc.s_assert_within(value, 0, end - 1, skip_runtime_bounds_check_because="a branch on the loop register keeps it")


def norm_inputs(nc, io, hT_hi, hT_lo, ident, eps):
    with ExitStack() as c:
        xs = [c.enter_context(nc.sbuf_tensor(f"n_x{i}", [P, D], F32)) for i in range(2)]
        sq = c.enter_context(nc.sbuf_tensor("n_sq", [P, D], F32))
        hn = [c.enter_context(nc.sbuf_tensor(f"n_h{i}", [P, D], F32)) for i in range(2)]
        wb = c.enter_context(nc.sbuf_tensor("n_w", [P, D], F32))
        ss = c.enter_context(nc.sbuf_tensor("n_ss", [P, 2], F32))
        rs = c.enter_context(nc.sbuf_tensor("n_rs", [P, 2], F32))
        pt = [c.enter_context(nc.psum_tensor(f"n_pt{i}", [P, D], F32)) for i in range(2)]
        w_in_sb = Signal(io["sems"], nc, "n_w_in", 16)
        x_in = [Signal(io["sems"], nc, f"n_x_in{i}", 16) for i in range(2)]
        ident_made = Signal(io["sems"], nc, "n_ident")
        squared = Signal(io["sems"], nc, "n_squared", 1, 1)
        rooted = Signal(io["sems"], nc, "n_rooted")
        rstd = Signal(io["sems"], nc, "n_rstd")
        normed = Signal(io["sems"], nc, "n_normed", 1, 2)
        turned = Signal(io["sems"], nc, "n_turned", 1, 2)
        hi_made = Signal(io["sems"], nc, "n_hi", 1)
        lo_made = Signal(io["sems"], nc, "n_lo", 1, 2)
        blk = c.enter_context(nc.Block())

        @blk.sync
        def _(sp):
            sp.dma_start(wb[:], io["mix_norm_w"].to_broadcast([P, D])).then_inc(w_in_sb.sem, 16)
            with sp.Fori(0, TILES // 2) as p:
                for i in range(2):
                    t = 2 * p + i
                    sp.wait_ge(normed.sem, normed.after(t - 2))
                    sp.dma_start(xs[i][:], io["x"][ds(t * P, P), :]).then_inc(x_in[i].sem, 16)

        @blk.gpsimd
        def _(pool):
            make_identity(pool, ident, ident_made)
            pool.memset(eps[:], EPS).then_inc(ident_made.sem, 1)

        @blk.scalar
        def _(act):
            squared.open(act)
            act.wait_ge(ident_made.sem, 3)
            with act.Fori(0, TILES // 2) as p:
                for i in range(2):
                    t = 2 * p + i
                    act.wait_ge(x_in[i].sem, x_in[i].after(p))
                    act.wait_ge(squared.sem, squared.after(t - 1))
                    act.activation(sq[:], xs[i][:], ACT.Square,
                                   accum_out=ss[:, i:i + 1]).then_inc(squared.sem, 1)
                    act.wait_ge(squared.sem, squared.after(t))
                    act.activation(rs[:, i:i + 1], ss[:, i:i + 1], ACT.Sqrt, scale=1.0 / D,
                                   bias=eps[:, 0:1]).then_inc(rooted.sem, 1)
                    act.wait_ge(turned.sem, turned.after(t))
                    act.copy(hT_hi[:, :, ds(t * P, P)],
                             pt[i][:].rearrange("p (k n) -> p k n", k=KD)).then_inc(hi_made.sem, 1)

        @blk.vector
        def _(dve):
            normed.open(dve)
            lo_made.open(dve)
            dve.wait_ge(w_in_sb.sem, 16)

            def norm(t, i):
                dve.wait_ge(rooted.sem, rooted.after(t))
                dve.reciprocal(rs[:, i:i + 1], rs[:, i:i + 1]).then_inc(rstd.sem, 1)
                dve.wait_ge(rstd.sem, rstd.after(t))
                dve.wait_ge(turned.sem, turned.after(t - 2))
                dve.scalar_tensor_tensor(out=hn[i][:], in0=xs[i][:], scalar=rs[:, i:i + 1], in1=wb[:],
                                         op0=ALU.mult, op1=ALU.mult).then_inc(normed.sem, 1)

            with dve.Fori(0, TILES // 2) as p:
                for i in range(2):
                    t = 2 * p + i
                    norm(t, i)
                    dve.wait_ge(turned.sem, turned.after(t))
                    dve.wait_ge(hi_made.sem, hi_made.after(t))
                    dve.tensor_tensor(hT_lo[:, :, ds(t * P, P)],
                                      pt[i][:].rearrange("p (k n) -> p k n", k=KD),
                                      hT_hi[:, :, ds(t * P, P)].bitcast(F32),
                                      ALU.subtract).then_inc(lo_made.sem, 1)

        @blk.tensor
        def _(pe):
            turned.open(pe)
            pe.wait_ge(ident_made.sem, 2)
            with pe.Fori(0, TILES // 2) as p:
                for i in range(2):
                    t = 2 * p + i
                    pe.wait_ge(normed.sem, normed.after(t))
                    pe.wait_ge(lo_made.sem, lo_made.after(t - 2))
                    for k in range(KD):
                        mm = pe.transpose(pt[i][:, k * P:(k + 1) * P], hn[i][:, k * P:(k + 1) * P], ident[:])
                    mm.then_inc(turned.sem, 1)


def make_identity(pool, ident, made):
    pool.memset(ident[:], 0.0).then_inc(made.sem, 1)
    pool.wait_ge(made.sem, 1)
    pool.affine_select(out=ident[:], in_=ident[:], compare_op=ALU.not_equal, fill=1.0, base=0,
                       pattern=[[-1, P]], channel_multiplier=1).then_inc(made.sem, 1)


def three_pass(pe, out, x_hi, x_lo, w_hi, w_lo, chunks):
    for k in chunks:
        first, last = k == chunks[0], k == chunks[-1]
        pe.matmul(out, x_hi(k), w_hi(k), start=first, stop=False)
        pe.matmul(out, x_hi(k), w_lo(k), start=False, stop=False)
        mm = pe.matmul(out, x_lo(k), w_hi(k), start=False, stop=last)
    return mm


def project_inputs(nc, io, hT_hi, hT_lo):
    GROUPS = 16
    G = ZW // GROUPS
    RAW, BANKS, OUTS = 4, 8, 4
    with ExitStack() as c:
        raw = [c.enter_context(nc.sbuf_tensor(f"p_raw{i}", [P, G], F32)) for i in range(RAW)]
        w_hi = [c.enter_context(nc.sbuf_tensor(f"p_hi{i}", [P, KD, G], F32R)) for i in range(2)]
        w_lo = [c.enter_context(nc.sbuf_tensor(f"p_lo{i}", [P, KD, G], F32R)) for i in range(2)]
        zs = [c.enter_context(nc.sbuf_tensor(f"p_z{i}", [P, G], F32)) for i in range(OUTS)]
        acc = [c.enter_context(nc.psum_tensor(f"p_acc{i}", [P, 512], F32)) for i in range(BANKS)]
        raw_in = [Signal(io["sems"], nc, f"p_raw_in{i}", 16 * KD // RAW) for i in range(RAW)]
        hi_made = Signal(io["sems"], nc, "p_hi_made", KD)
        lo_made = Signal(io["sems"], nc, "p_lo_made", KD, 1)
        summed = Signal(io["sems"], nc, "p_summed", TILES, 2)
        copied = Signal(io["sems"], nc, "p_copied", TILES, 1)
        z_out = [Signal(io["sems"], nc, f"p_z_out{i}", 16 * TILES // OUTS, 1) for i in range(OUTS)]
        blk = c.enter_context(nc.Block())

        @blk.sync
        def _(sp):
            def load(g, k):
                sp.wait_ge(lo_made.sem, lo_made.after(g, k + 1 - RAW))
                sp.dma_start(raw[k % RAW][:], io["w_in"][k * P:(k + 1) * P, ds(g * G, G)]).then_inc(
                    raw_in[k % RAW].sem, 16)

            for z in z_out:
                z.open(sp)
            for k in range(KD):
                load(0, k)
            with sp.Fori(0, GROUPS // 2) as p:
                for b in range(2):
                    g = 2 * p + b

                    def load_next():
                        for k in range(KD):
                            load(below(nc, g + 1, GROUPS), k)

                    if b == 0:
                        load_next()
                    else:
                        with sp.If(p < GROUPS // 2 - 1):
                            load_next()
                    for i in range(TILES):
                        sp.wait_ge(copied.sem, copied.after(g, i + 1))
                        sp.dma_start(io["z"][i * P:(i + 1) * P, ds(g * G, G)],
                                     zs[i % OUTS][:]).then_inc(z_out[i % OUTS].sem, 16)
            for z in z_out:
                sp.wait_ge(z.sem, z.after(GROUPS - 1))

        @blk.scalar
        def _(act):
            copied.open(act)

            def split(g, k, b):
                act.wait_ge(raw_in[k % RAW].sem, raw_in[k % RAW].after(g, 16 * (k // RAW + 1)))
                act.wait_ge(summed.sem, summed.after(g - 2))
                act.copy(w_hi[b][:, k, :], raw[k % RAW][:]).then_inc(hi_made.sem, 1)

            for k in range(KD):
                split(0, k, 0)
            with act.Fori(0, GROUPS // 2) as p:
                for b in range(2):
                    g = 2 * p + b

                    def split_next():
                        for k in range(KD):
                            split(g + 1, k, 1 - b)

                    if b == 0:
                        split_next()
                    else:
                        with act.If(p < GROUPS // 2 - 1):
                            split_next()
                    for i in range(TILES):
                        act.wait_ge(summed.sem, summed.after(g, i + 1))
                        j = 16 * (i // OUTS)
                        act.wait_ge(z_out[i % OUTS].sem, z_out[i % OUTS].after(g, j))
                        act.copy(zs[i % OUTS][:], acc[i % BANKS][:, 0:G]).then_inc(copied.sem, 1)

        @blk.vector
        def _(dve):
            lo_made.open(dve)

            def split(g, k, b):
                dve.wait_ge(hi_made.sem, hi_made.after(g, k + 1))
                dve.tensor_tensor(w_lo[b][:, k, :], raw[k % RAW][:], w_hi[b][:, k, :].bitcast(F32),
                                  ALU.subtract).then_inc(lo_made.sem, 1)

            for k in range(KD):
                split(0, k, 0)
            with dve.Fori(0, GROUPS // 2) as p:
                for b in range(2):
                    def split_next():
                        for k in range(KD):
                            split(2 * p + b + 1, k, 1 - b)

                    if b == 0:
                        split_next()
                    else:
                        with dve.If(p < GROUPS // 2 - 1):
                            split_next()

        @blk.tensor
        def _(pe):
            summed.open(pe)
            with pe.Fori(0, GROUPS // 2) as p:
                for b in range(2):
                    g = 2 * p + b
                    pe.wait_ge(lo_made.sem, lo_made.after(g))
                    for i in range(TILES):
                        pe.wait_ge(copied.sem, copied.after(g, i + 1 - BANKS))
                        rows = slice(i * P, (i + 1) * P)
                        three_pass(pe, acc[i % BANKS][:, 0:G],
                                   lambda k: hT_hi[:, k, rows], lambda k: hT_lo[:, k, rows],
                                   lambda k: w_hi[b][:, k, :], lambda k: w_lo[b][:, k, :],
                                   range(KD)).then_inc(summed.sem, 1)
def prepare_memory(nc, io, ident, eps, mkT, mv):
    MT = MEM_LEN // P
    W = MEM_H * MEM_D
    with ExitStack() as c:
        ms_in = c.enter_context(nc.sbuf_tensor("m_x", [P, MT, D], F32))
        wkv = c.enter_context(nc.sbuf_tensor("m_wkv", [P, KD, 2 * W], F32))
        wb = c.enter_context(nc.sbuf_tensor("m_w", [P, D], F32))
        kw = c.enter_context(nc.sbuf_tensor("m_kw", [P, 1], F32))
        kws = c.enter_context(nc.sbuf_tensor("m_kws", [P, 1], F32))
        sq = c.enter_context(nc.sbuf_tensor("m_sq", [P, MT, D], F32))
        hn = c.enter_context(nc.sbuf_tensor("m_h", [P, MT, D], F32))
        hT = c.enter_context(nc.sbuf_tensor("m_hT", [P, MT, D], F32))
        mk = c.enter_context(nc.sbuf_tensor("m_k", [P, MT, W], F32))
        ss = c.enter_context(nc.sbuf_tensor("m_ss", [P, MT], F32))
        ks = c.enter_context(nc.sbuf_tensor("m_ks", [P, MT * MEM_H], F32))
        pt = [c.enter_context(nc.psum_tensor(f"m_pt{i}", [P, D], F32)) for i in range(MT)]
        pk = [c.enter_context(nc.psum_tensor(f"m_pk{i}", [P, 2 * W], F32)) for i in range(MT)]
        loaded = Signal(io["sems"], nc, "m_loaded", 16)
        squared = Signal(io["sems"], nc, "m_squared")
        rooted = Signal(io["sems"], nc, "m_rooted")
        normed = Signal(io["sems"], nc, "m_normed")
        turned = Signal(io["sems"], nc, "m_turned")
        hT_made = Signal(io["sems"], nc, "m_hT_made")
        summed = Signal(io["sems"], nc, "m_summed")
        k_squared = Signal(io["sems"], nc, "m_k_squared")
        k_rooted = Signal(io["sems"], nc, "m_k_rooted")
        k_normed = Signal(io["sems"], nc, "m_k_normed")
        k_turned = Signal(io["sems"], nc, "m_k_turned")
        made = Signal(io["sems"], nc, "m_made")
        steps = Signal(io["sems"], nc, "m_steps")
        blk = c.enter_context(nc.Block())

        @blk.sync
        def _(sp):
            sp.dma_start(ms_in[:], io["mem"].rearrange("(m p) d -> p m d", p=P)).then_inc(loaded.sem, 16)
            sp.dma_start(wb[:], io["mem_norm_w"].to_broadcast([P, D])).then_inc(loaded.sem, 16)
            sp.dma_start(kw[:], io["mem_k_norm_w"].rearrange("a (p o) -> (a p) o", o=1)).then_inc(loaded.sem, 16)
            sp.dma_start(wkv[:], io["w_mem_kv"].rearrange("(k p) n -> p k n", p=P)).then_inc(loaded.sem, 16)

        @blk.scalar
        def _(act):
            act.wait_ge(loaded.sem, 64)
            for m in range(MT):
                act.activation(sq[:, m, :], ms_in[:, m, :], ACT.Square,
                               accum_out=ss[:, m:m + 1]).then_inc(squared.sem, 1)
            act.wait_ge(squared.sem, MT)
            act.activation(ss[:], ss[:], ACT.Sqrt, scale=1.0 / D, bias=eps[:, 0:1]).then_inc(rooted.sem, 1)
            for m in range(MT):
                act.wait_ge(turned.sem, m + 1)
                act.copy(hT[:, m, :], pt[m][:]).then_inc(hT_made.sem, 1)
            for m in range(MT):
                act.wait_ge(summed.sem, m + 1)
                for h in range(MEM_H):
                    cols = slice(h * MEM_D, (h + 1) * MEM_D)
                    act.activation(sq[:, m, cols], pk[m][:, cols], ACT.Square,
                                   accum_out=ks[:, m * MEM_H + h:m * MEM_H + h + 1]).then_inc(k_squared.sem, 1)
            act.wait_ge(k_squared.sem, MT * MEM_H)
            act.activation(ks[:], ks[:], ACT.Sqrt, scale=1.0 / MEM_D, bias=eps[:, 0:1]).then_inc(k_rooted.sem, 1)

        @blk.vector
        def _(dve):
            dve.wait_ge(rooted.sem, 1)
            dve.reciprocal(ss[:], ss[:]).then_inc(steps.sem, 1)
            dve.wait_ge(steps.sem, 1)
            for m in range(MT):
                dve.scalar_tensor_tensor(out=hn[:, m, :], in0=ms_in[:, m, :], scalar=ss[:, m:m + 1],
                                         in1=wb[:], op0=ALU.mult, op1=ALU.mult).then_inc(normed.sem, 1)
            dve.tensor_scalar(kws[:], kw[:], float(MEM_D) ** -0.5, None, ALU.mult).then_inc(steps.sem, 1)
            dve.wait_ge(k_rooted.sem, 1)
            dve.reciprocal(ks[:], ks[:]).then_inc(steps.sem, 1)
            dve.wait_ge(steps.sem, 3)
            for m in range(MT):
                dve.wait_ge(summed.sem, m + 1)
                dve.tensor_tensor(mk[:, m, :].rearrange("p (h d) -> p h d", h=MEM_H),
                                  pk[m][:, 0:W].rearrange("p (h d) -> p h d", h=MEM_H),
                                  ks[:, m * MEM_H:(m + 1) * MEM_H].unsqueeze(2).to_broadcast([P, MEM_H, MEM_D]),
                                  ALU.mult).then_inc(k_normed.sem, 1)
                dve.tensor_copy(mv[:, m, :], pk[m][:, W:2 * W]).then_inc(made.sem, 1)
            for m in range(MT):
                dve.wait_ge(k_turned.sem, m + 1)
                dve.tensor_scalar(mkT[:, :, m * P:(m + 1) * P],
                                  pt[m][:, 0:W].rearrange("p (h n) -> p h n", h=MEM_H), kws[:, 0:1], None,
                                  ALU.mult).then_inc(made.sem, 1)

        @blk.tensor
        def _(pe):
            for m in range(MT):
                pe.wait_ge(normed.sem, m + 1)
                for k in range(KD):
                    mm = pe.transpose(pt[m][:, k * P:(k + 1) * P], hn[:, m, k * P:(k + 1) * P], ident[:])
                mm.then_inc(turned.sem, 1)
            for m in range(MT):
                pe.wait_ge(hT_made.sem, m + 1)
                for n in range(2):
                    for k in range(KD):
                        mm = pe.matmul(pk[m][:, n * W:(n + 1) * W], hT[:, m, k * P:(k + 1) * P],
                                       wkv[:, k, n * W:(n + 1) * W], start=(k == 0), stop=(k == KD - 1))
                mm.then_inc(summed.sem, 1)
            for m in range(MT):
                pe.wait_ge(k_normed.sem, m + 1)
                for h in range(MEM_H):
                    mm = pe.transpose(pt[m][:, h * P:(h + 1) * P], mk[:, m, h * MEM_D:(h + 1) * MEM_D], ident[:])
                mm.then_inc(k_turned.sem, 1)


class Region:

    def __init__(self, ctx, sems, nc, name, banks, uses):
        self.ps = ctx.enter_context(nc.psum_tensor(f"{name}_ps", [P, banks * 512], F32))
        self.filled = Signal(sems, nc, f"{name}_filled", uses)
        self.taken = Signal(sems, nc, f"{name}_taken", uses, 1)

    def wait_free(self, pe, t, use):
        pe.wait_ge(self.taken.sem, self.taken.after(t, use))

    def wait_filled(self, eng, t, use):
        eng.wait_ge(self.filled.sem, self.filled.after(t, use + 1))


def mix_tokens(nc, io, ident, eps, mkT, mv):
    NH = SWA_H + SWA_KV
    QK = NH * SWA_D
    MW = MEM_H * MEM_D
    RQ = RET_H * RET_DK
    RV = RET_H * RET_DV
    HALF = RET_DK // 2
    lg = np.log1p(-(2.0 ** (-5.0 - np.arange(RET_H, dtype=np.float32)))).astype(np.float32)
    chunk_decay = [float(np.exp(np.float32(P) * g)) for g in lg]
    with ExitStack() as c:
        def sb(name, cols, n=1):
            got = [c.enter_context(nc.sbuf_tensor(f"x_{name}{i}", [P, cols], F32)) for i in range(n)]
            return got if n > 1 else got[0]

        zt = sb("z", ZG0, 2)
        rope = sb("rope", 4 * HALF, 2)
        oT = sb("oT", 16 * P, 2)
        kT, vals = sb("kT", P, 2), sb("vals", P, 2)
        sq, ss, rstd = sb("sq", QK + MW), sb("ss", NH + MEM_H), sb("rstd", NH + MEM_H)
        qn, mqn = sb("qn", QK), sb("mqn", MW)
        qc, qs, kc, ks = sb("qc", RQ), sb("qs", RQ), sb("kc", RQ), sb("ks", RQ)
        rqn, rkn, rkd = sb("rqn", RQ), sb("rkn", RQ), sb("rkd", RQ)
        qT, mqT, rqT, rqdT, rkT = sb("qT", 4 * P), sb("mqT", MW), sb("rqT", RQ), sb("rqdT", RQ), sb("rkT", RQ)
        probs, probsT = sb("probs", SWA_H * 2 * P), sb("probsT", SWA_H * 2 * P)
        mprobs, mprobsT = sb("mprobs", MEM_H * MEM_LEN), sb("mprobsT", MEM_H * MEM_LEN)
        inT = sb("inT", RET_H * P)
        state = sb("state", RV)
        gexp, gate, rgw, rnorm = sb("gexp", RV), sb("gate", RV), sb("rgw", RV), sb("rnorm", RV)
        decayT, qdec, kdec = sb("decayT", RET_H * P), sb("qdec", RET_H * P), sb("kdec", RET_H)
        mask = sb("mask", 2 * P)
        mask_now = sb("mask_now", 2 * P)
        sinks, wq, wk, wm, wret = sb("sinks", SWA_H), sb("wq", 1), sb("wk", 1), sb("wm", 1), sb("wret", RV)
        mx, neg, sk, rsum, rinv = (sb(n, SWA_H) for n in ("mx", "neg", "sk", "rsum", "rinv"))
        mmx, mneg, mrsum, mrinv = (sb(n, MEM_H) for n in ("mmx", "mneg", "mrsum", "mrinv"))
        st, mva, rr = sb("st", RET_H * 6), sb("mva", RET_H * 2), sb("rr", RET_H)

        RA = Region(c, io["sems"], nc, "ra", 2, 5)
        RB = Region(c, io["sems"], nc, "rb", 2, 3)
        RE = Region(c, io["sems"], nc, "re", 2, 1)
        RC = Region(c, io["sems"], nc, "rc", 1, 5)
        RD = Region(c, io["sems"], nc, "rd", 1, 3)

        def sig(name, per=1, ahead=0):
            return Signal(io["sems"], nc, f"x_{name}", per, ahead)

        consts_in, idle = sig("consts_in", 16), sig("idle")
        z_in = [sig(f"z_in{i}", 32) for i in range(2)]
        o_out = [sig(f"o_out{i}", 16, 1) for i in range(2)]
        prepared = sig("prepared")
        squared, ssum, scaled, rooted, rstd_made = sig("squared", 2), sig("ssum", 2), sig("scaled", 2), sig("rooted"), sig("rstd_made")
        qn_made = sig("qn_made", 4)
        roped, rot_made, kd_made = sig("roped", 4), sig("rot_made", 4), sig("kd_made")
        gexp_made, gden_made, grec_made, rgw_made, gate_made = (sig(n) for n in ("gexp_made", "gden_made", "grec_made", "rgw_made", "gate_made"))
        qT_made, kT_made, rkT_made, mqT_made, rqT_made = (sig(n) for n in ("qT_made", "kT_made", "rkT_made", "mqT_made", "rqT_made"))
        masked, maxed, topped, negated, exped, dened, inverted, probs_made = (
            sig("masked", 2), sig("maxed", 2), sig("topped"), sig("negated", 2), sig("exped", SWA_H + 1), sig("dened"),
            sig("inverted"), sig("probs_made"))
        mmaxed, mnegated, mexped, minverted, mprobs_made, mprobsT_made = (
            sig("mmaxed"), sig("mnegated"), sig("mexped", MEM_H), sig("minverted"), sig("mprobs_made"), sig("mprobsT_made"))
        probsT_made = sig("probsT_made", 2)
        vals_made = sig("vals_made")
        inT_made, state_made = sig("inT_made"), sig("state_made", RET_H, 1)
        stated, aggregated, rscaled, rrooted, rinverted, rnormed, gated = (
            sig("stated", RET_H), sig("aggregated", RET_H), sig("rscaled"), sig("rrooted"), sig("rinverted"), sig("rnormed", RET_H), sig("gated"))
        o_swa, o_mem, o_ret = sig("o_swa"), sig("o_mem"), sig("o_ret")
        blk = c.enter_context(nc.Block())
        z_dram, o_dram = io["z"], io["oT"]

        def heads(ap, h):
            return ap.rearrange("p (h d) -> p h d", h=h)

        def pairs(q):
            return q[:, 0:SWA_H * SWA_D].rearrange("p (j g d) -> p j g d", g=SWA_KV, d=SWA_D)

        def col(w, n):
            return w.unsqueeze(2).to_broadcast([P, w.shape[1], n])

        @blk.sync
        def _(sp):
            n = 0
            for dst, src in ((decayT[:], io["decayT"]), (qdec[:], io["qdec"].to_broadcast([P, RET_H * P])),
                             (kdec[:], io["kdec"]), (mask[:], io["mask"]), (mask_now[:], io["mask_first"]),
                             (sinks[:], io["swa_sinks"].to_broadcast([P, SWA_H])),
                             (wq[0:SWA_D, :], io["swa_q_norm_w"].rearrange("a (p o) -> (a p) o", o=1)),
                             (wq[SWA_D:P, :], io["swa_q_norm_w"].rearrange("a (p o) -> (a p) o", o=1)),
                             (wk[0:SWA_D, :], io["swa_k_norm_w"].rearrange("a (p o) -> (a p) o", o=1)),
                             (wk[SWA_D:P, :], io["swa_k_norm_w"].rearrange("a (p o) -> (a p) o", o=1)),
                             (wm[:], io["mem_q_norm_w"].rearrange("a (p o) -> (a p) o", o=1)),
                             (wret[:], io["ret_norm_w"].to_broadcast([P, RV]))):
                sp.dma_start(dst, src).then_inc(consts_in.sem, 16)
                n += 16
            assert n == 192
            for o in o_out:
                o.open(sp)

            def load(t, p, i):
                sp.dma_start(zt[i][:], z_dram[ds(t * P, P), 0:ZG0]).then_inc(z_in[i].sem, 16)
                sp.dma_start(rope[i][:], io["rope"][ds(t * P, P), :]).then_inc(z_in[i].sem, 16)

            load(0, 0, 0)
            load(1, 0, 1)

            def store(t, i):
                for s in (o_swa, o_mem, o_ret):
                    sp.wait_ge(s.sem, s.after(t))
                sp.dma_start(o_dram[ds(t, 1), :, :].rearrange("a p n -> (a p) n"), oT[i][:]).then_inc(o_out[i].sem, 16)

            with sp.Fori(0, TILES // 2 - 1) as p:
                store(2 * p, 0)
                sp.wait_ge(o_swa.sem, o_swa.after(2 * p + 1))
                sp.wait_ge(state_made.sem, state_made.after(2 * p))
                load(2 * p + 2, p, 0)
                store(2 * p + 1, 1)
                sp.wait_ge(o_swa.sem, o_swa.after(2 * p + 2))
                sp.wait_ge(state_made.sem, state_made.after(2 * p + 1))
                load(2 * p + 3, p, 1)
            store(TILES - 2, 0)
            store(TILES - 1, 1)
            for o in o_out:
                sp.wait_ge(o.sem, o.after(TILES // 2 - 1))

        @blk.gpsimd
        def _(pool):
            pool.wait_ge(consts_in.sem, 192)
            with pool.Fori(0, TILES // 2) as p:
                for i in range(2):
                    t = 2 * p + i
                    z = zt[i]
                    pool.wait_ge(z_in[i].sem, z_in[i].after(p))
                    pool.wait_ge(rot_made.sem, rot_made.after(t - 1))
                    for n, (x0, dst, tab) in enumerate(((RQ0, qc, 0), (RQ0, qs, 1), (RK0, kc, 2), (RK0, ks, 3))):
                        pool.tensor_tensor(
                            dst[:].rearrange("p (a d) -> p a d", d=HALF),
                            z[:, x0:x0 + RQ].rearrange("p (a d) -> p a d", d=HALF),
                            rope[i][:, tab * HALF:(tab + 1) * HALF].unsqueeze(1).to_broadcast([P, 2 * RET_H, HALF]),
                            ALU.mult).then_inc(roped.sem, 1)
                    pool.wait_ge(gate_made.sem, gate_made.after(t - 1))
                    pool.tensor_tensor(rgw[:], z[:, RG0:RG0 + RV], wret[:], ALU.mult).then_inc(rgw_made.sem, 1)
                    pool.wait_ge(rot_made.sem, rot_made.after(t))
                    pool.wait_ge(RA.filled.sem, RA.filled.after(t - 1))
                    pool.tensor_tensor(heads(rkd[:], RET_H), heads(rkn[:], RET_H), col(kdec[:], RET_DK),
                                       ALU.mult).then_inc(kd_made.sem, 1)
                    pool.wait_ge(grec_made.sem, grec_made.after(t))
                    pool.wait_ge(rgw_made.sem, rgw_made.after(t))
                    pool.wait_ge(gated.sem, gated.after(t - 1))
                    pool.tensor_tensor(gate[:], rgw[:], gexp[:], ALU.mult).then_inc(gate_made.sem, 1)
                    pool.wait_ge(minverted.sem, minverted.after(t))
                    pool.tensor_tensor(heads(mprobs[:], MEM_H), heads(mprobs[:], MEM_H), col(mrinv[:], MEM_LEN),
                                       ALU.mult).then_inc(mprobs_made.sem, 1)
                    pool.wait_ge(inverted.sem, inverted.after(t))
                    pool.tensor_tensor(heads(probs[:], SWA_H), heads(probs[:], SWA_H), col(rinv[:], 2 * P),
                                       ALU.mult).then_inc(probs_made.sem, 1)

        @blk.scalar
        def _(act):
            act.wait_ge(consts_in.sem, 192)
            act.wait_ge(prepared.sem, 4)
            with act.Fori(0, TILES // 2) as p:
                for i in range(2):
                    t = 2 * p + i
                    z = zt[i]
                    act.wait_ge(z_in[i].sem, z_in[i].after(p))
                    act.wait_ge(ssum.sem, ssum.after(t - 1))
                    act.activation(sq[:, 0:QK], z[:, 0:QK], ACT.Square).then_inc(squared.sem, 1)
                    act.activation(sq[:, QK:QK + MW], z[:, MQ0:MQ0 + MW], ACT.Square).then_inc(squared.sem, 1)
                    act.wait_ge(scaled.sem, scaled.after(t))
                    act.activation(rstd[:], ss[:], ACT.Sqrt).then_inc(rooted.sem, 1)
                    act.wait_ge(gate_made.sem, gate_made.after(t - 1))
                    act.activation(gexp[:], z[:, RG0:RG0 + RV], ACT.Exp, scale=-1.0).then_inc(gexp_made.sem, 1)
                    RC.wait_filled(act, t, 0)
                    act.activation(qT[:], RC.ps[:, 0:4 * P], ACT.Copy, scale=wq[:, 0:1]).then_inc(RC.taken.sem, 1)
                    RD.wait_filled(act, t, 0)
                    act.activation(kT[i][:], RD.ps[:, 0:P], ACT.Copy, scale=wk[:, 0:1]).then_inc(RD.taken.sem, 1)
                    RC.wait_filled(act, t, 2)
                    act.copy(rkT[:], RC.ps[:, 0:RQ]).then_inc(RC.taken.sem, 1)
                    act.wait_ge(mnegated.sem, mnegated.after(t))
                    RB.wait_free(act, t, 0)
                    for h in range(MEM_H):
                        cols = slice(h * MEM_LEN, (h + 1) * MEM_LEN)
                        ex = act.activation(mprobs[:, cols], RB.ps[:, cols], ACT.Exp, bias=mneg[:, h:h + 1],
                                            accum_out=mrsum[:, h:h + 1])
                        ex.then_inc(mexped.sem, 1)
                    act.wait_ge(mexped.sem, mexped.after(t))
                    act.sem_inc(RB.taken.sem, 1)
                    act.wait_ge(negated.sem, negated.after(t))
                    act.activation(sk[:], sk[:], ACT.Exp).then_inc(exped.sem, 1)
                    for h in range(SWA_H):
                        cols = slice(h * 2 * P, (h + 1) * 2 * P)
                        act.activation(probs[:, cols], probs[:, cols], ACT.Exp, bias=neg[:, h:h + 1],
                                       accum_out=rsum[:, h:h + 1]).then_inc(exped.sem, 1)
                    act.wait_ge(rscaled.sem, rscaled.after(t))
                    act.activation(rr[:], rr[:], ACT.Sqrt).then_inc(rrooted.sem, 1)
                    RB.wait_filled(act, t, 1)
                    act.copy(mprobsT[:], RB.ps[:]).then_inc(RB.taken.sem, 1)
                    act.wait_ge(RC.filled.sem, RC.filled.after(t - 1))
                    act.copy(vals[i][:], z[:, SV0:SV0 + P]).then_inc(vals_made.sem, 1)
                    for g in range(2):
                        RA.wait_filled(act, t, 3 + g)
                        act.copy(probsT[:, g * 8 * P:(g + 1) * 8 * P], RA.ps[:]).then_inc(RA.taken.sem, 1)
                    act.wait_ge(o_out[i].sem, o_out[i].after(p - 1))
                    RD.wait_filled(act, t, 2)
                    act.copy(oT[i][:, 12 * P:16 * P], RD.ps[:, 0:4 * P]).then_inc(o_mem.sem, 1)
                    act.wait_ge(o_mem.sem, o_mem.after(t))
                    act.sem_inc(RD.taken.sem, 1)
                    RC.wait_filled(act, t, 4)
                    act.copy(oT[i][:, 0:4 * P], RC.ps[:, 0:4 * P]).then_inc(o_swa.sem, 1)
                    act.wait_ge(o_swa.sem, o_swa.after(t))
                    act.sem_inc(RC.taken.sem, 1)

        @blk.vector
        def _(dve):
            dve.wait_ge(consts_in.sem, 192)
            state_made.open(dve)
            for r in (RA, RB, RC, RD, RE):
                r.taken.open(dve)
            dve.memset(state[:], 0.0).then_inc(prepared.sem, 1)
            dve.memset(kT[1][:], 0.0).then_inc(prepared.sem, 1)
            dve.memset(vals[1][:], 0.0).then_inc(prepared.sem, 1)
            dve.tensor_scalar(wq[:], wq[:], float(SWA_D) ** -0.5, None, ALU.mult).then_inc(prepared.sem, 1)
            with dve.Fori(0, TILES // 2) as p:
                for i in range(2):
                    t = 2 * p + i
                    z = zt[i]
                    dve.wait_ge(squared.sem, squared.after(t, 1))
                    dve.tensor_reduce(ss[:, 0:NH], heads(sq[:, 0:QK], NH), AX, ALU.add).then_inc(ssum.sem, 1)
                    dve.wait_ge(squared.sem, squared.after(t))
                    dve.tensor_reduce(ss[:, NH:NH + MEM_H], heads(sq[:, QK:QK + MW], MEM_H), AX,
                                      ALU.add).then_inc(ssum.sem, 1)
                    dve.wait_ge(ssum.sem, ssum.after(t))
                    dve.tensor_scalar(ss[:, 0:NH], ss[:, 0:NH], 1.0 / SWA_D, EPS, ALU.mult,
                                      ALU.add).then_inc(scaled.sem, 1)
                    dve.tensor_scalar(ss[:, NH:NH + MEM_H], ss[:, NH:NH + MEM_H], 1.0 / MEM_D, EPS, ALU.mult,
                                      ALU.add).then_inc(scaled.sem, 1)
                    dve.wait_ge(roped.sem, roped.after(t))
                    dve.wait_ge(RC.filled.sem, RC.filled.after(t - 1))
                    for out, cs, sn in ((rqn, qc, qs), (rkn, kc, ks)):
                        o4, c4, s4 = (a[:].rearrange("p (h a d) -> p h a d", a=2, d=HALF) for a in (out, cs, sn))
                        dve.tensor_tensor(o4[:, :, 0, :], c4[:, :, 0, :], s4[:, :, 1, :],
                                          ALU.subtract).then_inc(rot_made.sem, 1)
                        dve.tensor_tensor(o4[:, :, 1, :], s4[:, :, 0, :], c4[:, :, 1, :],
                                          ALU.add).then_inc(rot_made.sem, 1)
                    dve.wait_ge(rooted.sem, rooted.after(t))
                    dve.reciprocal(rstd[:], rstd[:]).then_inc(rstd_made.sem, 1)
                    dve.wait_ge(rstd_made.sem, rstd_made.after(t))
                    for g in range(SWA_KV):
                        dve.tensor_tensor(pairs(qn)[:, :, g, :], heads(z[:, g * 256:(g + 1) * 256], 4),
                                          col(rstd[:, g * 4:(g + 1) * 4], SWA_D), ALU.mult).then_inc(qn_made.sem, 1)
                    dve.tensor_tensor(heads(qn[:, SK0:QK], SWA_KV), heads(z[:, SK0:QK], SWA_KV),
                                      col(rstd[:, SWA_H:NH], SWA_D), ALU.mult).then_inc(qn_made.sem, 1)
                    dve.tensor_tensor(heads(mqn[:], MEM_H), heads(z[:, MQ0:MQ0 + MW], MEM_H),
                                      col(rstd[:, NH:NH + MEM_H], MEM_D), ALU.mult).then_inc(qn_made.sem, 1)
                    dve.wait_ge(gexp_made.sem, gexp_made.after(t))
                    dve.tensor_scalar(gexp[:], gexp[:], 1.0, None, ALU.add).then_inc(gden_made.sem, 1)
                    dve.wait_ge(gden_made.sem, gden_made.after(t))
                    dve.reciprocal(gexp[:], gexp[:]).then_inc(grec_made.sem, 1)
                    RC.wait_filled(dve, t, 1)
                    dve.tensor_scalar(mqT[:], RC.ps[:, 0:MW], wm[:, 0:1], None, ALU.mult).then_inc(RC.taken.sem, 1)
                    RD.wait_filled(dve, t, 1)
                    dve.tensor_copy(rqT[:], RD.ps[:, 0:RQ]).then_inc(rqT_made.sem, 1)
                    dve.wait_ge(rqT_made.sem, rqT_made.after(t))
                    dve.tensor_tensor(rqdT[:], RD.ps[:, 0:RQ], qdec[:], ALU.mult).then_inc(RD.taken.sem, 1)
                    RB.wait_filled(dve, t, 0)
                    dve.tensor_reduce(mmx[:], heads(RB.ps[:], MEM_H), AX, ALU.max).then_inc(mmaxed.sem, 1)
                    dve.wait_ge(mmaxed.sem, mmaxed.after(t))
                    dve.tensor_scalar(mneg[:], mmx[:], -1.0, None, ALU.mult).then_inc(mnegated.sem, 1)
                    for g in range(2):
                        cols = slice(g * 8 * P, (g + 1) * 8 * P)
                        RA.wait_filled(dve, t, g)
                        dve.tensor_tensor(heads(probs[:, cols], 4), heads(RA.ps[:], 4),
                                          mask_now[:].unsqueeze(1).to_broadcast([P, 4, 2 * P]),
                                          ALU.add).then_inc(masked.sem, 1)
                        dve.wait_ge(masked.sem, masked.after(t, g + 1))
                        dve.sem_inc(RA.taken.sem, 1)
                        dve.tensor_reduce(mx[:, g * 4:g * 4 + 4], heads(probs[:, cols], 4), AX,
                                          ALU.max).then_inc(maxed.sem, 1)
                        if g == 0:
                            RC.wait_filled(dve, t, 3)
                            dve.tensor_tensor(inT[:], RC.ps[:, 0:RET_H * P], decayT[:],
                                              ALU.mult).then_inc(RC.taken.sem, 1)
                    dve.tensor_copy(mask_now[:, 0:P], mask[:, 0:P])
                    dve.wait_ge(maxed.sem, maxed.after(t))
                    dve.tensor_tensor(mx[:], mx[:], sinks[:], ALU.max).then_inc(topped.sem, 1)
                    dve.wait_ge(topped.sem, topped.after(t))
                    dve.tensor_scalar(neg[:], mx[:], -1.0, None, ALU.mult).then_inc(negated.sem, 1)
                    dve.tensor_tensor(sk[:], sinks[:], mx[:], ALU.subtract).then_inc(negated.sem, 1)
                    RE.wait_filled(dve, t, 0)
                    RA.wait_filled(dve, t, 2)
                    for h in range(RET_H):
                        cols = slice(h * RET_DV, (h + 1) * RET_DV)
                        dve.scalar_tensor_tensor(out=state[:, cols], in0=state[:, cols], scalar=chunk_decay[h],
                                                 in1=RA.ps[:, cols], op0=ALU.mult,
                                                 op1=ALU.add).then_inc(state_made.sem, 1)
                    dve.wait_ge(state_made.sem, state_made.after(t))
                    dve.sem_inc(RA.taken.sem, 1)
                    for h in range(RET_H):
                        dve.bn_stats(st[:, 6 * h:6 * h + 6], RE.ps[:, h * RET_DV:(h + 1) * RET_DV]).then_inc(stated.sem, 1)
                    dve.wait_ge(stated.sem, stated.after(t))
                    stand(dve, idle)
                    for h in range(RET_H):
                        dve.bn_aggr(mva[:, 2 * h:2 * h + 2], st[:, 6 * h:6 * h + 6]).then_inc(aggregated.sem, 1)
                    dve.wait_ge(aggregated.sem, aggregated.after(t))
                    dve.tensor_scalar(rr[:], mva[:].rearrange("p (h a) -> p h a", a=2)[:, :, 1], EPS, None,
                                      ALU.add).then_inc(rscaled.sem, 1)
                    dve.wait_ge(mexped.sem, mexped.after(t))
                    dve.reciprocal(mrinv[:], mrsum[:]).then_inc(minverted.sem, 1)
                    dve.wait_ge(exped.sem, exped.after(t))
                    dve.tensor_tensor(rinv[:], rsum[:], sk[:], ALU.add).then_inc(dened.sem, 1)
                    dve.wait_ge(dened.sem, dened.after(t))
                    dve.reciprocal(rinv[:], rinv[:]).then_inc(inverted.sem, 1)
                    dve.wait_ge(rrooted.sem, rrooted.after(t))
                    dve.reciprocal(rr[:], rr[:]).then_inc(rinverted.sem, 1)
                    dve.wait_ge(rinverted.sem, rinverted.after(t))
                    for h in range(RET_H):
                        cols = slice(h * RET_DV, (h + 1) * RET_DV)
                        dve.tensor_scalar(rnorm[:, cols], RE.ps[:, cols], mva[:, 2 * h:2 * h + 1], rr[:, h:h + 1],
                                          ALU.subtract, ALU.mult).then_inc(rnormed.sem, 1)
                    dve.wait_ge(rnormed.sem, rnormed.after(t))
                    dve.sem_inc(RE.taken.sem, 1)
                    dve.wait_ge(gate_made.sem, gate_made.after(t))
                    dve.tensor_tensor(rnorm[:], rnorm[:], gate[:], ALU.mult).then_inc(gated.sem, 1)
                    dve.wait_ge(o_out[i].sem, o_out[i].after(p - 1))
                    RB.wait_filled(dve, t, 2)
                    dve.tensor_copy(oT[i][:, 4 * P:12 * P], RB.ps[:]).then_inc(o_ret.sem, 1)
                    dve.wait_ge(o_ret.sem, o_ret.after(t))
                    dve.sem_inc(RB.taken.sem, 1)

        @blk.tensor
        def _(pe):
            pe.wait_ge(prepared.sem, 4)
            with pe.Fori(0, TILES // 2) as p:
                for i in range(2):
                    t = 2 * p + i
                    z = zt[i]

                    def turn(region, use, ins):
                        region.wait_free(pe, t, use)
                        for n, x in enumerate(ins):
                            mm = pe.transpose(region.ps[:, n * P:(n + 1) * P], x, ident[:])
                        mm.then_inc(region.filled.sem, 1)

                    def cuts(x, n):
                        return [x[:, j * P:(j + 1) * P] for j in range(n)]

                    pe.wait_ge(qn_made.sem, qn_made.after(t))
                    turn(RC, 0, cuts(qn, 4))
                    turn(RD, 0, [qn[:, SWA_H * SWA_D:QK]])
                    turn(RC, 1, cuts(mqn, MEM_H))
                    pe.wait_ge(rot_made.sem, rot_made.after(t))
                    turn(RD, 1, cuts(rqn, RET_H))
                    turn(RC, 2, cuts(rkn, RET_H))
                    RB.wait_free(pe, t, 0)
                    pe.wait_ge(RC.taken.sem, RC.taken.after(t, 2))
                    for h in range(MEM_H):
                        mm = pe.matmul(RB.ps[:, h * MEM_LEN:(h + 1) * MEM_LEN], mqT[:, h * P:(h + 1) * P],
                                       mkT[:, h, :], start=True, stop=True)
                    mm.then_inc(RB.filled.sem, 1)
                    pe.wait_ge(RD.taken.sem, RD.taken.after(t, 2))
                    RC.wait_free(pe, t, 3)
                    for h in range(RET_H):
                        cols = slice(h * P, (h + 1) * P)
                        mm = pe.matmul(RC.ps[:, cols], rkT[:, cols], rqT[:, cols], start=True, stop=True)
                    mm.then_inc(RC.filled.sem, 1)
                    for g in range(SWA_KV):
                        rows = slice(g * SWA_D, (g + 1) * SWA_D)
                        RA.wait_free(pe, t, g)
                        for j in range(4):
                            for n, keys in enumerate((kT[1 - i], kT[i])):
                                at = (2 * j + n) * P
                                mm = pe.matmul(RA.ps[:, at:at + P], qT[rows, j * P:(j + 1) * P], keys[rows, :],
                                               start=True, stop=True)
                        mm.then_inc(RA.filled.sem, 1)
                    RE.wait_free(pe, t, 0)
                    pe.wait_ge(RC.taken.sem, RC.taken.after(t, 4))
                    pe.wait_ge(state_made.sem, state_made.after(t - 1))
                    for h in range(RET_H):
                        cols = slice(h * RET_DV, (h + 1) * RET_DV)
                        pe.matmul(RE.ps[:, cols], inT[:, h * P:(h + 1) * P],
                                  z[:, RV0 + h * RET_DV:RV0 + (h + 1) * RET_DV], start=True, stop=False)
                        mm = pe.matmul(RE.ps[:, cols], rqdT[:, h * P:(h + 1) * P], state[:, cols],
                                       start=False, stop=True)
                    mm.then_inc(RE.filled.sem, 1)
                    RA.wait_free(pe, t, 2)
                    pe.wait_ge(kd_made.sem, kd_made.after(t))
                    for h in range(RET_H):
                        mm = pe.matmul(RA.ps[:, h * RET_DV:(h + 1) * RET_DV], rkd[:, h * RET_DK:(h + 1) * RET_DK],
                                       z[:, RV0 + h * RET_DV:RV0 + (h + 1) * RET_DV], start=True, stop=True)
                    mm.then_inc(RA.filled.sem, 1)
                    pe.wait_ge(mprobs_made.sem, mprobs_made.after(t))
                    turn(RB, 1, cuts(mprobs, 8))
                    pe.wait_ge(RB.taken.sem, RB.taken.after(t, 2))
                    RD.wait_free(pe, t, 2)
                    for h in range(MEM_H):
                        for m in range(2):
                            at = (2 * h + m) * P
                            mm = pe.matmul(RD.ps[:, h * P:(h + 1) * P], mv[:, m, h * MEM_D:(h + 1) * MEM_D],
                                           mprobsT[:, at:at + P], start=(m == 0), stop=(m == 1))
                    mm.then_inc(RD.filled.sem, 1)
                    pe.wait_ge(probs_made.sem, probs_made.after(t))
                    turn(RA, 3, cuts(probs, 8))
                    turn(RA, 4, cuts(probs[:, 8 * P:16 * P], 8))
                    pe.wait_ge(RA.taken.sem, RA.taken.after(t, 5))
                    pe.wait_ge(vals_made.sem, vals_made.after(t))
                    RC.wait_free(pe, t, 4)
                    for h in range(SWA_H):
                        rows = slice((h % 2) * SWA_D, (h % 2 + 1) * SWA_D)
                        dims = slice((h // 4) * SWA_D, (h // 4 + 1) * SWA_D)
                        for n, v in enumerate((vals[1 - i], vals[i])):
                            at = (2 * h + n) * P
                            mm = pe.matmul(RC.ps[rows, (h // 2) * P:(h // 2 + 1) * P], v[:, dims],
                                           probsT[:, at:at + P], start=(n == 0), stop=(n == 1))
                    mm.then_inc(RC.filled.sem, 1)
                    pe.wait_ge(gated.sem, gated.after(t))
                    turn(RB, 2, cuts(rnorm, 8))


def mixer_constants():
    f = np.float32
    half = RET_DK // 2
    inv = (f(1.0) / (f(10000.0) ** (np.arange(half, dtype=f) / f(half)))).astype(f)
    ang = np.arange(S, dtype=f)[:, None] * inv[None, :]
    cs, sn = np.cos(ang).astype(f), np.sin(ang).astype(f)
    ksc = f(RET_DK ** -0.5)
    lg = np.log1p(-(f(2.0) ** (f(-5.0) - np.arange(RET_H, dtype=f)))).astype(f)
    pos = np.arange(P, dtype=f)
    diff = pos[None, :] - pos[:, None]
    dec = np.where(diff[:, None, :] >= 0, np.exp(np.maximum(diff, 0)[:, None, :] * lg[None, :, None]), 0)
    qi, kj = np.arange(P)[:, None], np.arange(2 * P)[None, :]
    gap = P + qi - kj
    mask = np.where((gap >= 0) & (gap < P), 0.0, NEG).astype(f)
    first = np.where(kj < P, f(NEG), mask).astype(f)
    return {
        "rope": np.concatenate([cs, sn, cs * ksc, sn * ksc], axis=1).astype(f),
        "decayT": dec.reshape(P, RET_H * P).astype(f),
        "qdec": np.exp((pos[None, :] + 1) * lg[:, None]).reshape(1, RET_H * P).astype(f),
        "kdec": np.exp((P - 1 - pos[:, None]) * lg[None, :]).astype(f),
        "mask": mask, "mask_first": first,
    }


def project_mixers(nc, io):
    KO = 16
    PARTS = ((0, 4), (4, 12), (12, 16))
    H = 512
    with ExitStack() as c:
        w_hi = c.enter_context(nc.sbuf_tensor("b_hi", [P, KO, D], F32R))
        w_lo = c.enter_context(nc.sbuf_tensor("b_lo", [P, KO, D], F32R))
        raw = [c.enter_context(nc.sbuf_tensor(f"b_raw{i}", [P, KO * P], F32)) for i in range(2)]
        o_hi = [c.enter_context(nc.sbuf_tensor(f"b_ohi{i}", [P, KO * P], F32R)) for i in range(2)]
        o_lo = [c.enter_context(nc.sbuf_tensor(f"b_olo{i}", [P, KO * P], F32R)) for i in range(2)]
        gates = c.enter_context(nc.sbuf_tensor("b_gates", [P, 3 * D], F32))
        part = c.enter_context(nc.sbuf_tensor("b_part", [P, 2, H], F32))
        merged = [c.enter_context(nc.sbuf_tensor(f"b_merged{i}", [P, D], F32)) for i in range(2)]
        acc = [c.enter_context(nc.psum_tensor(f"b_acc{i}", [P, 3, H], F32)) for i in range(2)]
        RING = 4
        w_in = [Signal(io["sems"], nc, f"b_w_in{i}", 16) for i in range(RING)]
        w_hi_made = Signal(io["sems"], nc, "b_w_hi_made")
        w_lo_made = Signal(io["sems"], nc, "b_w_lo_made")
        o_in = [Signal(io["sems"], nc, f"b_o_in{i}", 16) for i in range(2)]
        g_in = Signal(io["sems"], nc, "b_g_in", 16)
        hi_made = Signal(io["sems"], nc, "b_hi_made", 1)
        lo_made = Signal(io["sems"], nc, "b_lo_made", 1, 2)
        opened = Signal(io["sems"], nc, "b_opened")
        summed = Signal(io["sems"], nc, "b_summed", 2, 2)
        gated = Signal(io["sems"], nc, "b_gated", 10, 1)
        m_out = [Signal(io["sems"], nc, f"b_m_out{i}", 16, 1) for i in range(2)]
        blk = c.enter_context(nc.Block())

        def slot(n):
            return raw[n // 2 % 2][:, (n % 2) * D:(n % 2 + 1) * D]

        @blk.sync
        def _(sp):
            for m in m_out:
                m.open(sp)
            rows = [(io["w_br_swa"], k) for k in range(4)] + [(io["w_br_ret"], k) for k in range(8)] + [
                (io["w_br_mem"], k) for k in range(4)]
            for n, (w, k) in enumerate(rows):
                if n >= RING:
                    sp.wait_ge(w_lo_made.sem, n - RING + 1)
                sp.dma_start(slot(n), w[k * P:(k + 1) * P, :]).then_inc(w_in[n % RING].sem, 16)
            sp.wait_ge(w_lo_made.sem, KO)

            def load_outputs(t, i):
                sp.wait_ge(lo_made.sem, lo_made.after(t - 2))
                sp.dma_start(raw[i][:], io["oT"][ds(t, 1), :, :].rearrange("a p n -> (a p) n")).then_inc(
                    o_in[i].sem, 16)

            def load_gates(t):
                sp.dma_start(gates[:], io["z"][ds(t * P, P), ZG0:ZW]).then_inc(g_in.sem, 16)

            def tile(t, i, last=False):
                if not last:
                    load_outputs(t + 1, 1 - i)
                sp.wait_ge(gated.sem, gated.after(t))
                if not last:
                    load_gates(t + 1)
                sp.dma_start(io["merged"][ds(t * P, P), :], merged[i][:]).then_inc(m_out[i].sem, 16)

            load_outputs(0, 0)
            load_gates(0)
            with sp.Fori(0, TILES // 2 - 1) as p:
                tile(2 * p, 0)
                tile(2 * p + 1, 1)
            tile(TILES - 2, 0)
            tile(TILES - 1, 1, last=True)
            for i in range(2):
                sp.wait_ge(m_out[i].sem, m_out[i].after(TILES // 2 - 1))

        @blk.scalar
        def _(act):
            for n in range(KO):
                act.wait_ge(w_in[n % RING].sem, 16 * (n // RING + 1))
                act.copy(w_hi[:, n, :], slot(n)).then_inc(w_hi_made.sem, 1)
            with act.Fori(0, TILES // 2) as p:
                for i in range(2):
                    t = 2 * p + i
                    act.wait_ge(o_in[i].sem, o_in[i].after(p))
                    act.wait_ge(summed.sem, summed.after(t - 2))
                    act.copy(o_hi[i][:], raw[i][:]).then_inc(hi_made.sem, 1)
                    act.wait_ge(g_in.sem, g_in.after(t))
                    act.activation(gates[:], gates[:], ACT.Sigmoid).then_inc(opened.sem, 1)

        @blk.vector
        def _(dve):
            lo_made.open(dve)
            gated.open(dve)
            for n in range(KO):
                dve.wait_ge(w_hi_made.sem, n + 1)
                dve.tensor_tensor(w_lo[:, n, :], slot(n), w_hi[:, n, :].bitcast(F32),
                                  ALU.subtract).then_inc(w_lo_made.sem, 1)

            def split(t, i):
                dve.wait_ge(hi_made.sem, hi_made.after(t))
                dve.tensor_tensor(o_lo[i][:], raw[i][:], o_hi[i][:].bitcast(F32),
                                  ALU.subtract).then_inc(lo_made.sem, 1)

            def merge(t, p, i):
                dve.wait_ge(opened.sem, opened.after(t))
                dve.wait_ge(m_out[i].sem, m_out[i].after(p - 1))
                for h in range(2):
                    cols = slice(h * H, (h + 1) * H)
                    out = merged[i][:, cols]
                    n = 5 * h
                    dve.wait_ge(summed.sem, summed.after(t, h + 1))
                    dve.tensor_tensor(out, gates[:, h * H:(h + 1) * H], acc[h][:, 0, :],
                                      ALU.mult).then_inc(gated.sem, 1)
                    dve.wait_ge(gated.sem, gated.after(t - 1) if h == 0 else gated.after(t, 5))
                    for b in (1, 2):
                        dve.tensor_tensor(part[:, b - 1, :], gates[:, b * D + h * H:b * D + (h + 1) * H],
                                          acc[h][:, b, :], ALU.mult).then_inc(gated.sem, 1)
                    for b in (1, 2):
                        dve.wait_ge(gated.sem, gated.after(t, n + 2 + b))
                        dve.tensor_tensor(out, out, part[:, b - 1, :], ALU.add).then_inc(gated.sem, 1)

            split(0, 0)
            with dve.Fori(0, TILES // 2 - 1) as p:
                split(2 * p + 1, 1)
                merge(2 * p, p, 0)
                split(2 * p + 2, 0)
                merge(2 * p + 1, p, 1)
            split(TILES - 1, 1)
            merge(TILES - 2, TILES // 2 - 1, 0)
            merge(TILES - 1, TILES // 2 - 1, 1)

        @blk.tensor
        def _(pe):
            summed.open(pe)
            pe.wait_ge(w_lo_made.sem, KO)
            with pe.Fori(0, TILES // 2) as p:
                for i in range(2):
                    t = 2 * p + i
                    pe.wait_ge(lo_made.sem, lo_made.after(t))
                    for h in range(2):
                        pe.wait_ge(gated.sem, gated.after(t - 1, 5 * (h + 1)))
                        for b, (k0, k1) in enumerate(PARTS):
                            mm = three_pass(pe, acc[h][:, b, :],
                                            lambda k: o_hi[i][:, k * P:(k + 1) * P],
                                            lambda k: o_lo[i][:, k * P:(k + 1) * P],
                                            lambda k: w_hi[:, k, h * H:(h + 1) * H],
                                            lambda k: w_lo[:, k, h * H:(h + 1) * H], range(k0, k1))
                        mm.then_inc(summed.sem, 1)


BLOCK_TILES = 4
SLOTS = E * S
EXPERT, LIVE, FIRST, COUNT, PRIOR = range(5)
BLOCK_COLS = 8
MAX_TILES = E + S * TOPK // P
MAX_BLOCKS = E + S * TOPK // (BLOCK_TILES * P)


def finish_mixing(nc, io, ident, blocks):
    H = 512
    with ExitStack() as c:
        def sb(name, shape, dt=F32):
            return c.enter_context(nc.sbuf_tensor(f"f_{name}", shape, dt))

        w_hi, w_lo = sb("whi", [P, KD, D], F32R), sb("wlo", [P, KD, D], F32R)
        wraw = [sb(f"wraw{i}", [P, D]) for i in range(2)]
        mg = [sb(f"mg{i}", [P, D]) for i in range(2)]
        xs = [sb(f"x{i}", [P, D]) for i in range(2)]
        m_hi = [sb(f"mhi{i}", [P, D], F32R) for i in range(2)]
        m_lo = [sb(f"mlo{i}", [P, D], F32R) for i in range(2)]
        x1 = [sb(f"x1{i}", [P, D]) for i in range(2)]
        h2 = [sb(f"h2{i}", [P, D]) for i in range(2)]
        h2T = sb("h2T", [P, D])
        sq, wb = sb("sq", [P, D]), sb("wb", [P, D])
        wr, br = sb("wr", [P, KD, E]), sb("br", [P, E])
        ss, rstd = sb("ss", [P, 2]), sb("rstd", [P, 2])
        logits, top, topi = sb("logits", [P, E]), sb("top", [P, 8]), sb("topi", [P, 8], U32)
        ntop, ex, exs, exr = sb("ntop", [P, 1]), sb("ex", [P, TOPK]), sb("exs", [P, 1]), sb("exr", [P, 1])
        topf, onehot, sel = sb("topf", [P, TOPK]), sb("onehot", [P, TOPK, E]), sb("sel", [P, E])
        taken = sb("taken", [P, E])
        base, place, slotf = sb("base", [P, E]), sb("place", [P, TOPK, E]), sb("slotf", [P, TOPK])
        slots = [sb(f"slots{i}", [P, TOPK], U32) for i in range(2)]
        recs = [sb(f"recs{i}", [P, TOPK, 2], I32) for i in range(2)]
        tokf = sb("tokf", [P, TOPK])
        before, ones = sb("before", [P, P]), sb("ones", [P, P])
        ef, e0f, lane = sb("ef", [P, E]), sb("e0f", [P, E]), sb("lane", [P, 1])
        fill = sb("fill", [P, SLOTS // P, 2], I32)
        zero = sb("zero", [P, D])
        cnt, tl, nb, cum = sb("cnt", [P, E], I32), sb("tl", [P, E], I32), sb("nb", [P, E], I32), sb("cum", [P, E])
        tlf, nbf, le, tmp, zer = sb("tlf", [P, E]), sb("nbf", [P, E]), sb("le", [P, E]), sb("tmp", [P, E]), sb("zer", [P, E])
        col = sb("col", [P, 8])
        rowi = sb("rowi", [P, BLOCK_COLS], I32)
        mT = c.enter_context(nc.psum_tensor("f_mT", [P, D], F32))
        hT = c.enter_context(nc.psum_tensor("f_hT", [P, D], F32))
        acc = c.enter_context(nc.psum_tensor("f_acc", [P, D], F32))
        lgp = c.enter_context(nc.psum_tensor("f_lgp", [P, 512], F32))
        rkp = c.enter_context(nc.psum_tensor("f_rkp", [P, 512], F32))

        def sig(name, per=1, ahead=0):
            return Signal(io["sems"], nc, f"f_{name}", per, ahead)

        consts_in, idle = sig("consts_in", 16), sig("idle")
        w_in = [sig(f"w_in{i}", 16) for i in range(2)]
        w_hi_made, w_lo_made = sig("w_hi_made"), sig("w_lo_made")
        made = sig("made")
        filled = sig("filled", 16)
        mg_in = [sig(f"mg_in{i}", 16) for i in range(2)]
        x_in = [sig(f"x_in{i}", 16) for i in range(2)]
        turned, hi_made, lo_made, summed = sig("turned", 1, 2), sig("hi_made"), sig("lo_made", 1, 1), sig("summed", 1, 2)
        x1_made, squared, rooted, rinv, h2_made = sig("x1_made", 1, 2), sig("squared"), sig("rooted"), sig("rinv"), sig("h2_made")
        x1_out = [sig(f"x1_out{i}", 16, 1) for i in range(2)]
        h2_out = [sig(f"h2_out{i}", 16, 1) for i in range(2)]
        h2_turned, h2T_made, scored = sig("h2_turned", 1, 2), sig("h2T_made", 1, 2), sig("scored", 1, 2)
        biased, ranked, exped, steps, sel_made = (
            sig("biased", 1, 2), sig("ranked", 2, 2), sig("exped", 1, 2), sig("steps", 11, 2), sig("sel_made", 1, 2))
        placed, slotted = sig("placed", 1, 2), sig("slotted", 1, 2)
        sent = [sig(f"sent{i}", 16 * TOPK) for i in range(2)]
        counted, row_made, row_out, blocks_in = sig("counted"), sig("row_made"), sig("row_out", 16), sig("blocks_in", 16)
        blk = c.enter_context(nc.Block())

        @blk.sync
        def _(sp):
            n = 0
            for dst, src in ((wb[:], io["ffn_norm_w"].to_broadcast([P, D])),
                             (wr[:], io["w_router"].rearrange("(k p) e -> p k e", p=P)),
                             (br[:], io["b_router"].to_broadcast([P, E]))):
                sp.dma_start(dst, src).then_inc(consts_in.sem, 16)
            for x in (*x1_out, *h2_out):
                x.open(sp)
            for k in range(KD):
                if k >= 2:
                    sp.wait_ge(w_lo_made.sem, k - 1)
                sp.dma_start(wraw[k % 2][:], io["w_out"][k * P:(k + 1) * P, :]).then_inc(w_in[k % 2].sem, 16)

            def load(t, i):
                sp.wait_ge(turned.sem, turned.after(t - 2))
                sp.dma_start(mg[i][:], io["merged"][ds(t * P, P), :]).then_inc(mg_in[i].sem, 16)
                sp.wait_ge(x1_made.sem, x1_made.after(t - 2))
                sp.dma_start(xs[i][:], io["x"][ds(t * P, P), :]).then_inc(x_in[i].sem, 16)

            def tile(t, i, last=False):
                if not last:
                    load(t + 1, 1 - i)
                sp.wait_ge(x1_made.sem, x1_made.after(t))
                sp.dma_start(io["sum"][ds(t * P, P), :], x1[i][:]).then_inc(x1_out[i].sem, 16)
                sp.wait_ge(h2_made.sem, h2_made.after(t))
                sp.dma_start(io["h2"][ds(t * P, P), :], h2[i][:]).then_inc(h2_out[i].sem, 16)

            load(0, 0)
            with sp.Fori(0, TILES // 2 - 1) as p:
                tile(2 * p, 0)
                tile(2 * p + 1, 1)
            tile(TILES - 2, 0)
            tile(TILES - 1, 1, last=True)
            sp.wait_ge(row_made.sem, 1)
            sp.dma_start(io["blocks"][1:P + 1, :], rowi[:]).then_inc(row_out.sem, 16)
            sp.dma_start(io["blocks"][0:1, :], zero[0:1, 0:BLOCK_COLS].bitcast(I32)).then_inc(row_out.sem, 16)
            sp.wait_ge(row_out.sem, 32)
            sp.dma_start(blocks[:], io["blocks"].rearrange("(a b) w -> a (b w)", a=1)).then_inc(blocks_in.sem, 16)
            sp.wait_ge(blocks_in.sem, 16)
            for s in (*x1_out, *h2_out):
                sp.wait_ge(s.sem, s.after(TILES // 2 - 1))

        @blk.gpsimd
        def _(pool):
            for s in (scored, h2T_made, biased, ranked, exped, steps, sel_made, placed, slotted):
                s.open(pool)
            pool.iota(ef[:], pattern=[[1, E]], base=0, channel_multiplier=0,
                      allow_small_or_imprecise_dtypes=True).then_inc(made.sem, 1)
            pool.iota(e0f[:], pattern=[[S, E]], base=0, channel_multiplier=0,
                      allow_small_or_imprecise_dtypes=True).then_inc(made.sem, 1)
            pool.iota(lane[:], pattern=[[0, 1]], base=0, channel_multiplier=1,
                      allow_small_or_imprecise_dtypes=True).then_inc(made.sem, 1)
            pool.iota(tokf[:], pattern=[[0, TOPK]], base=0, channel_multiplier=1,
                      allow_small_or_imprecise_dtypes=True).then_inc(made.sem, 1)
            pool.memset(ones[:], 1.0).then_inc(made.sem, 1)
            pool.memset(before[:], 1.0).then_inc(made.sem, 1)
            pool.memset(taken[:], 0.0).then_inc(made.sem, 1)
            pool.memset(zer[:], 0.0).then_inc(made.sem, 1)
            pool.memset(zero[:], 0.0).then_inc(made.sem, 1)
            pool.memset(fill[:], 0).then_inc(made.sem, 1)
            pool.wait_ge(made.sem, 10)
            pool.affine_select(out=before[:], in_=before[:], compare_op=ALU.is_gt, fill=0.0, base=0,
                               pattern=[[1, P]], channel_multiplier=-1).then_inc(made.sem, 1)
            pool.iota(fill[:, :, 0], pattern=[[0, SLOTS // P // P], [1, P]], base=S,
                      channel_multiplier=0).then_inc(made.sem, 1)
            pool.wait_ge(made.sem, 12)
            pool.dma_start(io["slots"].rearrange("(p a) w -> p a w", p=P), fill[:]).then_inc(filled.sem, 16)
            pool.dma_start(io["sum"][S:S + PAD, :], zero[:]).then_inc(filled.sem, 16)
            pool.dma_start(io["h2"][S:S + PAD, :], zero[:]).then_inc(filled.sem, 16)
            pool.wait_ge(filled.sem, 48)

            def send(t, i):
                pool.wait_ge(slotted.sem, slotted.after(t))
                stand(pool, idle)
                for k in range(TOPK):
                    pool.indirect_dma_start(
                        out=io["slots"], out_offset=bass.IndirectOffsetOnAxis(ap=slots[i][:, k:k + 1], axis=0),
                        in_=recs[i][:, k, :], in_offset=None).then_inc(sent[i].sem, 16)

            for p in peeled(pool, TILES // 2):
                for i in range(2):
                    if not at_first(p):
                        send(2 * p + i - 2, i)
            send(TILES - 2, 0)
            send(TILES - 1, 1)
            for s in sent:
                pool.wait_ge(s.sem, s.after(TILES // 2 - 1))

        @blk.scalar
        def _(act):
            for k in range(KD):
                act.wait_ge(w_in[k % 2].sem, 16 * (k // 2 + 1))
                act.copy(w_hi[:, k, :], wraw[k % 2][:]).then_inc(w_hi_made.sem, 1)

            def route(t):
                act.wait_ge(h2_turned.sem, h2_turned.after(t))
                act.wait_ge(scored.sem, scored.after(t - 1))
                act.copy(h2T[:], hT[:]).then_inc(h2T_made.sem, 1)
                act.wait_ge(steps.sem, steps.after(t, 1))
                act.activation(ex[:], top[:, 0:TOPK], ACT.Exp, bias=ntop[:, 0:1],
                               accum_out=exs[:]).then_inc(exped.sem, 1)

            for p in peeled(act, TILES // 2):
                for i in range(2):
                    t = 2 * p + i
                    act.wait_ge(turned.sem, turned.after(t))
                    act.wait_ge(summed.sem, summed.after(t - 2))
                    act.copy(m_hi[i][:], mT[:]).then_inc(hi_made.sem, 1)
                    if i == 0:
                        if not at_first(p):
                            route(t - 1)
                    else:
                        route(t - 1)
                    act.wait_ge(x1_made.sem, x1_made.after(t))
                    act.wait_ge(squared.sem, squared.after(t - 1))
                    act.activation(sq[:], x1[i][:], ACT.Square, accum_out=ss[:, i:i + 1]).then_inc(squared.sem, 1)
                    act.wait_ge(squared.sem, squared.after(t))
                    act.activation(rstd[:, i:i + 1], ss[:, i:i + 1], ACT.Sqrt, scale=1.0 / D,
                                   bias=io["eps"][:, 0:1]).then_inc(rooted.sem, 1)
            route(TILES - 1)

        @blk.vector
        def _(dve):
            lo_made.open(dve)
            x1_made.open(dve)
            for k in range(KD):
                dve.wait_ge(w_hi_made.sem, k + 1)
                dve.tensor_tensor(w_lo[:, k, :], wraw[k % 2][:], w_hi[:, k, :].bitcast(F32),
                                  ALU.subtract).then_inc(w_lo_made.sem, 1)
            dve.wait_ge(consts_in.sem, 48)
            dve.wait_ge(made.sem, 12)

            def step(t, n, ins):
                ins.then_inc(steps.sem, 1)
                dve.wait_ge(steps.sem, steps.after(t, n))

            def choose(t, q, i):
                dve.wait_ge(scored.sem, scored.after(t))
                dve.tensor_tensor(logits[:], lgp[:, 0:E], br[:], ALU.add).then_inc(biased.sem, 1)
                dve.wait_ge(biased.sem, biased.after(t))
                stand(dve, idle)
                dve.max(top[:], logits[:]).then_inc(ranked.sem, 1)
                dve.wait_ge(ranked.sem, ranked.after(t, 1))
                stand(dve, idle)
                dve.max_index(topi[:], top[:], logits[:]).then_inc(ranked.sem, 1)
                step(t, 1, dve.tensor_scalar(ntop[:], top[:, 0:1], -1.0, None, ALU.mult))
                dve.wait_ge(ranked.sem, ranked.after(t))
                step(t, 2, dve.tensor_copy(topf[:], topi[:, 0:TOPK]))
                step(t, 3, dve.tensor_tensor(onehot[:], ef[:].unsqueeze(1).to_broadcast([P, TOPK, E]),
                                             topf[:].unsqueeze(2).to_broadcast([P, TOPK, E]), ALU.is_equal))
                dve.tensor_reduce(sel[:], onehot[:].rearrange("p k e -> p e k"), AX, ALU.add).then_inc(sel_made.sem, 1)
                dve.wait_ge(exped.sem, exped.after(t))
                step(t, 4, dve.reciprocal(exr[:], exs[:]))
                dve.wait_ge(sent[i].sem, sent[i].after(q - 1))
                step(t, 5, dve.tensor_scalar(recs[i][:, :, 1].bitcast(F32), ex[:], exr[:, 0:1], None, ALU.mult))
                step(t, 6, dve.tensor_copy(recs[i][:, :, 0], tokf[:]))
                step(t, 7, dve.tensor_scalar(tokf[:], tokf[:], float(P), None, ALU.add))

            def find_slots(t, i):
                dve.wait_ge(placed.sem, placed.after(t))
                step(t, 8, dve.tensor_tensor(base[:], rkp[:, 0:E], e0f[:], ALU.add))
                step(t, 9, dve.tensor_tensor(place[:], onehot[:],
                                             base[:].unsqueeze(1).to_broadcast([P, TOPK, E]), ALU.mult))
                step(t, 10, dve.tensor_reduce(slotf[:], place[:], AX, ALU.add))
                dve.tensor_copy(slots[i][:], slotf[:]).then_inc(slotted.sem, 1)
                step(t, 11, dve.tensor_tensor(taken[:], taken[:], sel[:], ALU.add))

            for p in peeled(dve, TILES // 2):
                for i in range(2):
                    t = 2 * p + i
                    dve.wait_ge(hi_made.sem, hi_made.after(t))
                    dve.wait_ge(summed.sem, summed.after(t - 2))
                    dve.tensor_tensor(m_lo[i][:], mT[:], m_hi[i][:].bitcast(F32), ALU.subtract).then_inc(lo_made.sem, 1)
                    if not at_first(p):
                        find_slots(t - 2, i)
                    dve.wait_ge(summed.sem, summed.after(t))
                    dve.wait_ge(x_in[i].sem, x_in[i].after(p))
                    dve.wait_ge(x1_out[i].sem, x1_out[i].after(p - 1))
                    dve.tensor_tensor(x1[i][:], acc[:], xs[i][:], ALU.add).then_inc(x1_made.sem, 1)
                    if i == 0:
                        if not at_first(p):
                            choose(t - 1, p - 1, 1)
                    else:
                        choose(t - 1, p, 0)
                    dve.wait_ge(rooted.sem, rooted.after(t))
                    dve.reciprocal(rstd[:, i:i + 1], rstd[:, i:i + 1]).then_inc(rinv.sem, 1)
                    dve.wait_ge(rinv.sem, rinv.after(t))
                    dve.wait_ge(h2_out[i].sem, h2_out[i].after(p - 1))
                    dve.wait_ge(h2_turned.sem, h2_turned.after(t - 2))
                    dve.scalar_tensor_tensor(out=h2[i][:], in0=x1[i][:], scalar=rstd[:, i:i + 1], in1=wb[:],
                                             op0=ALU.mult, op1=ALU.mult).then_inc(h2_made.sem, 1)
            find_slots(TILES - 2, 0)
            choose(TILES - 1, TILES // 2 - 1, 1)
            find_slots(TILES - 1, 1)

            n = 0

            def link(ins):
                nonlocal n
                n += 1
                ins.then_inc(counted.sem, 1)
                dve.wait_ge(counted.sem, n + 1)

            dve.wait_ge(counted.sem, 1)
            link(dve.tensor_copy(cnt[:], rkp[:, 0:E]))
            link(dve.tensor_scalar(cnt[:], cnt[:], P - 1, None, ALU.add))
            link(dve.tensor_scalar(tl[:], cnt[:], 7, None, ALU.arith_shift_right))
            link(dve.tensor_scalar(nb[:], tl[:], BLOCK_TILES - 1, None, ALU.add))
            link(dve.tensor_scalar(nb[:], nb[:], 2, None, ALU.arith_shift_right))
            link(dve.tensor_scalar(nb[:], nb[:], 1, None, ALU.max))
            link(dve.tensor_copy(tlf[:], tl[:]))
            link(dve.tensor_copy(nbf[:], nb[:]))
            link(dve.tensor_tensor_scan(cum[:], nbf[:], zer[:], 0.0, ALU.add, ALU.add))
            link(dve.tensor_scalar(le[:], cum[:], lane[:, 0:1], None, ALU.is_le))
            link(dve.tensor_reduce(col[:, 0:1], le[:], AX, ALU.add))
            link(dve.tensor_tensor(tmp[:], le[:], nbf[:], ALU.mult))
            link(dve.tensor_reduce(col[:, 1:2], tmp[:], AX, ALU.add))
            link(dve.tensor_scalar(tmp[:], ef[:], col[:, 0:1], None, ALU.is_equal))
            link(dve.tensor_tensor(tmp[:], tmp[:], tlf[:], ALU.mult))
            link(dve.tensor_reduce(col[:, 2:3], tmp[:], AX, ALU.add))
            link(dve.tensor_tensor(col[:, 3:4], lane[:], col[:, 1:2], ALU.subtract))
            link(dve.tensor_scalar(col[:, 4:5], col[:, 3:4], float(-BLOCK_TILES), None, ALU.mult))
            link(dve.tensor_tensor(col[:, 4:5], col[:, 4:5], col[:, 2:3], ALU.add))
            link(dve.tensor_scalar(col[:, 4:5], col[:, 4:5], 0.0, float(BLOCK_TILES), ALU.max, ALU.min))
            link(dve.tensor_scalar(col[:, 5:6], col[:, 0:1], float(E - 1), None, ALU.min))
            link(dve.tensor_scalar(col[:, 6:7], col[:, 5:6], float(S), None, ALU.mult))
            link(dve.scalar_tensor_tensor(out=col[:, 6:7], in0=col[:, 3:4], scalar=float(BLOCK_TILES * P),
                                          in1=col[:, 6:7], op0=ALU.mult, op1=ALU.add))
            link(dve.tensor_scalar(col[:, 6:7], col[:, 6:7], float(SLOTS - BLOCK_TILES * P), None, ALU.min))
            link(dve.tensor_tensor(tmp[:], le[:], tlf[:], ALU.mult))
            link(dve.tensor_reduce(col[:, 7:8], tmp[:], AX, ALU.add))
            link(dve.scalar_tensor_tensor(out=col[:, 7:8], in0=col[:, 3:4], scalar=float(BLOCK_TILES),
                                          in1=col[:, 7:8], op0=ALU.mult, op1=ALU.add))
            link(dve.tensor_scalar(col[:, 7:8], col[:, 7:8], float(MAX_TILES), None, ALU.min))
            link(dve.memset(rowi[:], 0))
            link(dve.tensor_copy(rowi[:, PRIOR:PRIOR + 1], col[:, 7:8]))
            link(dve.tensor_copy(rowi[:, EXPERT:EXPERT + 1], col[:, 5:6]))
            link(dve.tensor_copy(rowi[:, LIVE:LIVE + 1], col[:, 4:5]))
            link(dve.tensor_copy(rowi[:, FIRST:FIRST + 1], col[:, 6:7]))
            dve.tensor_copy(rowi[:, COUNT:COUNT + 1], cum[:, E - 1:E]).then_inc(row_made.sem, 1)

        @blk.tensor
        def _(pe):
            summed.open(pe)
            turned.open(pe)
            h2_turned.open(pe)
            pe.wait_ge(w_lo_made.sem, KD)
            pe.wait_ge(consts_in.sem, 48)
            pe.wait_ge(made.sem, 12)

            def gemm(i, h):
                return three_pass(pe, acc[:, h * H:(h + 1) * H],
                                  lambda k: m_hi[i][:, k * P:(k + 1) * P], lambda k: m_lo[i][:, k * P:(k + 1) * P],
                                  lambda k: w_hi[:, k, h * H:(h + 1) * H], lambda k: w_lo[:, k, h * H:(h + 1) * H],
                                  range(KD))

            def turn_h2(t, i):
                pe.wait_ge(h2_made.sem, h2_made.after(t))
                pe.wait_ge(h2T_made.sem, h2T_made.after(t - 1))
                for k in range(KD):
                    mm = pe.transpose(hT[:, k * P:(k + 1) * P], h2[i][:, k * P:(k + 1) * P], ident[:])
                mm.then_inc(h2_turned.sem, 1)

            def score(t):
                pe.wait_ge(h2T_made.sem, h2T_made.after(t))
                pe.wait_ge(biased.sem, biased.after(t - 1))
                for k in range(KD):
                    mm = pe.matmul(lgp[:, 0:E], h2T[:, k * P:(k + 1) * P], wr[:, k, :],
                                   start=(k == 0), stop=(k == KD - 1))
                mm.then_inc(scored.sem, 1)

            def prefix(t):
                pe.wait_ge(sel_made.sem, sel_made.after(t))
                pe.wait_ge(steps.sem, steps.after(t - 1))
                pe.matmul(rkp[:, 0:E], before[:], sel[:], start=True, stop=False)
                pe.matmul(rkp[:, 0:E], ones[:], taken[:], start=False, stop=True).then_inc(placed.sem, 1)

            for p in peeled(pe, TILES // 2):
                for i in range(2):
                    t = 2 * p + i
                    pe.wait_ge(mg_in[i].sem, mg_in[i].after(p))
                    pe.wait_ge(lo_made.sem, lo_made.after(t - 1))
                    for k in range(KD):
                        mm = pe.transpose(mT[:, k * P:(k + 1) * P], mg[i][:, k * P:(k + 1) * P], ident[:])
                    mm.then_inc(turned.sem, 1)
                    if not at_first(p):
                        prefix(t - 2)
                    pe.wait_ge(lo_made.sem, lo_made.after(t))
                    pe.wait_ge(x1_made.sem, x1_made.after(t - 1))
                    gemm(i, 0)
                    if i == 0:
                        if not at_first(p):
                            turn_h2(t - 1, 1)
                    else:
                        turn_h2(t - 1, 0)
                    gemm(i, 1).then_inc(summed.sem, 1)
                    if i == 0:
                        if not at_first(p):
                            score(t - 1)
                    else:
                        score(t - 1)
            prefix(TILES - 2)
            turn_h2(TILES - 1, 1)
            score(TILES - 1)
            prefix(TILES - 1)
            pe.wait_ge(steps.sem, steps.after(TILES - 1))
            pe.matmul(rkp[:, 0:E], ones[:], taken[:], start=True, stop=True).then_inc(counted.sem, 1)


def run_experts(nc, io, ident, blocks):
    C = 512
    UP = 2 * FF // C
    SLICES = UP + D // C
    HC = C // 2
    with ExitStack() as c:
        def sb(name, shape, dt=F32):
            return c.enter_context(nc.sbuf_tensor(f"e_{name}", shape, dt))

        w_hi = [sb(f"whi{i}", [P, KD, C], F32R) for i in range(2)]
        w_lo = [sb(f"wlo{i}", [P, KD, C], F32R) for i in range(2)]
        raw = sb("raw", [P, KD, C])
        bias = sb("bias", [P, SLICES, C])
        xg = [sb(f"xg{i}", [P, D]) for i in range(BLOCK_TILES)]
        x_hi = [sb(f"xhi{i}", [P, D], F32R) for i in range(BLOCK_TILES)]
        x_lo = [sb(f"xlo{i}", [P, D], F32R) for i in range(BLOCK_TILES)]
        a_hi = [sb(f"ahi{i}", [P, FF], F32R) for i in range(BLOCK_TILES)]
        a_lo = [sb(f"alo{i}", [P, FF], F32R) for i in range(BLOCK_TILES)]
        hid = [sb(f"hid{i}", [P, C]) for i in range(2)]
        glu = [sb(f"glu{i}", [P, HC]) for i in range(2)]
        sg = [sb(f"sg{i}", [P, HC]) for i in range(2)]
        lin = [sb(f"lin{i}", [P, HC]) for i in range(2)]
        av = [sb(f"av{i}", [P, HC]) for i in range(BLOCK_TILES)]
        ys = [sb(f"ys{i}", [P, D]) for i in range(BLOCK_TILES)]
        rec_in, rec_now, rec_out = (sb(f"rec_{n}", [P, BLOCK_TILES, 2], I32) for n in ("in", "now", "out"))
        acc = [c.enter_context(nc.psum_tensor(f"e_acc{i}", [P, C], F32)) for i in range(BLOCK_TILES)]
        aT = [c.enter_context(nc.psum_tensor(f"e_aT{i}", [P, C], F32)) for i in range(2)]
        xT = c.enter_context(nc.psum_tensor("e_xT", [P, D], F32))

        def sig(name, per=1, ahead=0):
            return Signal(io["sems"], nc, f"e_{name}", per, ahead)

        CH = SLICES * KD
        w_in = [sig(f"w_in{k}", 16 * SLICES) for k in range(KD)]
        b_in = [sig(f"b_in{s}", 16) for s in range(SLICES)]
        hi_made, lo_made = sig("hi_made", CH), sig("lo_made", CH, 1)
        rec_loaded, rec_kept, rec_moved, idle = sig("rec_loaded", 16), sig("rec_kept"), sig("rec_moved"), sig("idle")
        x_in, x_turned, x_hi_made, x_lo_made = sig("x_in"), sig("x_turned"), sig("x_hi_made"), sig("x_lo_made")
        y_sent = sig("y_sent")
        up_summed, hid_made, glu_made, sg_made, lin_made, gl_made, av_made, a_turned, a_hi_made, a_lo_made = (
            sig(n) for n in ("up_summed", "hid_made", "glu_made", "sg_made", "lin_made", "gl_made", "av_made",
                             "a_turned", "a_hi_made", "a_lo_made"))
        down_summed, y_made, y_gated = sig("down_summed"), sig("y_made"), sig("y_gated")
        y_copied = sig("y_copied")
        blk = c.enter_context(nc.Block())

        class Block:

            def __init__(self, eng, row):
                self.eng, self.row = eng, row
                self.live = self.get(LIVE, BLOCK_TILES)
                self.prior = self.get(PRIOR, MAX_TILES)

            def get(self, column, top):
                return self.eng.value_load(blocks[0:1, ds(self.row * BLOCK_COLS + column, 1)], min_val=0, max_val=top)

            def up(self, s, i):
                return self.prior * UP + self.live * s + i

            def down(self, s, i):
                return self.prior * (SLICES - UP) + self.live * (s - UP) + i

            def each(self):
                for i in range(BLOCK_TILES):
                    with self.eng.If(self.live > i):
                        yield i

            def tile(self, i):
                return self.eng.If(self.live > i)

        def count(eng):
            return eng.value_load(blocks[0:1, BLOCK_COLS + COUNT:BLOCK_COLS + COUNT + 1], min_val=1, max_val=MAX_BLOCKS)

        def weights(s, e, k):
            rows = slice(k * P, (k + 1) * P)
            if s < UP:
                return io["w_up"][ds(e, 1), rows, s * C:(s + 1) * C].rearrange("a p n -> (a p) n")
            return io["w_down"][ds(e, 1), rows, (s - UP) * C:(s - UP + 1) * C].rearrange("a p n -> (a p) n")

        @blk.sync
        def _(sp):
            def load_slice(b, s, e, prior):
                for k in range(KD):
                    sp.wait_ge(lo_made.sem, lo_made.after(b, (s - 1) * KD + k + 1))
                    sp.dma_start(raw[:, k, :], weights(s, e, k)).then_inc(w_in[k].sem, 16)
                if s < UP:
                    sp.wait_ge(hid_made.sem, prior * UP)
                    src = io["b_up"][ds(e, 1), s * C:(s + 1) * C]
                else:
                    sp.wait_ge(y_made.sem, prior * (SLICES - UP))
                    src = io["b_down"][ds(e, 1), (s - UP) * C:(s - UP + 1) * C]
                sp.dma_start(bias[:, s, :], src.to_broadcast([P, C])).then_inc(b_in[s].sem, 16)

            def load_records(row):
                first = sp.value_load(blocks[0:1, ds(row * BLOCK_COLS + FIRST, 1)], min_val=0,
                                      max_val=SLOTS - BLOCK_TILES * P)
                sp.dma_start(rec_in[:], io["slots"][ds(first, BLOCK_TILES * P), :].rearrange(
                    "(i p) w -> p i w", p=P)).then_inc(rec_loaded.sem, 16)

            load_records(1)
            load_slice(0, 0, 0, 0)
            with sp.Fori(0, count(sp)) as b:
                now = Block(sp, b + 1)
                e = now.get(EXPERT, E - 1)
                for s in range(1, SLICES):
                    load_slice(b, s, e, now.prior)
                    if s == 1:
                        sp.wait_ge(x_in.sem, (now.prior + now.live) * 16)
                        sp.wait_ge(rec_kept.sem, b + 1)
                        load_records(b + 2)
                following = Block(sp, b + 2)
                load_slice(b + 1, 0, following.get(EXPERT, E - 1), following.prior)
            last = Block(sp, count(sp))
            sp.wait_ge(y_sent.sem, (last.prior + last.live) * 16)
            for q in range(4):
                rows = slice(q * S // 4, (q + 1) * S // 4)
                sp.dma_start(io["out"][rows, :], io["sum"][rows, :]).then_inc(y_copied.sem, 16)
            sp.wait_ge(y_copied.sem, 64)

        @blk.gpsimd
        def _(pool):
            def gather(b, block):
                pool.wait_ge(rec_loaded.sem, (b + 1) * 16)
                pool.wait_ge(x_turned.sem, block.prior)
                stand(pool, idle)
                for i in block.each():
                    pool.indirect_dma_start(
                        out=xg[i][:], out_offset=None, in_=io["h2"],
                        in_offset=bass.IndirectOffsetOnAxis(ap=rec_in[:, i, 0:1].bitcast(U32), axis=0)).then_inc(
                            x_in.sem, 16)

            def scatter(block, i):
                with block.tile(i):
                    pool.wait_ge(y_gated.sem, block.down(SLICES - 1, i) + 1)
                    pool.wait_ge(y_sent.sem, (block.prior + i) * 16)
                    pool.wait_ge(rec_moved.sem, block.row)
                    stand(pool, idle)
                    pool.indirect_dma_start(
                        out=io["sum"], out_offset=bass.IndirectOffsetOnAxis(ap=rec_out[:, i, 0:1].bitcast(U32), axis=0),
                        in_=ys[i][:], in_offset=None, compute_op=ALU.add).then_inc(y_sent.sem, 16)

            def move_records(row, before):
                pool.wait_ge(y_sent.sem, before.prior * 16)
                stand(pool, idle)
                pool.tensor_copy(rec_out[:], rec_now[:]).then_inc(rec_moved.sem, 1)
                pool.wait_ge(rec_moved.sem, row + 1)
                stand(pool, idle)

            pool.memset(rec_now[:], 0).then_inc(idle.sem, 1)
            pool.wait_ge(idle.sem, 1)
            gather(0, Block(pool, 1))
            with pool.Fori(0, count(pool)) as b:
                before, now = Block(pool, b), Block(pool, b + 1)
                move_records(b, before)
                pool.wait_ge(y_gated.sem, now.prior * (SLICES - UP))
                pool.wait_ge(rec_loaded.sem, (b + 1) * 16)
                pool.wait_ge(x_in.sem, (now.prior + now.live) * 16)
                stand(pool, idle)
                pool.tensor_copy(rec_now[:], rec_in[:]).then_inc(rec_kept.sem, 1)
                for s in range(UP):
                    for i in now.each():
                        n = now.up(s, i)
                        pool.wait_ge(hid_made.sem, n + 1)
                        pool.wait_ge(av_made.sem, n if i == 0 else n - 1)
                        stand(pool, idle)
                        pool.tensor_scalar(lin[i % 2][:], hid[i % 2][:].rearrange("p (n a) -> p n a", a=2)[:, :, 1],
                                           LIMIT, -LIMIT, ALU.min, ALU.max).then_inc(lin_made.sem, 1)
                    if s == 1:
                        gather(b + 1, Block(pool, b + 2))
                    scatter(before, s)
            last = Block(pool, count(pool))
            move_records(count(pool), last)
            for i in range(BLOCK_TILES):
                scatter(last, i)

        @blk.scalar
        def _(act):
            def split(b, s, free):
                for k in range(KD):
                    act.wait_ge(w_in[k].sem, w_in[k].after(b, 16 * (s + 1)))
                    if k == 0:
                        act.wait_ge(*free)
                    act.copy(w_hi[s % 2][:, k, :], raw[:, k, :]).then_inc(hi_made.sem, 1)

            def split_x(block, i, ups):
                act.wait_ge(x_turned.sem, block.prior + i + 1)
                act.wait_ge(up_summed.sem, ups)
                act.copy(x_hi[i][:], xT[:]).then_inc(x_hi_made.sem, 1)

            def split_a(block, s, i):
                n = block.up(s, i)
                act.wait_ge(a_turned.sem, n + 1)
                act.wait_ge(down_summed.sem, block.prior * (SLICES - UP))
                act.copy(a_hi[i][:, s * HC:(s + 1) * HC], aT[i % 2][:, 0:HC]).then_inc(a_hi_made.sem, 1)

            def gate(block, s, i):
                act.wait_ge(y_made.sem, block.down(s, i) + 1)
                act.wait_ge(rec_kept.sem, block.row)
                cols = ys[i][:, (s - UP) * C:(s - UP + 1) * C]
                act.activation(cols, cols, ACT.Copy, scale=rec_now[:, i, 1:2].bitcast(F32)).then_inc(y_gated.sem, 1)

            split(0, 0, (up_summed.sem, 0))
            first = Block(act, 1)
            for i in first.each():
                split_x(first, i, 0)
            with act.Fori(0, count(act)) as b:
                now = Block(act, b + 1)
                for s in range(UP):
                    split(b, s + 1, (down_summed.sem, now.down(UP, 0)) if s == 0 else (up_summed.sem, now.up(s, 0)))
                    for i in now.each():
                        if s > 0:
                            split_a(now, s - 1, i)
                        act.wait_ge(glu_made.sem, now.up(s, i) + 1)
                        act.activation(sg[i % 2][:], glu[i % 2][:], ACT.Sigmoid, scale=ALPHA).then_inc(sg_made.sem, 1)
                following = Block(act, b + 2)
                for i in range(BLOCK_TILES):
                    with now.tile(i):
                        split_a(now, UP - 1, i)
                    with following.tile(i):
                        split_x(following, i, now.up(UP, 0))
                    if i == 0:
                        split(b, UP + 1, (up_summed.sem, now.up(UP, 0)))
                    with now.tile(i):
                        gate(now, UP, i)
                split(b + 1, 0, (down_summed.sem, now.down(UP + 1, 0)))
                for i in now.each():
                    gate(now, UP + 1, i)

        @blk.vector
        def _(dve):
            lo_made.open(dve)

            def split(b, s):
                for k in range(KD):
                    dve.wait_ge(hi_made.sem, hi_made.after(b, s * KD + k + 1))
                    dve.tensor_tensor(w_lo[s % 2][:, k, :], raw[:, k, :], w_hi[s % 2][:, k, :].bitcast(F32),
                                      ALU.subtract).then_inc(lo_made.sem, 1)

            def split_x(block, i):
                dve.wait_ge(x_hi_made.sem, block.prior + i + 1)
                dve.tensor_tensor(x_lo[i][:], xT[:], x_hi[i][:].bitcast(F32), ALU.subtract).then_inc(x_lo_made.sem, 1)

            def split_a(block, s, i):
                cols = slice(s * HC, (s + 1) * HC)
                dve.wait_ge(a_hi_made.sem, block.up(s, i) + 1)
                dve.tensor_tensor(a_lo[i][:, cols], aT[i % 2][:, 0:HC], a_hi[i][:, cols].bitcast(F32),
                                  ALU.subtract).then_inc(a_lo_made.sem, 1)

            def finish_down(b, block, s, i):
                dve.wait_ge(down_summed.sem, block.down(s, i) + 1)
                dve.wait_ge(b_in[s].sem, b_in[s].after(b))
                dve.wait_ge(y_sent.sem, block.prior * 16)
                dve.tensor_tensor(ys[i][:, (s - UP) * C:(s - UP + 1) * C], acc[i][:], bias[:, s, :],
                                  ALU.add).then_inc(y_made.sem, 1)

            split(0, 0)
            first = Block(dve, 1)
            for i in first.each():
                split_x(first, i)
            with dve.Fori(0, count(dve)) as b:
                now = Block(dve, b + 1)
                for s in range(UP):
                    split(b, s + 1)
                    for i in now.each():
                        n = now.up(s, i)
                        dve.wait_ge(up_summed.sem, n + 1)
                        dve.wait_ge(b_in[s].sem, b_in[s].after(b))
                        dve.wait_ge(lin_made.sem, n if i == 0 else n - 1)
                        dve.tensor_tensor(hid[i % 2][:], acc[i][:], bias[:, s, :], ALU.add).then_inc(hid_made.sem, 1)
                        dve.wait_ge(hid_made.sem, n + 1)
                        dve.tensor_scalar(glu[i % 2][:], hid[i % 2][:].rearrange("p (n a) -> p n a", a=2)[:, :, 0],
                                          LIMIT, None, ALU.min).then_inc(glu_made.sem, 1)
                        if s > 0:
                            split_a(now, s - 1, i)
                        dve.wait_ge(sg_made.sem, n + 1)
                        dve.tensor_tensor(glu[i % 2][:], glu[i % 2][:], sg[i % 2][:], ALU.mult).then_inc(gl_made.sem, 1)
                        dve.wait_ge(gl_made.sem, n + 1)
                        dve.wait_ge(lin_made.sem, n + 1)
                        if s > 0:
                            dve.wait_ge(a_turned.sem, now.up(s - 1, i) + 1)
                        dve.scalar_tensor_tensor(out=av[i][:], in0=lin[i % 2][:], scalar=1.0, in1=glu[i % 2][:],
                                                 op0=ALU.add, op1=ALU.mult).then_inc(av_made.sem, 1)
                following = Block(dve, b + 2)
                for i in range(BLOCK_TILES):
                    with now.tile(i):
                        split_a(now, UP - 1, i)
                    with following.tile(i):
                        split_x(following, i)
                    if i == 0:
                        split(b, UP + 1)
                    with now.tile(i):
                        finish_down(b, now, UP, i)
                split(b + 1, 0)
                for i in now.each():
                    finish_down(b, now, UP + 1, i)

        @blk.tensor
        def _(pe):
            def turn_x(block, i):
                pe.wait_ge(x_in.sem, (block.prior + block.live) * 16)
                pe.wait_ge(x_lo_made.sem, block.prior + i)
                for k in range(KD):
                    mm = pe.transpose(xT[:, k * P:(k + 1) * P], xg[i][:, k * P:(k + 1) * P], ident[:])
                mm.then_inc(x_turned.sem, 1)

            def turn_a(block, s, i):
                n = block.up(s, i)
                pe.wait_ge(av_made.sem, n + 1)
                pe.wait_ge(a_lo_made.sem, n if i == 0 else n - 1)
                for k in range(HC // P):
                    mm = pe.transpose(aT[i % 2][:, k * P:(k + 1) * P], av[i][:, k * P:(k + 1) * P], ident[:])
                mm.then_inc(a_turned.sem, 1)

            def product(s, i, hi, lo):
                return three_pass(pe, acc[i][:], lambda k: hi[i][:, k * P:(k + 1) * P],
                                  lambda k: lo[i][:, k * P:(k + 1) * P],
                                  lambda k: w_hi[s % 2][:, k, :], lambda k: w_lo[s % 2][:, k, :], range(KD))

            first = Block(pe, 1)
            for i in first.each():
                turn_x(first, i)
            with pe.Fori(0, count(pe)) as b:
                now = Block(pe, b + 1)
                for s in range(UP):
                    pe.wait_ge(lo_made.sem, lo_made.after(b, (s + 1) * KD))
                    for i in now.each():
                        if s == 0:
                            pe.wait_ge(x_lo_made.sem, now.prior + i + 1)
                            pe.wait_ge(y_made.sem, now.down(UP, 0))
                        else:
                            pe.wait_ge(hid_made.sem, now.up(s - 1, i) + 1)
                        product(s, i, x_hi, x_lo).then_inc(up_summed.sem, 1)
                        if s > 0:
                            turn_a(now, s - 1, i)
                following = Block(pe, b + 2)
                for s in (UP, UP + 1):
                    for i in range(BLOCK_TILES):
                        if s == UP:
                            with now.tile(i):
                                turn_a(now, UP - 1, i)
                            with following.tile(i):
                                turn_x(following, i)
                        if i == 0:
                            pe.wait_ge(lo_made.sem, lo_made.after(b, (s + 1) * KD))
                            stand(pe, idle)
                        with now.tile(i):
                            if s == UP:
                                pe.wait_ge(a_lo_made.sem, now.up(UP - 1, i) + 1)
                                pe.wait_ge(hid_made.sem, now.up(UP - 1, i) + 1)
                            else:
                                pe.wait_ge(y_made.sem, now.down(UP, i) + 1)
                            product(s, i, a_hi, a_lo).then_inc(down_summed.sem, 1)


def build(nc, io):
    def scratch(name, shape, dt=F32):
        return nc.dram_tensor(name, shape, dt, kind="Internal").ap()

    io = dict(io)
    sems = io["sems"] = []
    io["z"] = scratch("z", (S, ZW))
    io["oT"] = scratch("oT", (TILES, P, 16 * P))
    io["merged"] = scratch("merged", (S, D))
    io["sum"] = scratch("sum", (S + PAD, D))
    io["h2"] = scratch("h2", (S + PAD, D))
    io["slots"] = scratch("slots", (SLOTS, 2), I32)
    io["blocks"] = scratch("blocks", (P + 1, BLOCK_COLS), I32)
    with ExitStack() as c:
        ident = c.enter_context(nc.sbuf_tensor("ident", [P, P], F32))
        eps = c.enter_context(nc.sbuf_tensor("eps", [P, 1], F32))
        io["eps"] = eps
        with ExitStack() as s:
            hT_hi = s.enter_context(nc.sbuf_tensor("hT_hi", [P, KD, S], F32R))
            hT_lo = s.enter_context(nc.sbuf_tensor("hT_lo", [P, KD, S], F32R))
            norm_inputs(nc, io, hT_hi, hT_lo, ident, eps)
            end_stage(nc, sems)
            project_inputs(nc, io, hT_hi, hT_lo)
            end_stage(nc, sems)
        with ExitStack() as s:
            mkT = s.enter_context(nc.sbuf_tensor("mkT", [P, MEM_H, MEM_LEN], F32))
            mv = s.enter_context(nc.sbuf_tensor("mv", [P, MEM_LEN // P, MEM_H * MEM_D], F32))
            prepare_memory(nc, io, ident, eps, mkT, mv)
            end_stage(nc, sems)
            mix_tokens(nc, io, ident, eps, mkT, mv)
            end_stage(nc, sems)
        project_mixers(nc, io)
        end_stage(nc, sems)
        with ExitStack() as s:
            blocks = s.enter_context(nc.sbuf_tensor("blocks_row", [1, (P + 1) * BLOCK_COLS], I32))
            finish_mixing(nc, io, ident, blocks)
            end_stage(nc, sems)
            run_experts(nc, io, ident, blocks)


_INS = ["x", "mem", "mix_norm_w", "mem_norm_w", "w_in", "swa_q_norm_w", "swa_k_norm_w", "swa_sinks", "ret_norm_w",
        "w_mem_kv", "mem_q_norm_w", "mem_k_norm_w", "w_br_swa", "w_br_ret", "w_br_mem", "w_out", "ffn_norm_w",
        "w_router", "b_router", "w_up", "b_up", "w_down", "b_down"]
_MATRICES = {"x", "mem", "w_in", "w_mem_kv", "w_br_swa", "w_br_ret", "w_br_mem", "w_out", "w_router", "w_up", "b_up",
             "w_down", "b_down"}


def kernel(**inputs):
    import numpy as _np
    import concourse.bacc as _bacc
    from concourse import mybir as _mybir
    from concourse.bass_utils import run_bass_kernel_spmd as _run

    nc = _bacc.Bacc("TRN2", target_bir_lowering=False, num_devices=1)
    arrays, io = {}, {}
    given = {name: _np.ascontiguousarray(inputs[name]) for name in _INS}
    for name in _MATRICES:
        given[name] = given[name][0]
    given.update(mixer_constants())
    for name, a in given.items():
        arrays[f"in_{name}"] = a
        io[name] = nc.dram_tensor(f"in_{name}", a.shape, _mybir.dt.from_np(a.dtype), kind="ExternalInput").ap()
    io["out"] = nc.dram_tensor("out_0", (S, D), _mybir.dt.float32, kind="ExternalOutput").ap()
    build(nc, io)
    r = _run(nc, [arrays], core_ids=[0])
    return r.results[0]["out_0"].reshape(1, S, D)
```

```python
from contextlib import ExitStack

import numpy as np

import concourse.bass as bass
from concourse import mybir

F32 = mybir.dt.float32
F32R = mybir.dt.float32r
I32 = mybir.dt.int32
U32 = mybir.dt.uint32
ALU = mybir.AluOpType
ACT = mybir.ActivationFunctionType
AX = mybir.AxisListType.X

P = 128
D = 1024
S = 2048
KD = D // P
TILES = S // P
EPS = 1e-6
NEG = -1e30

SWA_H, SWA_KV, SWA_D = 8, 2, 64
RET_H, RET_DK, RET_DV = 4, 128, 256
MEM_H, MEM_D, MEM_LEN = 4, 128, 256
E, TOPK, FF = 32, 4, 1024
LIMIT, ALPHA = 7.0, 1.702

SQ0 = 0
SK0 = SQ0 + SWA_H * SWA_D
SV0 = SK0 + SWA_KV * SWA_D
RQ0 = SV0 + SWA_KV * SWA_D
RK0 = RQ0 + RET_H * RET_DK
RV0 = RK0 + RET_H * RET_DK
RG0 = RV0 + RET_H * RET_DV
MQ0 = RG0 + RET_H * RET_DV
ZG0 = MQ0 + MEM_H * MEM_D
ZW = ZG0 + 3 * D

PAD = P


class Signal:

    def __init__(self, sems, nc, name, per=1, ahead=0):
        self.sem = nc.alloc_semaphore(name=name)
        sems.append(self.sem)
        self.per, self.ahead = per, ahead

    def open(self, eng):
        eng.sem_inc(self.sem, self.ahead * self.per)

    def after(self, t, j=None):
        return (t + self.ahead) * self.per + (self.per if j is None else j)


def stand(eng, idle):
    eng.sem_inc(idle.sem, 1)


def end_stage(nc, sems):
    nc.clear_and_free_semaphores(sems)
    sems.clear()
    nc.all_engine_barrier()


def at_first(p):
    return isinstance(p, int)


def is_tile(t, n):
    return at_first(t) and t == n


def peeled(eng, n):
    yield 0
    with eng.Fori(1, n) as p:
        yield p


def ds(start, size):
    return bass.ds(start, size)


def below(nc, value, end):
    return nc.s_assert_within(value, 0, end - 1, skip_runtime_bounds_check_because="a branch on the loop register keeps it")


def peeled_ends(eng, n):
    yield 0
    with eng.Fori(1, n - 1) as p:
        yield p
    yield n - 1


def closing(eng, n):
    with eng.Fori(0, n - 1) as p:
        yield p
    yield n - 1


def norm_inputs(nc, io, hT_hi, hT_lo, ident, eps):
    XS = 4
    with ExitStack() as c:
        xs = [c.enter_context(nc.sbuf_tensor(f"n_x{i}", [P, D], F32)) for i in range(XS)]
        sq = c.enter_context(nc.sbuf_tensor("n_sq", [P, D], F32))
        hn = [c.enter_context(nc.sbuf_tensor(f"n_h{i}", [P, D], F32)) for i in range(2)]
        wb = c.enter_context(nc.sbuf_tensor("n_w", [P, D], F32))
        ss = c.enter_context(nc.sbuf_tensor("n_ss", [P, 2], F32))
        rs = c.enter_context(nc.sbuf_tensor("n_rs", [P, 2], F32))
        pt = [c.enter_context(nc.psum_tensor(f"n_pt{i}", [P, D], F32)) for i in range(2)]
        w_in_sb = Signal(io["sems"], nc, "n_w_in", 16)
        x_in = [Signal(io["sems"], nc, f"n_x_in{j}", 16) for j in range(XS)]
        ident_made = Signal(io["sems"], nc, "n_ident")
        squared = Signal(io["sems"], nc, "n_squared", 1, 1)
        rooted = Signal(io["sems"], nc, "n_rooted")
        rstd = Signal(io["sems"], nc, "n_rstd", 1, 2)
        normed = Signal(io["sems"], nc, "n_normed", 1, XS)
        turned = Signal(io["sems"], nc, "n_turned", 1, 2)
        hi_made = Signal(io["sems"], nc, "n_hi", 1)
        lo_made = Signal(io["sems"], nc, "n_lo", 1, 2)
        blk = c.enter_context(nc.Block())

        def tiles(p):
            for j in range(XS):
                yield XS * p + j, j, not (at_first(p) and p == TILES // XS - 1 and j == XS - 1)

        @blk.sync
        def _(sp):
            sp.dma_start(wb[:], io["mix_norm_w"].to_broadcast([P, D])).then_inc(w_in_sb.sem, 16)
            with sp.Fori(0, TILES // XS) as p:
                for t, j, _more in tiles(p):
                    sp.wait_ge(normed.sem, normed.after(t - XS))
                    sp.dma_start(xs[j][:], io["x"][ds(t * P, P), :]).then_inc(x_in[j].sem, 16)

        @blk.gpsimd
        def _(pool):
            make_identity(pool, ident, ident_made)
            pool.memset(eps[:], EPS).then_inc(ident_made.sem, 1)

        @blk.scalar
        def _(act):
            def root(t, j, r):
                act.wait_ge(x_in[j].sem, x_in[j].after(r))
                act.wait_ge(squared.sem, squared.after(t - 1))
                act.wait_ge(rstd.sem, rstd.after(t - 2))
                act.activation(sq[:], xs[j][:], ACT.Square,
                               accum_out=ss[:, j % 2:j % 2 + 1]).then_inc(squared.sem, 1)
                act.wait_ge(squared.sem, squared.after(t))
                act.wait_ge(normed.sem, normed.after(t - 2))
                act.activation(rs[:, j % 2:j % 2 + 1], ss[:, j % 2:j % 2 + 1], ACT.Sqrt, scale=1.0 / D,
                               bias=eps[:, 0:1]).then_inc(rooted.sem, 1)

            squared.open(act)
            act.preload_act_table(ACT.Sqrt)
            act.wait_ge(ident_made.sem, 3)
            root(0, 0, 0)
            for p in closing(act, TILES // XS):
                for t, j, more in tiles(p):
                    if more:
                        root(t + 1, (j + 1) % XS, p + (j + 1) // XS)
                    act.wait_ge(turned.sem, turned.after(t))
                    act.copy(hT_hi[:, :, ds(t * P, P)],
                             pt[j % 2][:].rearrange("p (k n) -> p k n", k=KD)).then_inc(hi_made.sem, 1)

        @blk.vector
        def _(dve):
            def norm(t, j):
                i = j % 2
                dve.wait_ge(rooted.sem, rooted.after(t))
                dve.reciprocal(rs[:, i:i + 1], rs[:, i:i + 1]).then_inc(rstd.sem, 1)
                dve.wait_ge(rstd.sem, rstd.after(t))
                dve.wait_ge(turned.sem, turned.after(t - 2))
                dve.scalar_tensor_tensor(out=hn[i][:], in0=xs[j][:], scalar=rs[:, i:i + 1], in1=wb[:],
                                         op0=ALU.mult, op1=ALU.mult).then_inc(normed.sem, 1)

            normed.open(dve)
            lo_made.open(dve)
            rstd.open(dve)
            dve.wait_ge(w_in_sb.sem, 16)
            norm(0, 0)
            for p in closing(dve, TILES // XS):
                for t, j, more in tiles(p):
                    if more:
                        norm(t + 1, (j + 1) % XS)
                    dve.wait_ge(turned.sem, turned.after(t))
                    dve.wait_ge(hi_made.sem, hi_made.after(t))
                    dve.tensor_tensor(hT_lo[:, :, ds(t * P, P)],
                                      pt[j % 2][:].rearrange("p (k n) -> p k n", k=KD),
                                      hT_hi[:, :, ds(t * P, P)].bitcast(F32),
                                      ALU.subtract).then_inc(lo_made.sem, 1)

        @blk.tensor
        def _(pe):
            turned.open(pe)
            pe.wait_ge(ident_made.sem, 2)
            with pe.Fori(0, TILES // XS) as p:
                for t, j, _more in tiles(p):
                    i = j % 2
                    pe.wait_ge(normed.sem, normed.after(t))
                    pe.wait_ge(lo_made.sem, lo_made.after(t - 2))
                    for k in range(KD):
                        mm = pe.transpose(pt[i][:, k * P:(k + 1) * P], hn[i][:, k * P:(k + 1) * P], ident[:])
                    mm.then_inc(turned.sem, 1)


def make_identity(pool, ident, made):
    pool.memset(ident[:], 0.0).then_inc(made.sem, 1)
    pool.wait_ge(made.sem, 1)
    pool.affine_select(out=ident[:], in_=ident[:], compare_op=ALU.not_equal, fill=1.0, base=0,
                       pattern=[[-1, P]], channel_multiplier=1).then_inc(made.sem, 1)


def three_pass(pe, out, x_hi, x_lo, w_hi, w_lo, chunks, now=None):
    for k in now or chunks:
        first, last = k == chunks[0], k == chunks[-1]
        pe.matmul(out, x_hi(k), w_hi(k), start=first, stop=False)
        pe.matmul(out, x_hi(k), w_lo(k), start=False, stop=False)
        mm = pe.matmul(out, x_lo(k), w_hi(k), start=False, stop=last)
    return mm


def project_inputs(nc, io, hT_hi, hT_lo):
    GROUPS = 16
    G = ZW // GROUPS
    RAW, BANKS, OUTS = 4, 8, 4
    with ExitStack() as c:
        raw = [c.enter_context(nc.sbuf_tensor(f"p_raw{i}", [P, G], F32)) for i in range(RAW)]
        w_hi = [c.enter_context(nc.sbuf_tensor(f"p_hi{i}", [P, KD, G], F32R)) for i in range(2)]
        w_lo = [c.enter_context(nc.sbuf_tensor(f"p_lo{i}", [P, KD, G], F32R)) for i in range(2)]
        zs = [c.enter_context(nc.sbuf_tensor(f"p_z{i}", [P, G], F32)) for i in range(OUTS)]
        acc = [c.enter_context(nc.psum_tensor(f"p_acc{i}", [P, 512], F32)) for i in range(BANKS)]
        raw_in = [Signal(io["sems"], nc, f"p_raw_in{i}", 16 * KD // RAW) for i in range(RAW)]
        hi_made = Signal(io["sems"], nc, "p_hi_made", KD)
        lo_made = Signal(io["sems"], nc, "p_lo_made", KD, 1)
        summed = Signal(io["sems"], nc, "p_summed", TILES, 2)
        copied = Signal(io["sems"], nc, "p_copied", TILES, 1)
        z_out = [Signal(io["sems"], nc, f"p_z_out{i}", 16 * TILES // OUTS, 1) for i in range(OUTS)]
        blk = c.enter_context(nc.Block())

        @blk.sync
        def _(sp):
            def load(g, k):
                sp.wait_ge(lo_made.sem, lo_made.after(g, k + 1 - RAW))
                sp.dma_start(raw[k % RAW][:], io["w_in"][k * P:(k + 1) * P, ds(g * G, G)]).then_inc(
                    raw_in[k % RAW].sem, 16)

            for z in z_out:
                z.open(sp)
            for k in range(KD):
                load(0, k)
            with sp.Fori(0, GROUPS // 2) as p:
                for b in range(2):
                    g = 2 * p + b

                    def load_next():
                        for k in range(KD):
                            load(below(nc, g + 1, GROUPS), k)

                    if b == 0:
                        load_next()
                    else:
                        with sp.If(p < GROUPS // 2 - 1):
                            load_next()
                    for i in range(TILES):
                        sp.wait_ge(copied.sem, copied.after(g, i + 1))
                        sp.dma_start(io["z"][i * P:(i + 1) * P, ds(g * G, G)],
                                     zs[i % OUTS][:]).then_inc(z_out[i % OUTS].sem, 16)
            for z in z_out:
                sp.wait_ge(z.sem, z.after(GROUPS - 1))

        @blk.scalar
        def _(act):
            copied.open(act)

            def split(g, k, b):
                act.wait_ge(raw_in[k % RAW].sem, raw_in[k % RAW].after(g, 16 * (k // RAW + 1)))
                act.wait_ge(summed.sem, summed.after(g - 2))
                act.copy(w_hi[b][:, k, :], raw[k % RAW][:]).then_inc(hi_made.sem, 1)

            for k in range(KD):
                split(0, k, 0)
            with act.Fori(0, GROUPS // 2) as p:
                for b in range(2):
                    g = 2 * p + b

                    def split_next():
                        for k in range(KD):
                            split(g + 1, k, 1 - b)

                    if b == 0:
                        split_next()
                    else:
                        with act.If(p < GROUPS // 2 - 1):
                            split_next()
                    for i in range(TILES):
                        act.wait_ge(summed.sem, summed.after(g, i + 1))
                        j = 16 * (i // OUTS)
                        act.wait_ge(z_out[i % OUTS].sem, z_out[i % OUTS].after(g, j))
                        act.copy(zs[i % OUTS][:], acc[i % BANKS][:, 0:G]).then_inc(copied.sem, 1)

        @blk.vector
        def _(dve):
            lo_made.open(dve)

            def split(g, k, b):
                dve.wait_ge(hi_made.sem, hi_made.after(g, k + 1))
                dve.tensor_tensor(w_lo[b][:, k, :], raw[k % RAW][:], w_hi[b][:, k, :].bitcast(F32),
                                  ALU.subtract).then_inc(lo_made.sem, 1)

            for k in range(KD):
                split(0, k, 0)
            with dve.Fori(0, GROUPS // 2) as p:
                for b in range(2):
                    def split_next():
                        for k in range(KD):
                            split(2 * p + b + 1, k, 1 - b)

                    if b == 0:
                        split_next()
                    else:
                        with dve.If(p < GROUPS // 2 - 1):
                            split_next()

        @blk.tensor
        def _(pe):
            summed.open(pe)
            with pe.Fori(0, GROUPS // 2) as p:
                for b in range(2):
                    g = 2 * p + b
                    pe.wait_ge(lo_made.sem, lo_made.after(g))
                    for i in range(TILES):
                        pe.wait_ge(copied.sem, copied.after(g, i + 1 - BANKS))
                        rows = slice(i * P, (i + 1) * P)
                        three_pass(pe, acc[i % BANKS][:, 0:G],
                                   lambda k: hT_hi[:, k, rows], lambda k: hT_lo[:, k, rows],
                                   lambda k: w_hi[b][:, k, :], lambda k: w_lo[b][:, k, :],
                                   range(KD)).then_inc(summed.sem, 1)
def prepare_memory(nc, io, ident, eps, mkT, mv):
    MT = MEM_LEN // P
    W = MEM_H * MEM_D
    with ExitStack() as c:
        ms_in = c.enter_context(nc.sbuf_tensor("m_x", [P, MT, D], F32))
        wkv = c.enter_context(nc.sbuf_tensor("m_wkv", [P, KD, 2 * W], F32))
        wb = c.enter_context(nc.sbuf_tensor("m_w", [P, D], F32))
        kw = c.enter_context(nc.sbuf_tensor("m_kw", [P, 1], F32))
        kws = c.enter_context(nc.sbuf_tensor("m_kws", [P, 1], F32))
        sq = c.enter_context(nc.sbuf_tensor("m_sq", [P, MT, D], F32))
        hn = c.enter_context(nc.sbuf_tensor("m_h", [P, MT, D], F32))
        hT = c.enter_context(nc.sbuf_tensor("m_hT", [P, MT, D], F32))
        mk = c.enter_context(nc.sbuf_tensor("m_k", [P, MT, W], F32))
        ss = c.enter_context(nc.sbuf_tensor("m_ss", [P, MT], F32))
        ks = c.enter_context(nc.sbuf_tensor("m_ks", [P, MT * MEM_H], F32))
        pt = [c.enter_context(nc.psum_tensor(f"m_pt{i}", [P, D], F32)) for i in range(MT)]
        pk = [c.enter_context(nc.psum_tensor(f"m_pk{i}", [P, 2 * W], F32)) for i in range(MT)]
        loaded = Signal(io["sems"], nc, "m_loaded", 16)
        w_loaded = Signal(io["sems"], nc, "m_w_loaded", 16)
        squared = Signal(io["sems"], nc, "m_squared")
        rooted = Signal(io["sems"], nc, "m_rooted")
        normed = Signal(io["sems"], nc, "m_normed")
        turned = Signal(io["sems"], nc, "m_turned")
        hT_made = Signal(io["sems"], nc, "m_hT_made")
        summed = Signal(io["sems"], nc, "m_summed")
        k_squared = Signal(io["sems"], nc, "m_k_squared")
        k_rooted = Signal(io["sems"], nc, "m_k_rooted")
        k_normed = Signal(io["sems"], nc, "m_k_normed")
        k_turned = Signal(io["sems"], nc, "m_k_turned")
        made = Signal(io["sems"], nc, "m_made")
        steps = Signal(io["sems"], nc, "m_steps")
        blk = c.enter_context(nc.Block())

        @blk.sync
        def _(sp):
            sp.dma_start(ms_in[:], io["mem"].rearrange("(m p) d -> p m d", p=P)).then_inc(loaded.sem, 16)
            sp.dma_start(wb[:], io["mem_norm_w"].to_broadcast([P, D])).then_inc(loaded.sem, 16)
            sp.dma_start(kw[:], io["mem_k_norm_w"].rearrange("a (p o) -> (a p) o", o=1)).then_inc(loaded.sem, 16)
            for k in range(0, KD, 2):
                sp.dma_start(wkv[:, k:k + 2, :], io["w_mem_kv"][k * P:(k + 2) * P, :].rearrange(
                    "(k p) n -> p k n", p=P)).then_inc(w_loaded.sem, 16)

        @blk.scalar
        def _(act):
            act.preload_act_table(ACT.Sqrt)
            act.wait_ge(loaded.sem, 48)
            for m in range(MT):
                act.activation(sq[:, m, :], ms_in[:, m, :], ACT.Square,
                               accum_out=ss[:, m:m + 1]).then_inc(squared.sem, 1)
            act.wait_ge(squared.sem, MT)
            act.activation(ss[:], ss[:], ACT.Sqrt, scale=1.0 / D, bias=eps[:, 0:1]).then_inc(rooted.sem, 1)
            for m in range(MT):
                act.wait_ge(turned.sem, m + 1)
                act.copy(hT[:, m, :], pt[m][:]).then_inc(hT_made.sem, 1)
            for m in range(MT):
                act.wait_ge(summed.sem, m + 1)
                for h in range(MEM_H):
                    cols = slice(h * MEM_D, (h + 1) * MEM_D)
                    act.activation(sq[:, m, cols], pk[m][:, cols], ACT.Square,
                                   accum_out=ks[:, m * MEM_H + h:m * MEM_H + h + 1]).then_inc(k_squared.sem, 1)
            act.wait_ge(k_squared.sem, MT * MEM_H)
            act.activation(ks[:], ks[:], ACT.Sqrt, scale=1.0 / MEM_D, bias=eps[:, 0:1]).then_inc(k_rooted.sem, 1)

        @blk.vector
        def _(dve):
            dve.wait_ge(rooted.sem, 1)
            dve.reciprocal(ss[:], ss[:]).then_inc(steps.sem, 1)
            dve.wait_ge(steps.sem, 1)
            for m in range(MT):
                dve.scalar_tensor_tensor(out=hn[:, m, :], in0=ms_in[:, m, :], scalar=ss[:, m:m + 1],
                                         in1=wb[:], op0=ALU.mult, op1=ALU.mult).then_inc(normed.sem, 1)
            dve.tensor_scalar(kws[:], kw[:], float(MEM_D) ** -0.5, None, ALU.mult).then_inc(steps.sem, 1)
            dve.wait_ge(k_rooted.sem, 1)
            dve.reciprocal(ks[:], ks[:]).then_inc(steps.sem, 1)
            dve.wait_ge(steps.sem, 3)
            for m in range(MT):
                dve.wait_ge(summed.sem, m + 1)
                dve.tensor_tensor(mk[:, m, :].rearrange("p (h d) -> p h d", h=MEM_H),
                                  pk[m][:, 0:W].rearrange("p (h d) -> p h d", h=MEM_H),
                                  ks[:, m * MEM_H:(m + 1) * MEM_H].unsqueeze(2).to_broadcast([P, MEM_H, MEM_D]),
                                  ALU.mult).then_inc(k_normed.sem, 1)
                dve.tensor_copy(mv[:, m, :], pk[m][:, W:2 * W]).then_inc(made.sem, 1)
            for m in range(MT):
                dve.wait_ge(k_turned.sem, m + 1)
                dve.tensor_scalar(mkT[:, :, m * P:(m + 1) * P],
                                  pt[m][:, 0:W].rearrange("p (h n) -> p h n", h=MEM_H), kws[:, 0:1], None,
                                  ALU.mult).then_inc(made.sem, 1)

        @blk.tensor
        def _(pe):
            for m in range(MT):
                pe.wait_ge(normed.sem, m + 1)
                for k in range(KD):
                    mm = pe.transpose(pt[m][:, k * P:(k + 1) * P], hn[:, m, k * P:(k + 1) * P], ident[:])
                mm.then_inc(turned.sem, 1)
            pe.wait_ge(w_loaded.sem, 16 * KD // 2)
            for m in range(MT):
                pe.wait_ge(hT_made.sem, m + 1)
                for n in range(2):
                    for k in range(KD):
                        mm = pe.matmul(pk[m][:, n * W:(n + 1) * W], hT[:, m, k * P:(k + 1) * P],
                                       wkv[:, k, n * W:(n + 1) * W], start=(k == 0), stop=(k == KD - 1))
                mm.then_inc(summed.sem, 1)
            for m in range(MT):
                pe.wait_ge(k_normed.sem, m + 1)
                for h in range(MEM_H):
                    mm = pe.transpose(pt[m][:, h * P:(h + 1) * P], mk[:, m, h * MEM_D:(h + 1) * MEM_D], ident[:])
                mm.then_inc(k_turned.sem, 1)


CONSTS = 12
PREPARED = 5


def inverse_root(dve, out, x, tmp, steps, t):
    def wait(n):
        dve.wait_ge(steps.sem, steps.after(t, n))

    dve.tensor_scalar(out[:].bitcast(I32), x[:].bitcast(I32), -0.5, float(0x5f3759df), ALU.mult,
                      ALU.add).then_inc(steps.sem, 1)
    for n in range(3):
        wait(3 * n + 1)
        dve.tensor_tensor(tmp[:], out[:], out[:], ALU.mult).then_inc(steps.sem, 1)
        wait(3 * n + 2)
        dve.scalar_tensor_tensor(out=tmp[:], in0=tmp[:], scalar=-0.5, in1=x[:], op0=ALU.mult,
                                 op1=ALU.mult).then_inc(steps.sem, 1)
        wait(3 * n + 3)
        dve.scalar_tensor_tensor(out=out[:], in0=tmp[:], scalar=1.5, in1=out[:], op0=ALU.add,
                                 op1=ALU.mult).then_inc(steps.sem, 1)
    wait(10)


class Region:

    def __init__(self, ctx, sems, nc, name, banks, takes):
        self.ps = ctx.enter_context(nc.psum_tensor(f"{name}_ps", [P, banks * 512], F32))
        self.takes = takes
        self.filled = Signal(sems, nc, f"{name}_filled", len(takes))
        self.taken = Signal(sems, nc, f"{name}_taken", sum(takes), 1)

    def wait_free(self, eng, t, use):
        eng.wait_ge(self.taken.sem, self.taken.after(t, sum(self.takes[:use])))

    def wait_filled(self, eng, t, use):
        eng.wait_ge(self.filled.sem, self.filled.after(t, use + 1))

    def wait_taken(self, eng, t, use):
        eng.wait_ge(self.taken.sem, self.taken.after(t, sum(self.takes[:use + 1])))


class Tile:

    def __init__(self, r, i):
        self.r, self.i, self.t = r, i, 2 * r + i

    def plus(self, n):
        return Tile(self.r + (self.i + n) // 2, (self.i + n) % 2)


def pipelined(eng, prepare, step):
    prepare(Tile(0, 0))
    step(Tile(0, 1), Tile(0, 0), None)
    with eng.Fori(0, TILES // 2 - 1) as r:
        for now in (Tile(r, 1), Tile(r, 1).plus(1)):
            step(now.plus(1), now, now.plus(-1))
    last = Tile(TILES // 2 - 1, 1)
    step(None, last, last.plus(-1))
    step(None, None, last)


def mix_tokens(nc, io, ident, mkT, mv):
    NH = SWA_H + SWA_KV
    QK = NH * SWA_D
    MW = MEM_H * MEM_D
    RQ = RET_H * RET_DK
    RV = RET_H * RET_DV
    HALF = RET_DK // 2
    lg = np.log1p(-(2.0 ** (-5.0 - np.arange(RET_H, dtype=np.float32)))).astype(np.float32)
    chunk_decay = [float(np.exp(np.float32(P) * g)) for g in lg]
    with ExitStack() as c:
        def sb(name, cols, n=1):
            got = [c.enter_context(nc.sbuf_tensor(f"x_{name}{i}", [P, cols], F32)) for i in range(n)]
            return got if n > 1 else got[0]

        zt = sb("z", ZG0, 2)
        rope = sb("rope", 4 * HALF, 2)
        oT = sb("oT", 16 * P, 2)
        kT, vals = sb("kT", P, 2), sb("vals", P, 2)
        sq, ss, root, rstd = sb("sq", QK + MW), sb("ss", NH + MEM_H), sb("root", NH + MEM_H), sb("rstd", NH + MEM_H)
        qn, mqn = sb("qn", QK), sb("mqn", MW)
        qc, qs, kc, ks = sb("qc", RQ), sb("qs", RQ), sb("kc", RQ), sb("ks", RQ)
        rqn, rkn, rkd = sb("rqn", RQ), sb("rkn", RQ), sb("rkd", RQ, 2)
        qT, mqT, rqT, rqdT, rkT = sb("qT", 4 * P), sb("mqT", MW), sb("rqT", RQ), sb("rqdT", RQ), sb("rkT", RQ)
        probs, probsT = sb("probs", SWA_H * 2 * P, 2), sb("probsT", SWA_H * 2 * P)
        mprobs, mprobsT = sb("mprobs", MEM_H * MEM_LEN), sb("mprobsT", MEM_H * MEM_LEN)
        inT = sb("inT", RET_H * P)
        state = sb("state", RV)
        tanh, gate, rgw, rnorm = sb("tanh", RV), sb("gate", RV), sb("rgw", RV), sb("rnorm", RV)
        decayT, qdec, kdec = sb("decayT", RET_H * P), sb("qdec", RET_H * P), sb("kdec", RET_H)
        mask, mask_first = sb("mask", 2 * P), sb("mask_first", 2 * P)
        sinks, wq, wk, wm, wret = sb("sinks", SWA_H), sb("wq", 1), sb("wk", 1), sb("wm", 1), sb("wret", RV)
        mx, neg, sk, rsum, rinv = (sb(n, SWA_H) for n in ("mx", "neg", "sk", "rsum", "rinv"))
        mmx, mneg, mrsum, mrinv = (sb(n, MEM_H) for n in ("mmx", "mneg", "mrsum", "mrinv"))
        st, mva, var, rr, rroot = sb("st", RET_H * 6), sb("mva", RET_H * 2), sb("var", RET_H), sb("rr", RET_H), sb("rroot", RET_H)

        F1 = Region(c, io["sems"], nc, "f1", 1, (1, 1, 1))
        F2 = Region(c, io["sems"], nc, "f2", 1, (1, 2, 1))
        S_ps = c.enter_context(nc.psum_tensor("scores_ps", [P, 1024], F32))
        O = Region(c, io["sems"], nc, "o", 2, (RET_H,))
        T = [Region(c, io["sems"], nc, f"t{n}", 1, (2, 1, 1, 1, 1, 1)) for n in range(2)]

        def sig(name, per=1, ahead=0):
            return Signal(io["sems"], nc, f"x_{name}", per, ahead)

        consts_in, prepared, idle = sig("consts_in", 16), sig("prepared"), sig("idle")
        z_in = [sig(f"z_in{i}", 48) for i in range(2)]
        v_in = [sig(f"v_in{i}", 16) for i in range(2)]
        o_out = [sig(f"o_out{i}", 16, 1) for i in range(2)]
        squared, ssum, scaled, rstd_steps, qn_made = (
            sig("squared", 2), sig("ssum", 2), sig("scaled", 2), sig("rstd_steps", 10), sig("qn_made", 4))
        roped, rot_made, kd_made = sig("roped", 4), sig("rot_made", 4), sig("kd_made")
        tanh_made, rgw_made, gate_made = sig("tanh_made"), sig("rgw_made"), sig("gate_made")
        scored, masked = sig("scored", 3), sig("masked", 2, 1)
        mmaxed, mnegated, mexped, minverted, mprobs_made = (
            sig("mmaxed"), sig("mnegated"), sig("mexped", MEM_H), sig("minverted"), sig("mprobs_made"))
        maxed, topped, negated, exped, dened, inverted, probs_made = (
            sig("maxed", 2), sig("topped"), sig("negated", 2), sig("exped", SWA_H + 1), sig("dened"),
            sig("inverted"), sig("probs_made"))
        vals_made = sig("vals_made")
        stated, aggregated, rscaled, rroot_steps, gated = (
            sig("stated", RET_H), sig("aggregated", RET_H), sig("rscaled"), sig("rroot_steps", 10), sig("gated"))
        blk = c.enter_context(nc.Block())
        z_dram, o_dram = io["z"], io["oT"]

        def heads(ap, h):
            return ap.rearrange("p (h d) -> p h d", h=h)

        def pairs(q):
            return q[:, 0:SWA_H * SWA_D].rearrange("p (j g d) -> p j g d", g=SWA_KV, d=SWA_D)

        def col(w, n):
            return w.unsqueeze(2).to_broadcast([P, w.shape[1], n])

        def halves(b, use):
            return [(T[n], b.t, use) for n in range(2)]

        QUARTERS = ((1, 2), (0, 3), (1, 3), (0, 4))

        @blk.sync
        def _(sp):
            loads = ((decayT[:], io["decayT"]), (qdec[:], io["qdec"].to_broadcast([P, RET_H * P])),
                     (kdec[:], io["kdec"]), (mask[:], io["mask"]), (mask_first[:], io["mask_first"]),
                     (sinks[:], io["swa_sinks"].to_broadcast([P, SWA_H])),
                     (wq[0:SWA_D, :], io["swa_q_norm_w"].rearrange("a (p o) -> (a p) o", o=1)),
                     (wq[SWA_D:P, :], io["swa_q_norm_w"].rearrange("a (p o) -> (a p) o", o=1)),
                     (wk[0:SWA_D, :], io["swa_k_norm_w"].rearrange("a (p o) -> (a p) o", o=1)),
                     (wk[SWA_D:P, :], io["swa_k_norm_w"].rearrange("a (p o) -> (a p) o", o=1)),
                     (wm[:], io["mem_q_norm_w"].rearrange("a (p o) -> (a p) o", o=1)),
                     (wret[:], io["ret_norm_w"].to_broadcast([P, RV])))
            assert len(loads) == CONSTS

            def load(a):
                for cols in (slice(0, RV0), slice(RG0, ZG0)):
                    sp.dma_start(zt[a.i][:, cols], z_dram[ds(a.t * P, P), cols]).then_inc(z_in[a.i].sem, 16)
                sp.dma_start(rope[a.i][:], io["rope"][ds(a.t * P, P), :]).then_inc(z_in[a.i].sem, 16)

            def load_values(a):
                sp.dma_start(zt[a.i][:, RV0:RG0], z_dram[ds(a.t * P, P), RV0:RG0]).then_inc(v_in[a.i].sem, 16)

            def store(b):
                for region in T:
                    region.wait_taken(sp, b.t, 5)
                sp.dma_start(o_dram[ds(b.t, 1), :, :].rearrange("a p n -> (a p) n"), oT[b.i][:]).then_inc(
                    o_out[b.i].sem, 16)

            load(Tile(0, 0))
            for dst, src in loads:
                sp.dma_start(dst, src).then_inc(consts_in.sem, 16)
            for o in o_out:
                o.open(sp)
            load_values(Tile(0, 0))
            load(Tile(0, 1))
            load_values(Tile(0, 1))
            with sp.Fori(0, TILES // 2 - 1) as r:
                for b in (Tile(r, 0), Tile(r, 1)):
                    sp.wait_ge(vals_made.sem, vals_made.after(b.t))
                    sp.wait_ge(rgw_made.sem, rgw_made.after(b.t))
                    load(b.plus(2))
                    T[1].wait_filled(sp, b.t, 0)
                    load_values(b.plus(2))
                    store(b)
            last = Tile(TILES // 2 - 1, 0)
            store(last)
            store(last.plus(1))
            for o in o_out:
                sp.wait_ge(o.sem, o.after(TILES // 2 - 1))

        @blk.gpsimd
        def _(pool):
            def prepare(a):
                t, z = a.t, zt[a.i]
                pool.wait_ge(z_in[a.i].sem, z_in[a.i].after(a.r))
                if not is_tile(t, 0):
                    pool.wait_ge(rot_made.sem, rot_made.after(t - 1))
                for x0, dst, tab in ((RQ0, qc, 0), (RQ0, qs, 1), (RK0, kc, 2), (RK0, ks, 3)):
                    pool.tensor_tensor(
                        dst[:].rearrange("p (a d) -> p a d", d=HALF),
                        z[:, x0:x0 + RQ].rearrange("p (a d) -> p a d", d=HALF),
                        rope[a.i][:, tab * HALF:(tab + 1) * HALF].unsqueeze(1).to_broadcast([P, 2 * RET_H, HALF]),
                        ALU.mult).then_inc(roped.sem, 1)
                if not (is_tile(t, 0) or is_tile(t, 1)):
                    T[1].wait_filled(pool, t - 2, 0)
                pool.wait_ge(rot_made.sem, rot_made.after(t))
                pool.tensor_tensor(heads(rkd[a.i][:], RET_H), heads(rkn[:], RET_H), col(kdec[:], RET_DK),
                                   ALU.mult).then_inc(kd_made.sem, 1)

            def step(a, f, b):
                if b:
                    pool.wait_ge(inverted.sem, inverted.after(b.t))
                    pool.tensor_tensor(heads(probs[b.i][:], SWA_H), heads(probs[b.i][:], SWA_H), col(rinv[:], 2 * P),
                                       ALU.mult).then_inc(probs_made.sem, 1)
                if f:
                    if b:
                        pool.wait_ge(gate_made.sem, gate_made.after(b.t))
                    pool.tensor_tensor(rgw[:], zt[f.i][:, RG0:RG0 + RV], wret[:], ALU.mult).then_inc(rgw_made.sem, 1)
                    pool.wait_ge(minverted.sem, minverted.after(f.t))
                    pool.tensor_tensor(heads(mprobs[:], MEM_H), heads(mprobs[:], MEM_H), col(mrinv[:], MEM_LEN),
                                       ALU.mult).then_inc(mprobs_made.sem, 1)
                if a:
                    prepare(a)

            pool.wait_ge(consts_in.sem, 16 * CONSTS)
            pool.wait_ge(prepared.sem, PREPARED)
            pipelined(pool, prepare, step)

        @blk.scalar
        def _(act):
            def prepare(a):
                t, z = a.t, zt[a.i]
                act.wait_ge(z_in[a.i].sem, z_in[a.i].after(a.r))
                if not is_tile(t, 0):
                    act.wait_ge(ssum.sem, ssum.after(t - 1))
                act.activation(sq[:, 0:QK], z[:, 0:QK], ACT.Square).then_inc(squared.sem, 1)
                act.activation(sq[:, QK:QK + MW], z[:, MQ0:MQ0 + MW], ACT.Square).then_inc(squared.sem, 1)

            def take(region, t, use, out, cols=512):
                region.wait_filled(act, t, use)
                act.copy(out, region.ps[:, 0:cols]).then_inc(region.taken.sem, 1)

            def probs_turned(b, quarters):
                for q in quarters:
                    n, use = QUARTERS[q]
                    take(T[n], b.t, use, probsT[:, q * 512:(q + 1) * 512])

            def step(a, f, b):
                if b:
                    if not is_tile(b.t, 0):
                        act.wait_ge(T[1].filled.sem, T[1].filled.after(b.t, 0))
                    act.copy(vals[b.i][:], zt[b.i][:, SV0:SV0 + P]).then_inc(vals_made.sem, 1)
                if f:
                    t = f.t
                    F1.wait_filled(act, t, 0)
                    act.activation(mqT[:], F1.ps[:, 0:MW], ACT.Copy, scale=wm[:, 0:1]).then_inc(F1.taken.sem, 1)
                    F2.wait_filled(act, t, 0)
                    act.activation(kT[f.i][:], F2.ps[:, 0:P], ACT.Copy, scale=wk[:, 0:1]).then_inc(F2.taken.sem, 1)
                    F1.wait_filled(act, t, 1)
                    act.activation(qT[:], F1.ps[:, 0:4 * P], ACT.Copy, scale=wq[:, 0:1]).then_inc(F1.taken.sem, 1)
                    take(F1, t, 2, rkT[:])
                if b:
                    for n, (region, bt, use) in enumerate(halves(b, 1)):
                        take(region, bt, use, mprobsT[:, n * 512:(n + 1) * 512])
                if f:
                    act.wait_ge(mnegated.sem, mnegated.after(t))
                    for h in range(MEM_H):
                        cols = slice(h * MEM_LEN, (h + 1) * MEM_LEN)
                        act.activation(mprobs[:, cols], S_ps[:, cols], ACT.Exp, bias=mneg[:, h:h + 1],
                                       accum_out=mrsum[:, h:h + 1]).then_inc(mexped.sem, 1)
                if b:
                    act.wait_ge(o_out[b.i].sem, o_out[b.i].after(b.r - 1))
                    take(T[0], b.t, 2, oT[b.i][:, 12 * P:16 * P])
                    probs_turned(b, (0, 1))
                if a:
                    prepare(a)
                if b:
                    probs_turned(b, (2, 3))
                if f:
                    if b:
                        act.wait_ge(gate_made.sem, gate_made.after(b.t))
                    act.activation(tanh[:], zt[f.i][:, RG0:RG0 + RV], ACT.Tanh, scale=0.5).then_inc(tanh_made.sem, 1)
                if b:
                    take(T[1], b.t, 4, oT[b.i][:, 0:4 * P])
                    for n, (region, bt, use) in enumerate(halves(b, 5)):
                        take(region, bt, use, oT[b.i][:, (4 + 4 * n) * P:(8 + 4 * n) * P])
                if f:
                    act.wait_ge(negated.sem, negated.after(t))
                    act.activation(sk[:], sk[:], ACT.Exp).then_inc(exped.sem, 1)
                    for h in range(SWA_H):
                        cols = slice(h * 2 * P, (h + 1) * 2 * P)
                        act.activation(probs[f.i][:, cols], probs[f.i][:, cols], ACT.Exp, bias=neg[:, h:h + 1],
                                       accum_out=rsum[:, h:h + 1]).then_inc(exped.sem, 1)

            act.preload_act_table(ACT.Exp)
            act.wait_ge(consts_in.sem, 16 * CONSTS)
            act.wait_ge(prepared.sem, PREPARED)
            pipelined(act, prepare, step)

        @blk.vector
        def _(dve):
            def prepare(a):
                t, z = a.t, zt[a.i]
                dve.wait_ge(squared.sem, squared.after(t, 1))
                dve.tensor_reduce(ss[:, 0:NH], heads(sq[:, 0:QK], NH), AX, ALU.add).then_inc(ssum.sem, 1)
                dve.wait_ge(squared.sem, squared.after(t))
                dve.tensor_reduce(ss[:, NH:NH + MEM_H], heads(sq[:, QK:QK + MW], MEM_H), AX,
                                  ALU.add).then_inc(ssum.sem, 1)
                dve.wait_ge(ssum.sem, ssum.after(t))
                dve.tensor_scalar(ss[:, 0:NH], ss[:, 0:NH], 1.0 / SWA_D, EPS, ALU.mult,
                                  ALU.add).then_inc(scaled.sem, 1)
                dve.tensor_scalar(ss[:, NH:NH + MEM_H], ss[:, NH:NH + MEM_H], 1.0 / MEM_D, EPS, ALU.mult,
                                  ALU.add).then_inc(scaled.sem, 1)
                dve.wait_ge(scaled.sem, scaled.after(t))
                inverse_root(dve, rstd, ss, root, rstd_steps, t)
                if not is_tile(t, 0):
                    F1.wait_filled(dve, t - 1, 2)
                for g in range(SWA_KV):
                    dve.tensor_tensor(pairs(qn)[:, :, g, :], heads(z[:, g * 256:(g + 1) * 256], 4),
                                      col(rstd[:, g * 4:(g + 1) * 4], SWA_D), ALU.mult).then_inc(qn_made.sem, 1)
                dve.tensor_tensor(heads(qn[:, SK0:QK], SWA_KV), heads(z[:, SK0:QK], SWA_KV),
                                  col(rstd[:, SWA_H:NH], SWA_D), ALU.mult).then_inc(qn_made.sem, 1)
                dve.tensor_tensor(heads(mqn[:], MEM_H), heads(z[:, MQ0:MQ0 + MW], MEM_H),
                                  col(rstd[:, NH:NH + MEM_H], MEM_D), ALU.mult).then_inc(qn_made.sem, 1)
                dve.wait_ge(roped.sem, roped.after(t))
                if not is_tile(t, 0):
                    dve.wait_ge(kd_made.sem, kd_made.after(t - 1))
                for out, cs, sn in ((rqn, qc, qs), (rkn, kc, ks)):
                    o4, c4, s4 = (a[:].rearrange("p (h a d) -> p h a d", a=2, d=HALF) for a in (out, cs, sn))
                    dve.tensor_tensor(o4[:, :, 0, :], c4[:, :, 0, :], s4[:, :, 1, :],
                                      ALU.subtract).then_inc(rot_made.sem, 1)
                    dve.tensor_tensor(o4[:, :, 1, :], s4[:, :, 0, :], c4[:, :, 1, :],
                                      ALU.add).then_inc(rot_made.sem, 1)

            def window_scores(f, g):
                cols = slice(g * 8 * P, (g + 1) * 8 * P)
                bound = mask_first if is_tile(f.t, 0) else mask
                dve.wait_ge(scored.sem, scored.after(f.t, g + 2))
                dve.tensor_tensor(heads(probs[f.i][:, cols], 4), heads(S_ps[:], 4),
                                  bound[:].unsqueeze(1).to_broadcast([P, 4, 2 * P]), ALU.add).then_inc(masked.sem, 1)
                dve.wait_ge(masked.sem, masked.after(f.t, g + 1))
                dve.tensor_reduce(mx[:, g * 4:g * 4 + 4], heads(probs[f.i][:, cols], 4), AX,
                                  ALU.max).then_inc(maxed.sem, 1)

            def step(a, f, b):
                if b:
                    O.wait_filled(dve, b.t, 0)
                    for h in range(RET_H):
                        region, at = T[h // 2], (h % 2) * RET_DV
                        cols = slice(h * RET_DV, (h + 1) * RET_DV)
                        region.wait_filled(dve, b.t, 0)
                        dve.scalar_tensor_tensor(out=state[:, cols], in0=state[:, cols], scalar=chunk_decay[h],
                                                 in1=region.ps[:, at:at + RET_DV], op0=ALU.mult,
                                                 op1=ALU.add).then_inc(region.taken.sem, 1)
                    for h in range(RET_H):
                        dve.bn_stats(st[:, 6 * h:6 * h + 6], O.ps[:, h * RET_DV:(h + 1) * RET_DV]).then_inc(stated.sem, 1)
                    dve.wait_ge(stated.sem, stated.after(b.t))
                    stand(dve, idle)
                    for h in range(RET_H):
                        dve.bn_aggr(mva[:, 2 * h:2 * h + 2], st[:, 6 * h:6 * h + 6]).then_inc(aggregated.sem, 1)
                if f:
                    t = f.t
                    F2.wait_filled(dve, t, 1)
                    dve.tensor_copy(rqT[:], F2.ps[:, 0:RQ]).then_inc(F2.taken.sem, 1)
                    dve.tensor_tensor(rqdT[:], F2.ps[:, 0:RQ], qdec[:], ALU.mult).then_inc(F2.taken.sem, 1)
                    dve.wait_ge(scored.sem, scored.after(t, 1))
                    dve.tensor_reduce(mmx[:], heads(S_ps[:], MEM_H), AX, ALU.max).then_inc(mmaxed.sem, 1)
                    dve.wait_ge(mmaxed.sem, mmaxed.after(t))
                    dve.tensor_scalar(mneg[:], mmx[:], -1.0, None, ALU.mult).then_inc(mnegated.sem, 1)
                if b:
                    dve.wait_ge(aggregated.sem, aggregated.after(b.t))
                    dve.tensor_scalar(var[:], mva[:].rearrange("p (h a) -> p h a", a=2)[:, :, 1], EPS, None,
                                      ALU.add).then_inc(rscaled.sem, 1)
                    dve.wait_ge(rscaled.sem, rscaled.after(b.t))
                    inverse_root(dve, rr, var, rroot, rroot_steps, b.t)
                if f:
                    F2.wait_filled(dve, t, 2)
                    dve.tensor_tensor(inT[:], F2.ps[:, 0:RET_H * P], decayT[:], ALU.mult).then_inc(F2.taken.sem, 1)
                if b:
                    for h in range(RET_H):
                        cols = slice(h * RET_DV, (h + 1) * RET_DV)
                        dve.tensor_scalar(rnorm[:, cols], O.ps[:, cols], mva[:, 2 * h:2 * h + 1], rr[:, h:h + 1],
                                          ALU.subtract, ALU.mult).then_inc(O.taken.sem, 1)
                    O.wait_taken(dve, b.t, 0)
                    dve.wait_ge(gate_made.sem, gate_made.after(b.t))
                    dve.tensor_tensor(rnorm[:], rnorm[:], gate[:], ALU.mult).then_inc(gated.sem, 1)
                if f:
                    window_scores(f, 0)
                    dve.wait_ge(mexped.sem, mexped.after(t))
                    dve.reciprocal(mrinv[:], mrsum[:]).then_inc(minverted.sem, 1)
                    window_scores(f, 1)
                    dve.wait_ge(maxed.sem, maxed.after(t))
                    dve.tensor_tensor(mx[:], mx[:], sinks[:], ALU.max).then_inc(topped.sem, 1)
                    dve.wait_ge(topped.sem, topped.after(t))
                    dve.tensor_scalar(neg[:], mx[:], -1.0, None, ALU.mult).then_inc(negated.sem, 1)
                    dve.tensor_tensor(sk[:], sinks[:], mx[:], ALU.subtract).then_inc(negated.sem, 1)
                if a:
                    prepare(a)
                if f:
                    dve.wait_ge(rgw_made.sem, rgw_made.after(t))
                    dve.wait_ge(tanh_made.sem, tanh_made.after(t))
                    dve.scalar_tensor_tensor(out=gate[:], in0=tanh[:], scalar=1.0, in1=rgw[:], op0=ALU.add,
                                             op1=ALU.mult).then_inc(gate_made.sem, 1)
                    dve.wait_ge(exped.sem, exped.after(t))
                    dve.tensor_tensor(rinv[:], rsum[:], sk[:], ALU.add).then_inc(dened.sem, 1)
                    dve.wait_ge(dened.sem, dened.after(t))
                    dve.reciprocal(rinv[:], rinv[:]).then_inc(inverted.sem, 1)

            for r in (F1, F2, O, T[0], T[1]):
                r.taken.open(dve)
            masked.open(dve)
            dve.memset(state[:], 0.0).then_inc(prepared.sem, 1)
            dve.memset(kT[1][:], 0.0).then_inc(prepared.sem, 1)
            dve.memset(vals[1][:], 0.0).then_inc(prepared.sem, 1)
            dve.wait_ge(consts_in.sem, 16 * CONSTS)
            dve.tensor_scalar(wq[:], wq[:], float(SWA_D) ** -0.5, None, ALU.mult).then_inc(prepared.sem, 1)
            dve.tensor_scalar(wret[:], wret[:], 0.5, None, ALU.mult).then_inc(prepared.sem, 1)
            pipelined(dve, prepare, step)

        @blk.tensor
        def _(pe):
            def turn(region, t, use, ins):
                region.wait_free(pe, t, use)
                for n, x in enumerate(ins):
                    mm = pe.transpose(region.ps[:, n * P:(n + 1) * P], x, ident[:])
                mm.then_inc(region.filled.sem, 1)

            def cuts(x, first, n):
                return [x[:, j * P:(j + 1) * P] for j in range(first, first + n)]

            def turn_probs(b, quarters):
                for q in quarters:
                    n, use = QUARTERS[q]
                    turn(T[n], b.t, use, cuts(probs[b.i], 4 * q, 4))

            def window_scores(f, g):
                rows = slice(g * SWA_D, (g + 1) * SWA_D)
                for j in range(4):
                    for n, keys in enumerate((kT[1 - f.i], kT[f.i])):
                        at = (2 * j + n) * P
                        mm = pe.matmul(S_ps[:, at:at + P], qT[rows, j * P:(j + 1) * P], keys[rows, :],
                                       start=True, stop=True)
                mm.then_inc(scored.sem, 1)

            def step(a, f, b):
                if b:
                    z = zt[b.i]
                    O.wait_free(pe, b.t, 0)
                    F2.wait_taken(pe, b.t, 2)
                    pe.wait_ge(v_in[b.i].sem, v_in[b.i].after(b.r))
                    for h in range(RET_H):
                        cols = slice(h * RET_DV, (h + 1) * RET_DV)
                        pe.matmul(O.ps[:, cols], inT[:, h * P:(h + 1) * P],
                                  z[:, RV0 + h * RET_DV:RV0 + (h + 1) * RET_DV], start=True, stop=False)
                        mm = pe.matmul(O.ps[:, cols], rqdT[:, h * P:(h + 1) * P], state[:, cols],
                                       start=False, stop=True)
                    mm.then_inc(O.filled.sem, 1)
                    pe.wait_ge(kd_made.sem, kd_made.after(b.t))
                    for n, (region, bt, use) in enumerate(halves(b, 0)):
                        region.wait_free(pe, bt, use)
                        for j in range(2):
                            h = 2 * n + j
                            mm = pe.matmul(region.ps[:, j * RET_DV:(j + 1) * RET_DV],
                                           rkd[b.i][:, h * RET_DK:(h + 1) * RET_DK],
                                           z[:, RV0 + h * RET_DV:RV0 + (h + 1) * RET_DV], start=True, stop=True)
                        mm.then_inc(region.filled.sem, 1)
                if f:
                    t = f.t
                    pe.wait_ge(qn_made.sem, qn_made.after(t))
                    turn(F1, t, 0, cuts(mqn, 0, MEM_H))
                    turn(F2, t, 0, cuts(qn, 4, 1))
                    turn(F1, t, 1, cuts(qn, 0, 4))
                    pe.wait_ge(rot_made.sem, rot_made.after(t))
                    turn(F2, t, 1, cuts(rqn, 0, RET_H))
                    pe.wait_ge(masked.sem, masked.after(t - 1))
                    F1.wait_taken(pe, t, 0)
                    for h in range(MEM_H):
                        mm = pe.matmul(S_ps[:, h * MEM_LEN:(h + 1) * MEM_LEN], mqT[:, h * P:(h + 1) * P],
                                       mkT[:, h, :], start=True, stop=True)
                    mm.then_inc(scored.sem, 1)
                    turn(F1, t, 2, cuts(rkn, 0, RET_H))
                if b:
                    pe.wait_ge(mprobs_made.sem, mprobs_made.after(b.t))
                    for n, (region, bt, use) in enumerate(halves(b, 1)):
                        turn(region, bt, use, cuts(mprobs, 4 * n, 4))
                if f:
                    F1.wait_taken(pe, t, 2)
                    F2.wait_free(pe, t, 2)
                    for h in range(RET_H):
                        cols = slice(h * P, (h + 1) * P)
                        mm = pe.matmul(F2.ps[:, cols], rkT[:, cols], rqT[:, cols], start=True, stop=True)
                    mm.then_inc(F2.filled.sem, 1)
                if b:
                    for region, bt, use in halves(b, 1):
                        region.wait_taken(pe, bt, use)
                    for h in range(MEM_H):
                        for m in range(2):
                            at = (2 * h + m) * P
                            mm = pe.matmul(T[0].ps[:, h * P:(h + 1) * P], mv[:, m, h * MEM_D:(h + 1) * MEM_D],
                                           mprobsT[:, at:at + P], start=(m == 0), stop=(m == 1))
                    mm.then_inc(T[0].filled.sem, 1)
                    pe.wait_ge(probs_made.sem, probs_made.after(b.t))
                    turn_probs(b, (0, 1))
                if f:
                    pe.wait_ge(mexped.sem, mexped.after(t))
                    window_scores(f, 0)
                if b:
                    turn_probs(b, (2, 3))
                if f:
                    pe.wait_ge(masked.sem, masked.after(t, 1))
                    window_scores(f, 1)
                if b:
                    pe.wait_ge(vals_made.sem, vals_made.after(b.t))
                    T[0].wait_taken(pe, b.t, 4)
                    T[1].wait_free(pe, b.t, 4)
                    for h in range(SWA_H):
                        rows = slice((h % 2) * SWA_D, (h % 2 + 1) * SWA_D)
                        dims = slice((h // 4) * SWA_D, (h // 4 + 1) * SWA_D)
                        for n, v in enumerate((vals[1 - b.i], vals[b.i])):
                            at = (2 * h + n) * P
                            mm = pe.matmul(T[1].ps[rows, (h // 2) * P:(h // 2 + 1) * P], v[:, dims],
                                           probsT[:, at:at + P], start=(n == 0), stop=(n == 1))
                    mm.then_inc(T[1].filled.sem, 1)
                    pe.wait_ge(gated.sem, gated.after(b.t))
                    for n, (region, bt, use) in enumerate(halves(b, 5)):
                        turn(region, bt, use, cuts(rnorm, 4 * n, 4))

            pe.wait_ge(prepared.sem, PREPARED)
            pipelined(pe, lambda a: None, step)


def mixer_constants():
    f = np.float32
    half = RET_DK // 2
    inv = (f(1.0) / (f(10000.0) ** (np.arange(half, dtype=f) / f(half)))).astype(f)
    ang = np.arange(S, dtype=f)[:, None] * inv[None, :]
    cs, sn = np.cos(ang).astype(f), np.sin(ang).astype(f)
    ksc = f(RET_DK ** -0.5)
    lg = np.log1p(-(f(2.0) ** (f(-5.0) - np.arange(RET_H, dtype=f)))).astype(f)
    pos = np.arange(P, dtype=f)
    diff = pos[None, :] - pos[:, None]
    dec = np.where(diff[:, None, :] >= 0, np.exp(np.maximum(diff, 0)[:, None, :] * lg[None, :, None]), 0)
    qi, kj = np.arange(P)[:, None], np.arange(2 * P)[None, :]
    gap = P + qi - kj
    mask = np.where((gap >= 0) & (gap < P), 0.0, NEG).astype(f)
    first = np.where(kj < P, f(NEG), mask).astype(f)
    return {
        "rope": np.concatenate([cs, sn, cs * ksc, sn * ksc], axis=1).astype(f),
        "decayT": dec.reshape(P, RET_H * P).astype(f),
        "qdec": np.exp((pos[None, :] + 1) * lg[:, None]).reshape(1, RET_H * P).astype(f),
        "kdec": np.exp((P - 1 - pos[:, None]) * lg[None, :]).astype(f),
        "mask": mask, "mask_first": first,
    }


def project_mixers(nc, io):
    KO = 16
    PARTS = ((0, 4), (4, 12), (12, 16))
    H = 512
    with ExitStack() as c:
        w_hi = c.enter_context(nc.sbuf_tensor("b_hi", [P, KO, D], F32R))
        w_lo = c.enter_context(nc.sbuf_tensor("b_lo", [P, KO, D], F32R))
        raw = [c.enter_context(nc.sbuf_tensor(f"b_raw{i}", [P, KO * P], F32)) for i in range(2)]
        o_hi = [c.enter_context(nc.sbuf_tensor(f"b_ohi{i}", [P, KO * P], F32R)) for i in range(2)]
        o_lo = [c.enter_context(nc.sbuf_tensor(f"b_olo{i}", [P, KO * P], F32R)) for i in range(2)]
        gates = c.enter_context(nc.sbuf_tensor("b_gates", [P, 3 * D], F32))
        part = c.enter_context(nc.sbuf_tensor("b_part", [P, 2, H], F32))
        merged = [c.enter_context(nc.sbuf_tensor(f"b_merged{i}", [P, D], F32)) for i in range(2)]
        acc = [c.enter_context(nc.psum_tensor(f"b_acc{i}", [P, 3, H], F32)) for i in range(2)]
        RING = 4
        w_in = [Signal(io["sems"], nc, f"b_w_in{i}", 16) for i in range(RING)]
        w_hi_made = Signal(io["sems"], nc, "b_w_hi_made")
        w_lo_made = Signal(io["sems"], nc, "b_w_lo_made")
        o_in = [Signal(io["sems"], nc, f"b_o_in{i}", 16) for i in range(2)]
        g_in = Signal(io["sems"], nc, "b_g_in", 16)
        hi_made = Signal(io["sems"], nc, "b_hi_made", 1)
        lo_made = Signal(io["sems"], nc, "b_lo_made", 1, 2)
        opened = Signal(io["sems"], nc, "b_opened")
        summed = Signal(io["sems"], nc, "b_summed", 2, 2)
        gated = Signal(io["sems"], nc, "b_gated", 10, 1)
        m_out = [Signal(io["sems"], nc, f"b_m_out{i}", 16, 1) for i in range(2)]
        blk = c.enter_context(nc.Block())

        def slot(n):
            return (raw[1][:, 0:D], raw[1][:, D:2 * D], merged[0][:], merged[1][:])[n % RING]

        @blk.sync
        def _(sp):
            def load_outputs(t, i):
                sp.wait_ge(lo_made.sem, lo_made.after(t - 2))
                sp.dma_start(raw[i][:], io["oT"][ds(t, 1), :, :].rearrange("a p n -> (a p) n")).then_inc(
                    o_in[i].sem, 16)

            def load_gates(t):
                sp.dma_start(gates[:], io["z"][ds(t * P, P), ZG0:ZW]).then_inc(g_in.sem, 16)

            for m in m_out:
                m.open(sp)
            rows = [(io["w_br_swa"], k) for k in range(4)] + [(io["w_br_ret"], k) for k in range(8)] + [
                (io["w_br_mem"], k) for k in range(4)]
            load_outputs(0, 0)
            for n, (w, k) in enumerate(rows):
                if n >= RING:
                    sp.wait_ge(w_lo_made.sem, n - RING + 1)
                sp.dma_start(slot(n), w[k * P:(k + 1) * P, :]).then_inc(w_in[n % RING].sem, 16)
            load_gates(0)
            sp.wait_ge(w_lo_made.sem, KO)

            def tile(t, i, last=False):
                if not last:
                    load_outputs(t + 1, 1 - i)
                sp.wait_ge(gated.sem, gated.after(t))
                if not last:
                    load_gates(t + 1)
                sp.dma_start(io["merged"][ds(t * P, P), :], merged[i][:]).then_inc(m_out[i].sem, 16)

            with sp.Fori(0, TILES // 2 - 1) as p:
                tile(2 * p, 0)
                tile(2 * p + 1, 1)
            tile(TILES - 2, 0)
            tile(TILES - 1, 1, last=True)
            for i in range(2):
                sp.wait_ge(m_out[i].sem, m_out[i].after(TILES // 2 - 1))

        @blk.scalar
        def _(act):
            def split(t, p, i):
                act.wait_ge(o_in[i].sem, o_in[i].after(p))
                act.wait_ge(summed.sem, summed.after(t - 2))
                act.copy(o_hi[i][:], raw[i][:]).then_inc(hi_made.sem, 1)

            act.preload_act_table(ACT.Sigmoid)
            split(0, 0, 0)
            for n in range(KO):
                act.wait_ge(w_in[n % RING].sem, 16 * (n // RING + 1))
                act.copy(w_hi[:, n, :], slot(n)).then_inc(w_hi_made.sem, 1)
            for p in peeled(act, TILES // 2):
                for i in range(2):
                    t = 2 * p + i
                    if not is_tile(t, 0):
                        split(t, p, i)
                    act.wait_ge(g_in.sem, g_in.after(t))
                    act.activation(gates[:], gates[:], ACT.Sigmoid).then_inc(opened.sem, 1)

        @blk.vector
        def _(dve):
            lo_made.open(dve)
            gated.open(dve)

            def split(t, i):
                dve.wait_ge(hi_made.sem, hi_made.after(t))
                dve.tensor_tensor(o_lo[i][:], raw[i][:], o_hi[i][:].bitcast(F32),
                                  ALU.subtract).then_inc(lo_made.sem, 1)

            split(0, 0)
            for n in range(KO):
                dve.wait_ge(w_hi_made.sem, n + 1)
                dve.tensor_tensor(w_lo[:, n, :], slot(n), w_hi[:, n, :].bitcast(F32),
                                  ALU.subtract).then_inc(w_lo_made.sem, 1)

            def merge(t, p, i):
                dve.wait_ge(opened.sem, opened.after(t))
                dve.wait_ge(m_out[i].sem, m_out[i].after(p - 1))
                for h in range(2):
                    cols = slice(h * H, (h + 1) * H)
                    out = merged[i][:, cols]
                    n = 5 * h
                    dve.wait_ge(summed.sem, summed.after(t, h + 1))
                    dve.tensor_tensor(out, gates[:, h * H:(h + 1) * H], acc[h][:, 0, :],
                                      ALU.mult).then_inc(gated.sem, 1)
                    dve.wait_ge(gated.sem, gated.after(t - 1) if h == 0 else gated.after(t, 5))
                    for b in (1, 2):
                        dve.tensor_tensor(part[:, b - 1, :], gates[:, b * D + h * H:b * D + (h + 1) * H],
                                          acc[h][:, b, :], ALU.mult).then_inc(gated.sem, 1)
                    for b in (1, 2):
                        dve.wait_ge(gated.sem, gated.after(t, n + 2 + b))
                        dve.tensor_tensor(out, out, part[:, b - 1, :], ALU.add).then_inc(gated.sem, 1)

            with dve.Fori(0, TILES // 2 - 1) as p:
                split(2 * p + 1, 1)
                merge(2 * p, p, 0)
                split(2 * p + 2, 0)
                merge(2 * p + 1, p, 1)
            split(TILES - 1, 1)
            merge(TILES - 2, TILES // 2 - 1, 0)
            merge(TILES - 1, TILES // 2 - 1, 1)

        @blk.tensor
        def _(pe):
            summed.open(pe)

            def products(i, h, b, chunks, now):
                return three_pass(pe, acc[h][:, b, :],
                                  lambda k: o_hi[i][:, k * P:(k + 1) * P],
                                  lambda k: o_lo[i][:, k * P:(k + 1) * P],
                                  lambda k: w_hi[:, k, h * H:(h + 1) * H],
                                  lambda k: w_lo[:, k, h * H:(h + 1) * H], chunks, now)

            for p in peeled(pe, TILES // 2):
                for i in range(2):
                    t = 2 * p + i
                    pe.wait_ge(lo_made.sem, lo_made.after(t))
                    if is_tile(t, 0):
                        for b, (k0, k1) in enumerate(PARTS):
                            for n in range(k0, k1, 4):
                                pe.wait_ge(w_lo_made.sem, n + 4)
                                for h in range(2):
                                    mm = products(i, h, b, range(k0, k1), range(n, n + 4))
                                    if n + 4 == KO:
                                        mm.then_inc(summed.sem, 1)
                    else:
                        for h in range(2):
                            pe.wait_ge(gated.sem, gated.after(t - 1, 5 * (h + 1)))
                            for b, (k0, k1) in enumerate(PARTS):
                                mm = products(i, h, b, range(k0, k1), range(k0, k1))
                            mm.then_inc(summed.sem, 1)


BLOCK_TILES = 4
C = 512
UP = 2 * FF // C
SLICES = UP + D // C
SLOTS = E * S
EXPERT, LIVE, FIRST, COUNT, PRIOR = range(5)
BLOCK_COLS = 8
MAX_TILES = E + S * TOPK // P
MAX_BLOCKS = E + S * TOPK // (BLOCK_TILES * P)


def expert_weights(io, s, e, k):
    rows = slice(k * P, (k + 1) * P)
    if s < UP:
        return io["w_up"][ds(e, 1), rows, s * C:(s + 1) * C].rearrange("a p n -> (a p) n")
    return io["w_down"][ds(e, 1), rows, (s - UP) * C:(s - UP + 1) * C].rearrange("a p n -> (a p) n")


def finish_mixing(nc, io, ident, blocks, ahead):
    H = 512
    RING = 4
    with ExitStack() as c:
        def sb(name, shape, dt=F32):
            return c.enter_context(nc.sbuf_tensor(f"f_{name}", shape, dt))

        w_hi, w_lo = sb("whi", [P, KD, D], F32R), sb("wlo", [P, KD, D], F32R)
        wraw = [sb(f"wraw{i}", [P, D]) for i in range(RING)]
        mg = [sb(f"mg{i}", [P, D]) for i in range(2)]
        xs = [sb(f"x{i}", [P, D]) for i in range(2)]
        m_hi = [sb(f"mhi{i}", [P, D], F32R) for i in range(2)]
        m_lo = [sb(f"mlo{i}", [P, D], F32R) for i in range(2)]
        x1 = [sb(f"x1{i}", [P, D]) for i in range(2)]
        h2 = [sb(f"h2{i}", [P, D]) for i in range(2)]
        h2T = sb("h2T", [P, D])
        sq, wb = sb("sq", [P, D]), sb("wb", [P, D])
        wr, br = sb("wr", [P, KD, E]), sb("br", [P, E])
        ss, mean, root, rstd = sb("ss", [P, 2]), sb("mean", [P, 1]), sb("root", [P, 1]), sb("rstd", [P, 1])
        logits, top, topi = sb("logits", [P, E]), sb("top", [P, 8]), sb("topi", [P, 8], U32)
        ntop, ex, exs, exr = sb("ntop", [P, 1]), sb("ex", [P, TOPK]), sb("exs", [P, 1]), sb("exr", [P, 1])
        topf, onehot, sel = sb("topf", [P, TOPK]), sb("onehot", [P, TOPK, E]), sb("sel", [P, E])
        taken = sb("taken", [P, E])
        base, place, slotf = sb("base", [P, E]), sb("place", [P, TOPK, E]), sb("slotf", [P, TOPK])
        slots = [sb(f"slots{i}", [P, TOPK], U32) for i in range(2)]
        recs = [sb(f"recs{i}", [P, TOPK, 2], I32) for i in range(2)]
        tokf = sb("tokf", [P, TOPK])
        before, ones = sb("before", [P, P]), sb("ones", [P, P])
        ef, e0f, lane = sb("ef", [P, E]), sb("e0f", [P, E]), sb("lane", [P, 1])
        fill = sb("fill", [P, SLOTS // P, 2], I32)
        zero = sb("zero", [P, D])
        cnt, tl, nb, cum = sb("cnt", [P, E], I32), sb("tl", [P, E], I32), sb("nb", [P, E], I32), sb("cum", [P, E])
        tlf, nbf, le, tmp, zer = sb("tlf", [P, E]), sb("nbf", [P, E]), sb("le", [P, E]), sb("tmp", [P, E]), sb("zer", [P, E])
        col = sb("col", [P, 8])
        rowi = sb("rowi", [P, BLOCK_COLS], I32)
        mT = c.enter_context(nc.psum_tensor("f_mT", [P, D], F32))
        hT = c.enter_context(nc.psum_tensor("f_hT", [P, D], F32))
        acc = c.enter_context(nc.psum_tensor("f_acc", [P, D], F32))
        lgp = c.enter_context(nc.psum_tensor("f_lgp", [P, 512], F32))
        rkp = c.enter_context(nc.psum_tensor("f_rkp", [P, 512], F32))

        def sig(name, per=1, ahead=0):
            return Signal(io["sems"], nc, f"f_{name}", per, ahead)

        consts_in, idle = sig("consts_in", 16), sig("idle")
        w_in = [sig(f"w_in{i}", 16) for i in range(RING)]
        w_hi_made, w_lo_made = sig("w_hi_made"), sig("w_lo_made")
        made = sig("made")
        filled = sig("filled", 16)
        ahead_in = sig("ahead_in", 16)
        mg_in = [sig(f"mg_in{i}", 16) for i in range(2)]
        x_in = [sig(f"x_in{i}", 16) for i in range(2)]
        turned, hi_made, lo_made, summed = sig("turned", 1, 2), sig("hi_made"), sig("lo_made", 1, 1), sig("summed", 2, 2)
        x1_made, squared, meaned, root_steps, h2_made = (
            sig("x1_made", 2, 2), sig("squared"), sig("meaned"), sig("root_steps", 10), sig("h2_made"))
        x1_out = [sig(f"x1_out{i}", 16, 1) for i in range(2)]
        h2_out = [sig(f"h2_out{i}", 16, 1) for i in range(2)]
        h2_turned, h2T_made, scored = sig("h2_turned", 1, 2), sig("h2T_made", 1, 2), sig("scored", 1, 2)
        biased, ranked, exped, steps, sel_made = (
            sig("biased", 1, 2), sig("ranked", 2, 2), sig("exped", 1, 2), sig("steps", 11, 2), sig("sel_made", 1, 2))
        placed, slotted = sig("placed", 1, 2), sig("slotted", 1, 2)
        sent = [sig(f"sent{i}", 16 * TOPK) for i in range(2)]
        counted, row_made, row_out, blocks_in = sig("counted"), sig("row_made"), sig("row_out", 16), sig("blocks_in", 16)
        blk = c.enter_context(nc.Block())

        @blk.sync
        def _(sp):
            def load_weights(k):
                if k >= RING:
                    sp.wait_ge(w_lo_made.sem, k - RING + 1)
                sp.dma_start(wraw[k % RING][:], io["w_out"][k * P:(k + 1) * P, :]).then_inc(w_in[k % RING].sem, 16)

            def load_merged(t, i):
                sp.wait_ge(turned.sem, turned.after(t - 2))
                sp.dma_start(mg[i][:], io["merged"][ds(t * P, P), :]).then_inc(mg_in[i].sem, 16)

            load_merged(0, 0)
            for k in range(RING):
                load_weights(k)
            for dst, src in ((wb[:], io["ffn_norm_w"].to_broadcast([P, D])),
                             (wr[:], io["w_router"].rearrange("(k p) e -> p k e", p=P)),
                             (br[:], io["b_router"].to_broadcast([P, E]))):
                sp.dma_start(dst, src).then_inc(consts_in.sem, 16)
            for x in (*x1_out, *h2_out):
                x.open(sp)

            def load_x(t, i):
                sp.wait_ge(x1_made.sem, x1_made.after(t - 2))
                sp.dma_start(xs[i][:], io["x"][ds(t * P, P), :]).then_inc(x_in[i].sem, 16)

            def store(t, i):
                sp.wait_ge(x1_made.sem, x1_made.after(t))
                sp.dma_start(io["sum"][ds(t * P, P), :], x1[i][:]).then_inc(x1_out[i].sem, 16)
                sp.wait_ge(h2_made.sem, h2_made.after(t))
                sp.dma_start(io["h2"][ds(t * P, P), :], h2[i][:]).then_inc(h2_out[i].sem, 16)

            for k in range(RING, KD):
                load_weights(k)
            load_merged(1, 1)
            load_x(0, 0)
            with sp.Fori(0, TILES // 2 - 1) as p:
                for i in range(2):
                    t = 2 * p + i
                    load_merged(t + 2, i)
                    load_x(t + 1, 1 - i)
                    store(t, i)
            load_x(TILES - 1, 1)
            for k in range(KD):
                sp.dma_start(ahead[:, k, :], expert_weights(io, 0, 0, k)).then_inc(ahead_in.sem, 16)
            store(TILES - 2, 0)
            store(TILES - 1, 1)
            sp.wait_ge(row_made.sem, 1)
            sp.dma_start(io["blocks"][1:P + 1, :], rowi[:]).then_inc(row_out.sem, 16)
            sp.dma_start(io["blocks"][0:1, :], zero[0:1, 0:BLOCK_COLS].bitcast(I32)).then_inc(row_out.sem, 16)
            sp.wait_ge(row_out.sem, 32)
            sp.dma_start(blocks[:], io["blocks"].rearrange("(a b) w -> a (b w)", a=1)).then_inc(blocks_in.sem, 16)
            sp.wait_ge(blocks_in.sem, 16)
            sp.wait_ge(ahead_in.sem, 16 * KD)
            for s in (*x1_out, *h2_out):
                sp.wait_ge(s.sem, s.after(TILES // 2 - 1))

        @blk.gpsimd
        def _(pool):
            for s in (scored, h2T_made, biased, ranked, exped, steps, sel_made, placed, slotted):
                s.open(pool)
            pool.iota(ef[:], pattern=[[1, E]], base=0, channel_multiplier=0,
                      allow_small_or_imprecise_dtypes=True).then_inc(made.sem, 1)
            pool.iota(e0f[:], pattern=[[S, E]], base=0, channel_multiplier=0,
                      allow_small_or_imprecise_dtypes=True).then_inc(made.sem, 1)
            pool.iota(lane[:], pattern=[[0, 1]], base=0, channel_multiplier=1,
                      allow_small_or_imprecise_dtypes=True).then_inc(made.sem, 1)
            pool.iota(tokf[:], pattern=[[0, TOPK]], base=0, channel_multiplier=1,
                      allow_small_or_imprecise_dtypes=True).then_inc(made.sem, 1)
            pool.memset(ones[:], 1.0).then_inc(made.sem, 1)
            pool.memset(before[:], 1.0).then_inc(made.sem, 1)
            pool.memset(taken[:], 0.0).then_inc(made.sem, 1)
            pool.memset(zer[:], 0.0).then_inc(made.sem, 1)
            pool.memset(zero[:], 0.0).then_inc(made.sem, 1)
            pool.memset(fill[:], 0).then_inc(made.sem, 1)
            pool.wait_ge(made.sem, 10)
            pool.affine_select(out=before[:], in_=before[:], compare_op=ALU.is_gt, fill=0.0, base=0,
                               pattern=[[1, P]], channel_multiplier=-1).then_inc(made.sem, 1)
            pool.iota(fill[:, :, 0], pattern=[[0, SLOTS // P // P], [1, P]], base=S,
                      channel_multiplier=0).then_inc(made.sem, 1)
            pool.wait_ge(made.sem, 12)
            pool.dma_start(io["slots"].rearrange("(p a) w -> p a w", p=P), fill[:]).then_inc(filled.sem, 16)
            pool.dma_start(io["sum"][S:S + PAD, :], zero[:]).then_inc(filled.sem, 16)
            pool.dma_start(io["h2"][S:S + PAD, :], zero[:]).then_inc(filled.sem, 16)
            pool.wait_ge(filled.sem, 48)

            def send(t, i):
                pool.wait_ge(slotted.sem, slotted.after(t))
                stand(pool, idle)
                for k in range(TOPK):
                    pool.indirect_dma_start(
                        out=io["slots"], out_offset=bass.IndirectOffsetOnAxis(ap=slots[i][:, k:k + 1], axis=0),
                        in_=recs[i][:, k, :], in_offset=None).then_inc(sent[i].sem, 16)

            for p in peeled(pool, TILES // 2):
                for i in range(2):
                    if not at_first(p):
                        send(2 * p + i - 2, i)
            send(TILES - 2, 0)
            send(TILES - 1, 1)
            for s in sent:
                pool.wait_ge(s.sem, s.after(TILES // 2 - 1))

        @blk.scalar
        def _(act):
            act.preload_act_table(ACT.Exp)

            def split(t, i):
                act.wait_ge(turned.sem, turned.after(t))
                act.wait_ge(summed.sem, summed.after(t - 2))
                act.copy(m_hi[i][:], mT[:]).then_inc(hi_made.sem, 1)

            def take_h2(t):
                act.wait_ge(h2_turned.sem, h2_turned.after(t))
                act.wait_ge(scored.sem, scored.after(t - 1))
                act.copy(h2T[:], hT[:]).then_inc(h2T_made.sem, 1)

            def weigh(t):
                act.wait_ge(steps.sem, steps.after(t, 1))
                act.activation(ex[:], top[:, 0:TOPK], ACT.Exp, bias=ntop[:, 0:1],
                               accum_out=exs[:]).then_inc(exped.sem, 1)

            split(0, 0)
            for k in range(KD):
                act.wait_ge(w_in[k % RING].sem, 16 * (k // RING + 1))
                act.copy(w_hi[:, k, :], wraw[k % RING][:]).then_inc(w_hi_made.sem, 1)
            for p in peeled_ends(act, TILES // 2):
                for i in range(2):
                    t = 2 * p + i
                    if not is_tile(t, 0):
                        take_h2(t - 1)
                    if not is_tile(t, TILES - 1):
                        split(t + 1, 1 - i)
                    act.wait_ge(x1_made.sem, x1_made.after(t))
                    if not is_tile(t, 0):
                        act.wait_ge(squared.sem, squared.after(t - 1))
                    act.activation(sq[:], x1[i][:], ACT.Square, accum_out=ss[:, i:i + 1]).then_inc(squared.sem, 1)
                    if not is_tile(t, 0):
                        weigh(t - 1)
            take_h2(TILES - 1)
            weigh(TILES - 1)

        @blk.vector
        def _(dve):
            lo_made.open(dve)
            x1_made.open(dve)

            def step(t, n, ins):
                ins.then_inc(steps.sem, 1)
                dve.wait_ge(steps.sem, steps.after(t, n))

            def choose(t, q, i):
                dve.wait_ge(scored.sem, scored.after(t))
                dve.tensor_tensor(logits[:], lgp[:, 0:E], br[:], ALU.add).then_inc(biased.sem, 1)
                dve.wait_ge(biased.sem, biased.after(t))
                stand(dve, idle)
                dve.max(top[:], logits[:]).then_inc(ranked.sem, 1)
                dve.wait_ge(ranked.sem, ranked.after(t, 1))
                stand(dve, idle)
                dve.max_index(topi[:], top[:], logits[:]).then_inc(ranked.sem, 1)
                step(t, 1, dve.tensor_scalar(ntop[:], top[:, 0:1], -1.0, None, ALU.mult))
                dve.wait_ge(ranked.sem, ranked.after(t))
                step(t, 2, dve.tensor_copy(topf[:], topi[:, 0:TOPK]))
                step(t, 3, dve.tensor_tensor(onehot[:], ef[:].unsqueeze(1).to_broadcast([P, TOPK, E]),
                                             topf[:].unsqueeze(2).to_broadcast([P, TOPK, E]), ALU.is_equal))
                dve.tensor_reduce(sel[:], onehot[:].rearrange("p k e -> p e k"), AX, ALU.add).then_inc(sel_made.sem, 1)
                dve.wait_ge(exped.sem, exped.after(t))
                step(t, 4, dve.reciprocal(exr[:], exs[:]))
                dve.wait_ge(sent[i].sem, sent[i].after(q - 1))
                step(t, 5, dve.tensor_scalar(recs[i][:, :, 1].bitcast(F32), ex[:], exr[:, 0:1], None, ALU.mult))
                step(t, 6, dve.tensor_copy(recs[i][:, :, 0], tokf[:]))
                step(t, 7, dve.tensor_scalar(tokf[:], tokf[:], float(P), None, ALU.add))

            def find_slots(t, i):
                dve.wait_ge(placed.sem, placed.after(t))
                step(t, 8, dve.tensor_tensor(base[:], rkp[:, 0:E], e0f[:], ALU.add))
                step(t, 9, dve.tensor_tensor(place[:], onehot[:],
                                             base[:].unsqueeze(1).to_broadcast([P, TOPK, E]), ALU.mult))
                step(t, 10, dve.tensor_reduce(slotf[:], place[:], AX, ALU.add))
                dve.tensor_copy(slots[i][:], slotf[:]).then_inc(slotted.sem, 1)
                step(t, 11, dve.tensor_tensor(taken[:], taken[:], sel[:], ALU.add))

            def split(t, i):
                dve.wait_ge(hi_made.sem, hi_made.after(t))
                dve.wait_ge(summed.sem, summed.after(t - 2))
                dve.tensor_tensor(m_lo[i][:], mT[:], m_hi[i][:].bitcast(F32), ALU.subtract).then_inc(lo_made.sem, 1)

            def add_x(t, i, h):
                cols = slice(h * H, (h + 1) * H)
                dve.wait_ge(summed.sem, summed.after(t, h + 1))
                dve.tensor_tensor(x1[i][:, cols], acc[:, cols], xs[i][:, cols], ALU.add).then_inc(x1_made.sem, 1)

            split(0, 0)
            for k in range(KD):
                dve.wait_ge(w_hi_made.sem, k + 1)
                dve.tensor_tensor(w_lo[:, k, :], wraw[k % RING][:], w_hi[:, k, :].bitcast(F32),
                                  ALU.subtract).then_inc(w_lo_made.sem, 1)
            dve.wait_ge(consts_in.sem, 48)
            dve.wait_ge(made.sem, 12)
            for p in peeled_ends(dve, TILES // 2):
                for i in range(2):
                    t = 2 * p + i
                    dve.wait_ge(x_in[i].sem, x_in[i].after(p))
                    dve.wait_ge(x1_out[i].sem, x1_out[i].after(p - 1))
                    add_x(t, i, 0)
                    if not is_tile(t, TILES - 1):
                        split(t + 1, 1 - i)
                    add_x(t, i, 1)
                    if not (is_tile(t, 0) or is_tile(t, 1)):
                        find_slots(t - 2, i)
                    dve.wait_ge(squared.sem, squared.after(t))
                    dve.tensor_scalar(mean[:], ss[:, i:i + 1], 1.0 / D, EPS, ALU.mult, ALU.add).then_inc(meaned.sem, 1)
                    dve.wait_ge(meaned.sem, meaned.after(t))
                    inverse_root(dve, rstd, mean, root, root_steps, t)
                    dve.wait_ge(h2_out[i].sem, h2_out[i].after(p - 1))
                    dve.wait_ge(h2_turned.sem, h2_turned.after(t - 2))
                    dve.scalar_tensor_tensor(out=h2[i][:], in0=x1[i][:], scalar=rstd[:, 0:1], in1=wb[:],
                                             op0=ALU.mult, op1=ALU.mult).then_inc(h2_made.sem, 1)
                    if not is_tile(t, 0):
                        choose(t - 1, p - 1 if i == 0 else p, 1 - i)
            find_slots(TILES - 2, 0)
            choose(TILES - 1, TILES // 2 - 1, 1)
            find_slots(TILES - 1, 1)

            n = 0

            def link(ins):
                nonlocal n
                n += 1
                ins.then_inc(counted.sem, 1)
                dve.wait_ge(counted.sem, n + 1)

            dve.wait_ge(counted.sem, 1)
            link(dve.tensor_copy(cnt[:], rkp[:, 0:E]))
            link(dve.tensor_scalar(cnt[:], cnt[:], P - 1, None, ALU.add))
            link(dve.tensor_scalar(tl[:], cnt[:], 7, None, ALU.arith_shift_right))
            link(dve.tensor_scalar(nb[:], tl[:], BLOCK_TILES - 1, None, ALU.add))
            link(dve.tensor_scalar(nb[:], nb[:], 2, None, ALU.arith_shift_right))
            link(dve.tensor_scalar(nb[:], nb[:], 1, None, ALU.max))
            link(dve.tensor_copy(tlf[:], tl[:]))
            link(dve.tensor_copy(nbf[:], nb[:]))
            link(dve.tensor_tensor_scan(cum[:], nbf[:], zer[:], 0.0, ALU.add, ALU.add))
            link(dve.tensor_scalar(le[:], cum[:], lane[:, 0:1], None, ALU.is_le))
            link(dve.tensor_reduce(col[:, 0:1], le[:], AX, ALU.add))
            link(dve.tensor_tensor(tmp[:], le[:], nbf[:], ALU.mult))
            link(dve.tensor_reduce(col[:, 1:2], tmp[:], AX, ALU.add))
            link(dve.tensor_scalar(tmp[:], ef[:], col[:, 0:1], None, ALU.is_equal))
            link(dve.tensor_tensor(tmp[:], tmp[:], tlf[:], ALU.mult))
            link(dve.tensor_reduce(col[:, 2:3], tmp[:], AX, ALU.add))
            link(dve.tensor_tensor(col[:, 3:4], lane[:], col[:, 1:2], ALU.subtract))
            link(dve.tensor_scalar(col[:, 4:5], col[:, 3:4], float(-BLOCK_TILES), None, ALU.mult))
            link(dve.tensor_tensor(col[:, 4:5], col[:, 4:5], col[:, 2:3], ALU.add))
            link(dve.tensor_scalar(col[:, 4:5], col[:, 4:5], 0.0, float(BLOCK_TILES), ALU.max, ALU.min))
            link(dve.tensor_scalar(col[:, 5:6], col[:, 0:1], float(E - 1), None, ALU.min))
            link(dve.tensor_scalar(col[:, 6:7], col[:, 5:6], float(S), None, ALU.mult))
            link(dve.scalar_tensor_tensor(out=col[:, 6:7], in0=col[:, 3:4], scalar=float(BLOCK_TILES * P),
                                          in1=col[:, 6:7], op0=ALU.mult, op1=ALU.add))
            link(dve.tensor_scalar(col[:, 6:7], col[:, 6:7], float(SLOTS - BLOCK_TILES * P), None, ALU.min))
            link(dve.tensor_tensor(tmp[:], le[:], tlf[:], ALU.mult))
            link(dve.tensor_reduce(col[:, 7:8], tmp[:], AX, ALU.add))
            link(dve.scalar_tensor_tensor(out=col[:, 7:8], in0=col[:, 3:4], scalar=float(BLOCK_TILES),
                                          in1=col[:, 7:8], op0=ALU.mult, op1=ALU.add))
            link(dve.tensor_scalar(col[:, 7:8], col[:, 7:8], float(MAX_TILES), None, ALU.min))
            link(dve.memset(rowi[:], 0))
            link(dve.tensor_copy(rowi[:, PRIOR:PRIOR + 1], col[:, 7:8]))
            link(dve.tensor_copy(rowi[:, EXPERT:EXPERT + 1], col[:, 5:6]))
            link(dve.tensor_copy(rowi[:, LIVE:LIVE + 1], col[:, 4:5]))
            link(dve.tensor_copy(rowi[:, FIRST:FIRST + 1], col[:, 6:7]))
            dve.tensor_copy(rowi[:, COUNT:COUNT + 1], cum[:, E - 1:E]).then_inc(row_made.sem, 1)

        @blk.tensor
        def _(pe):
            summed.open(pe)
            turned.open(pe)
            h2_turned.open(pe)

            def gemm(i, h, now=None):
                return three_pass(pe, acc[:, h * H:(h + 1) * H],
                                  lambda k: m_hi[i][:, k * P:(k + 1) * P], lambda k: m_lo[i][:, k * P:(k + 1) * P],
                                  lambda k: w_hi[:, k, h * H:(h + 1) * H], lambda k: w_lo[:, k, h * H:(h + 1) * H],
                                  range(KD), now)

            def turn_h2(t, i):
                pe.wait_ge(h2_made.sem, h2_made.after(t))
                pe.wait_ge(h2T_made.sem, h2T_made.after(t - 1))
                for k in range(KD):
                    mm = pe.transpose(hT[:, k * P:(k + 1) * P], h2[i][:, k * P:(k + 1) * P], ident[:])
                mm.then_inc(h2_turned.sem, 1)

            def score(t):
                pe.wait_ge(h2T_made.sem, h2T_made.after(t))
                pe.wait_ge(biased.sem, biased.after(t - 1))
                for k in range(KD):
                    mm = pe.matmul(lgp[:, 0:E], h2T[:, k * P:(k + 1) * P], wr[:, k, :],
                                   start=(k == 0), stop=(k == KD - 1))
                mm.then_inc(scored.sem, 1)

            def prefix(t):
                pe.wait_ge(sel_made.sem, sel_made.after(t))
                pe.wait_ge(steps.sem, steps.after(t - 1))
                pe.matmul(rkp[:, 0:E], before[:], sel[:], start=True, stop=False)
                pe.matmul(rkp[:, 0:E], ones[:], taken[:], start=False, stop=True).then_inc(placed.sem, 1)

            def turn_merged(t, r, i):
                pe.wait_ge(mg_in[i].sem, mg_in[i].after(r))
                pe.wait_ge(lo_made.sem, lo_made.after(t - 1))
                for k in range(KD):
                    mm = pe.transpose(mT[:, k * P:(k + 1) * P], mg[i][:, k * P:(k + 1) * P], ident[:])
                mm.then_inc(turned.sem, 1)

            turn_merged(0, 0, 0)
            for p in peeled_ends(pe, TILES // 2):
                for i in range(2):
                    t = 2 * p + i
                    pe.wait_ge(lo_made.sem, lo_made.after(t))
                    if is_tile(t, 0):
                        for k in range(0, KD, 2):
                            pe.wait_ge(w_lo_made.sem, k + 2)
                            for h in range(2):
                                mm = gemm(i, h, range(k, k + 2))
                                if k + 2 == KD:
                                    mm.then_inc(summed.sem, 1)
                        turn_merged(1, 0, 1)
                        pe.wait_ge(consts_in.sem, 48)
                        pe.wait_ge(made.sem, 12)
                        continue
                    pe.wait_ge(x1_made.sem, x1_made.after(t - 1, 1))
                    gemm(i, 0).then_inc(summed.sem, 1)
                    turn_h2(t - 1, 1 - i)
                    if not is_tile(t, TILES - 1):
                        turn_merged(t + 1, p + i, 1 - i)
                    if not is_tile(t, 1):
                        prefix(t - 2)
                    pe.wait_ge(x1_made.sem, x1_made.after(t - 1))
                    gemm(i, 1).then_inc(summed.sem, 1)
                    score(t - 1)
            prefix(TILES - 2)
            turn_h2(TILES - 1, 1)
            score(TILES - 1)
            prefix(TILES - 1)
            pe.wait_ge(steps.sem, steps.after(TILES - 1))
            pe.matmul(rkp[:, 0:E], ones[:], taken[:], start=True, stop=True).then_inc(counted.sem, 1)


def run_experts(nc, io, ident, blocks, raw):
    HC = C // 2
    with ExitStack() as c:
        def sb(name, shape, dt=F32):
            return c.enter_context(nc.sbuf_tensor(f"e_{name}", shape, dt))

        w_hi = [sb(f"whi{i}", [P, KD, C], F32R) for i in range(2)]
        w_lo = [sb(f"wlo{i}", [P, KD, C], F32R) for i in range(2)]
        bias = sb("bias", [P, SLICES, C])
        xg = [sb(f"xg{i}", [P, D]) for i in range(BLOCK_TILES)]
        x_hi = [sb(f"xhi{i}", [P, D], F32R) for i in range(BLOCK_TILES)]
        x_lo = [sb(f"xlo{i}", [P, D], F32R) for i in range(BLOCK_TILES)]
        a_hi = [sb(f"ahi{i}", [P, FF], F32R) for i in range(BLOCK_TILES)]
        a_lo = [sb(f"alo{i}", [P, FF], F32R) for i in range(BLOCK_TILES)]
        hid = [sb(f"hid{i}", [P, C]) for i in range(2)]
        glu = [sb(f"glu{i}", [P, HC]) for i in range(2)]
        sg = [sb(f"sg{i}", [P, HC]) for i in range(2)]
        lin = [sb(f"lin{i}", [P, HC]) for i in range(2)]
        av = [sb(f"av{i}", [P, HC]) for i in range(BLOCK_TILES)]
        ys = [sb(f"ys{i}", [P, D]) for i in range(BLOCK_TILES)]
        rec_in, rec_now, rec_out = (sb(f"rec_{n}", [P, BLOCK_TILES, 2], I32) for n in ("in", "now", "out"))
        acc = [c.enter_context(nc.psum_tensor(f"e_acc{i}", [P, C], F32)) for i in range(BLOCK_TILES)]
        aT = [c.enter_context(nc.psum_tensor(f"e_aT{i}", [P, C], F32)) for i in range(2)]
        xT = c.enter_context(nc.psum_tensor("e_xT", [P, D], F32))

        def sig(name, per=1, ahead=0):
            return Signal(io["sems"], nc, f"e_{name}", per, ahead)

        CH = SLICES * KD
        w_in = [sig(f"w_in{k}", 16 * SLICES) for k in range(KD)]
        b_in = [sig(f"b_in{s}", 16) for s in range(SLICES)]
        hi_made, lo_made = sig("hi_made", CH), sig("lo_made", CH, 1)
        rec_loaded, rec_kept, rec_moved, idle = sig("rec_loaded", 16), sig("rec_kept"), sig("rec_moved"), sig("idle")
        x_in, x_turned, x_hi_made, x_lo_made = sig("x_in"), sig("x_turned"), sig("x_hi_made"), sig("x_lo_made")
        y_sent = sig("y_sent")
        up_summed, hid_made, glu_made, sg_made, lin_made, gl_made, av_made, a_turned, a_hi_made, a_lo_made = (
            sig(n) for n in ("up_summed", "hid_made", "glu_made", "sg_made", "lin_made", "gl_made", "av_made",
                             "a_turned", "a_hi_made", "a_lo_made"))
        down_summed, y_made, y_gated = sig("down_summed"), sig("y_made"), sig("y_gated")
        y_copied = sig("y_copied")
        blk = c.enter_context(nc.Block())

        class Block:

            def __init__(self, eng, row):
                self.eng, self.row = eng, row
                self.live = self.get(LIVE, BLOCK_TILES)
                self.prior = self.get(PRIOR, MAX_TILES)

            def get(self, column, top):
                return self.eng.value_load(blocks[0:1, ds(self.row * BLOCK_COLS + column, 1)], min_val=0, max_val=top)

            def up(self, s, i):
                return self.prior * UP + self.live * s + i

            def down(self, s, i):
                return self.prior * (SLICES - UP) + self.live * (s - UP) + i

            def each(self):
                for i in range(BLOCK_TILES):
                    with self.eng.If(self.live > i):
                        yield i

            def tile(self, i):
                return self.eng.If(self.live > i)

        def count(eng):
            return eng.value_load(blocks[0:1, BLOCK_COLS + COUNT:BLOCK_COLS + COUNT + 1], min_val=1, max_val=MAX_BLOCKS)

        @blk.sync
        def _(sp):
            def load_slice(b, s, e, prior):
                for k in range(KD):
                    if at_first(b):
                        sp.sem_inc(w_in[k].sem, 16)
                        continue
                    sp.wait_ge(lo_made.sem, lo_made.after(b, (s - 1) * KD + k + 1))
                    sp.dma_start(raw[:, k, :], expert_weights(io, s, e, k)).then_inc(w_in[k].sem, 16)
                if s < UP:
                    sp.wait_ge(hid_made.sem, prior * UP)
                    src = io["b_up"][ds(e, 1), s * C:(s + 1) * C]
                else:
                    sp.wait_ge(y_made.sem, prior * (SLICES - UP))
                    src = io["b_down"][ds(e, 1), (s - UP) * C:(s - UP + 1) * C]
                sp.dma_start(bias[:, s, :], src.to_broadcast([P, C])).then_inc(b_in[s].sem, 16)

            def load_records(row):
                first = sp.value_load(blocks[0:1, ds(row * BLOCK_COLS + FIRST, 1)], min_val=0,
                                      max_val=SLOTS - BLOCK_TILES * P)
                sp.dma_start(rec_in[:], io["slots"][ds(first, BLOCK_TILES * P), :].rearrange(
                    "(i p) w -> p i w", p=P)).then_inc(rec_loaded.sem, 16)

            load_records(1)
            load_slice(0, 0, 0, 0)
            with sp.Fori(0, count(sp)) as b:
                now = Block(sp, b + 1)
                e = now.get(EXPERT, E - 1)
                for s in range(1, SLICES):
                    load_slice(b, s, e, now.prior)
                    if s == 1:
                        sp.wait_ge(x_in.sem, (now.prior + now.live) * 16)
                        sp.wait_ge(rec_kept.sem, b + 1)
                        load_records(b + 2)
                following = Block(sp, b + 2)
                load_slice(b + 1, 0, following.get(EXPERT, E - 1), following.prior)
            last = Block(sp, count(sp))
            sp.wait_ge(y_sent.sem, (last.prior + last.live) * 16)
            for q in range(4):
                rows = slice(q * S // 4, (q + 1) * S // 4)
                sp.dma_start(io["out"][rows, :], io["sum"][rows, :]).then_inc(y_copied.sem, 16)
            sp.wait_ge(y_copied.sem, 64)

        @blk.gpsimd
        def _(pool):
            def gather(b, block):
                pool.wait_ge(rec_loaded.sem, (b + 1) * 16)
                pool.wait_ge(x_turned.sem, block.prior)
                stand(pool, idle)
                for i in block.each():
                    pool.indirect_dma_start(
                        out=xg[i][:], out_offset=None, in_=io["h2"],
                        in_offset=bass.IndirectOffsetOnAxis(ap=rec_in[:, i, 0:1].bitcast(U32), axis=0)).then_inc(
                            x_in.sem, 16)

            def scatter(block, i):
                with block.tile(i):
                    pool.wait_ge(y_gated.sem, block.down(SLICES - 1, i) + 1)
                    pool.wait_ge(y_sent.sem, (block.prior + i) * 16)
                    pool.wait_ge(rec_moved.sem, block.row)
                    stand(pool, idle)
                    pool.indirect_dma_start(
                        out=io["sum"], out_offset=bass.IndirectOffsetOnAxis(ap=rec_out[:, i, 0:1].bitcast(U32), axis=0),
                        in_=ys[i][:], in_offset=None, compute_op=ALU.add).then_inc(y_sent.sem, 16)

            def move_records(row, before):
                pool.wait_ge(y_sent.sem, before.prior * 16)
                stand(pool, idle)
                pool.tensor_copy(rec_out[:], rec_now[:]).then_inc(rec_moved.sem, 1)
                pool.wait_ge(rec_moved.sem, row + 1)
                stand(pool, idle)

            pool.memset(rec_now[:], 0).then_inc(idle.sem, 1)
            pool.wait_ge(idle.sem, 1)
            gather(0, Block(pool, 1))
            with pool.Fori(0, count(pool)) as b:
                before, now = Block(pool, b), Block(pool, b + 1)
                move_records(b, before)
                pool.wait_ge(y_gated.sem, now.prior * (SLICES - UP))
                pool.wait_ge(rec_loaded.sem, (b + 1) * 16)
                pool.wait_ge(x_in.sem, (now.prior + now.live) * 16)
                stand(pool, idle)
                pool.tensor_copy(rec_now[:], rec_in[:]).then_inc(rec_kept.sem, 1)
                for s in range(UP):
                    for i in now.each():
                        n = now.up(s, i)
                        pool.wait_ge(hid_made.sem, n + 1)
                        pool.wait_ge(av_made.sem, n if i == 0 else n - 1)
                        stand(pool, idle)
                        pool.tensor_scalar(lin[i % 2][:], hid[i % 2][:].rearrange("p (n a) -> p n a", a=2)[:, :, 1],
                                           LIMIT, -LIMIT, ALU.min, ALU.max).then_inc(lin_made.sem, 1)
                    if s == 1:
                        gather(b + 1, Block(pool, b + 2))
                    scatter(before, s)
            last = Block(pool, count(pool))
            move_records(count(pool), last)
            for i in range(BLOCK_TILES):
                scatter(last, i)

        @blk.scalar
        def _(act):
            def split(b, s, free):
                for k in range(KD):
                    act.wait_ge(w_in[k].sem, w_in[k].after(b, 16 * (s + 1)))
                    if k == 0:
                        act.wait_ge(*free)
                    act.copy(w_hi[s % 2][:, k, :], raw[:, k, :]).then_inc(hi_made.sem, 1)

            def split_x(block, i, ups):
                act.wait_ge(x_turned.sem, block.prior + i + 1)
                act.wait_ge(up_summed.sem, ups)
                act.copy(x_hi[i][:], xT[:]).then_inc(x_hi_made.sem, 1)

            def split_a(block, s, i):
                n = block.up(s, i)
                act.wait_ge(a_turned.sem, n + 1)
                act.wait_ge(down_summed.sem, block.prior * (SLICES - UP))
                act.copy(a_hi[i][:, s * HC:(s + 1) * HC], aT[i % 2][:, 0:HC]).then_inc(a_hi_made.sem, 1)

            def gate(block, s, i):
                act.wait_ge(y_made.sem, block.down(s, i) + 1)
                act.wait_ge(rec_kept.sem, block.row)
                cols = ys[i][:, (s - UP) * C:(s - UP + 1) * C]
                act.activation(cols, cols, ACT.Copy, scale=rec_now[:, i, 1:2].bitcast(F32)).then_inc(y_gated.sem, 1)

            act.preload_act_table(ACT.Sigmoid)
            split(0, 0, (up_summed.sem, 0))
            first = Block(act, 1)
            for i in first.each():
                split_x(first, i, 0)
            with act.Fori(0, count(act)) as b:
                now = Block(act, b + 1)
                for s in range(UP):
                    split(b, s + 1, (down_summed.sem, now.down(UP, 0)) if s == 0 else (up_summed.sem, now.up(s, 0)))
                    for i in now.each():
                        if s > 0:
                            split_a(now, s - 1, i)
                        act.wait_ge(glu_made.sem, now.up(s, i) + 1)
                        act.activation(sg[i % 2][:], glu[i % 2][:], ACT.Sigmoid, scale=ALPHA).then_inc(sg_made.sem, 1)
                    if s == 1:
                        following = Block(act, b + 2)
                with now.tile(0):
                    split_a(now, UP - 1, 0)
                for i in range(BLOCK_TILES):
                    with following.tile(i):
                        split_x(following, i, now.up(UP, 0))
                    if i + 1 < BLOCK_TILES:
                        with now.tile(i + 1):
                            split_a(now, UP - 1, i + 1)
                    if i == 0:
                        split(b, UP + 1, (up_summed.sem, now.up(UP, 0)))
                    with now.tile(i):
                        gate(now, UP, i)
                split(b + 1, 0, (down_summed.sem, now.down(UP + 1, 0)))
                for i in now.each():
                    gate(now, UP + 1, i)

        @blk.vector
        def _(dve):
            lo_made.open(dve)

            def split(b, s):
                for k in range(KD):
                    dve.wait_ge(hi_made.sem, hi_made.after(b, s * KD + k + 1))
                    dve.tensor_tensor(w_lo[s % 2][:, k, :], raw[:, k, :], w_hi[s % 2][:, k, :].bitcast(F32),
                                      ALU.subtract).then_inc(lo_made.sem, 1)

            def split_x(block, i):
                dve.wait_ge(x_hi_made.sem, block.prior + i + 1)
                dve.tensor_tensor(x_lo[i][:], xT[:], x_hi[i][:].bitcast(F32), ALU.subtract).then_inc(x_lo_made.sem, 1)

            def split_a(block, s, i):
                cols = slice(s * HC, (s + 1) * HC)
                dve.wait_ge(a_hi_made.sem, block.up(s, i) + 1)
                dve.tensor_tensor(a_lo[i][:, cols], aT[i % 2][:, 0:HC], a_hi[i][:, cols].bitcast(F32),
                                  ALU.subtract).then_inc(a_lo_made.sem, 1)

            def finish_down(b, block, s, i):
                dve.wait_ge(down_summed.sem, block.down(s, i) + 1)
                dve.wait_ge(b_in[s].sem, b_in[s].after(b))
                dve.wait_ge(y_sent.sem, block.prior * 16)
                dve.tensor_tensor(ys[i][:, (s - UP) * C:(s - UP + 1) * C], acc[i][:], bias[:, s, :],
                                  ALU.add).then_inc(y_made.sem, 1)

            split(0, 0)
            first = Block(dve, 1)
            for i in first.each():
                split_x(first, i)
            with dve.Fori(0, count(dve)) as b:
                now = Block(dve, b + 1)
                for s in range(UP):
                    split(b, s + 1)
                    for i in now.each():
                        n = now.up(s, i)
                        dve.wait_ge(up_summed.sem, n + 1)
                        dve.wait_ge(b_in[s].sem, b_in[s].after(b))
                        dve.wait_ge(lin_made.sem, n if i == 0 else n - 1)
                        dve.tensor_tensor(hid[i % 2][:], acc[i][:], bias[:, s, :], ALU.add).then_inc(hid_made.sem, 1)
                        dve.wait_ge(hid_made.sem, n + 1)
                        dve.tensor_scalar(glu[i % 2][:], hid[i % 2][:].rearrange("p (n a) -> p n a", a=2)[:, :, 0],
                                          LIMIT, None, ALU.min).then_inc(glu_made.sem, 1)
                        if s > 0:
                            split_a(now, s - 1, i)
                        dve.wait_ge(sg_made.sem, n + 1)
                        dve.tensor_tensor(glu[i % 2][:], glu[i % 2][:], sg[i % 2][:], ALU.mult).then_inc(gl_made.sem, 1)
                        dve.wait_ge(gl_made.sem, n + 1)
                        dve.wait_ge(lin_made.sem, n + 1)
                        if s > 0:
                            dve.wait_ge(a_turned.sem, now.up(s - 1, i) + 1)
                        dve.scalar_tensor_tensor(out=av[i][:], in0=lin[i % 2][:], scalar=1.0, in1=glu[i % 2][:],
                                                 op0=ALU.add, op1=ALU.mult).then_inc(av_made.sem, 1)
                    if s == 1:
                        following = Block(dve, b + 2)
                with now.tile(0):
                    split_a(now, UP - 1, 0)
                for i in range(BLOCK_TILES):
                    with following.tile(i):
                        split_x(following, i)
                    if i + 1 < BLOCK_TILES:
                        with now.tile(i + 1):
                            split_a(now, UP - 1, i + 1)
                    if i == 0:
                        split(b, UP + 1)
                    with now.tile(i):
                        finish_down(b, now, UP, i)
                split(b + 1, 0)
                for i in now.each():
                    finish_down(b, now, UP + 1, i)

        @blk.tensor
        def _(pe):
            def turn_x(block, i):
                pe.wait_ge(x_in.sem, (block.prior + block.live) * 16)
                pe.wait_ge(x_lo_made.sem, block.prior + i)
                for k in range(KD):
                    mm = pe.transpose(xT[:, k * P:(k + 1) * P], xg[i][:, k * P:(k + 1) * P], ident[:])
                mm.then_inc(x_turned.sem, 1)

            def turn_a(block, s, i):
                n = block.up(s, i)
                pe.wait_ge(av_made.sem, n + 1)
                pe.wait_ge(a_lo_made.sem, n if i == 0 else n - 1)
                for k in range(HC // P):
                    mm = pe.transpose(aT[i % 2][:, k * P:(k + 1) * P], av[i][:, k * P:(k + 1) * P], ident[:])
                mm.then_inc(a_turned.sem, 1)

            def product(s, i, hi, lo):
                return three_pass(pe, acc[i][:], lambda k: hi[i][:, k * P:(k + 1) * P],
                                  lambda k: lo[i][:, k * P:(k + 1) * P],
                                  lambda k: w_hi[s % 2][:, k, :], lambda k: w_lo[s % 2][:, k, :], range(KD))

            first = Block(pe, 1)
            for i in first.each():
                turn_x(first, i)
            with pe.Fori(0, count(pe)) as b:
                before, now = Block(pe, b), Block(pe, b + 1)
                for s in range(UP):
                    pe.wait_ge(lo_made.sem, lo_made.after(b, (s + 1) * KD))
                    for i in range(BLOCK_TILES):
                        if s == 0:
                            with before.tile(i):
                                pe.wait_ge(y_made.sem, before.down(SLICES - 1, i) + 1)
                                stand(pe, idle)
                        with now.tile(i):
                            if s == 0:
                                pe.wait_ge(x_lo_made.sem, now.prior + i + 1)
                            else:
                                pe.wait_ge(hid_made.sem, now.up(s - 1, i) + 1)
                            product(s, i, x_hi, x_lo).then_inc(up_summed.sem, 1)
                            if s > 0:
                                turn_a(now, s - 1, i)
                    if s == 1:
                        following = Block(pe, b + 2)
                with now.tile(0):
                    turn_a(now, UP - 1, 0)
                for s in (UP, UP + 1):
                    for i in range(BLOCK_TILES):
                        if s == UP:
                            with following.tile(i):
                                turn_x(following, i)
                            if i + 1 < BLOCK_TILES:
                                with now.tile(i + 1):
                                    turn_a(now, UP - 1, i + 1)
                        if i == 0:
                            pe.wait_ge(lo_made.sem, lo_made.after(b, (s + 1) * KD))
                            stand(pe, idle)
                        with now.tile(i):
                            if s == UP:
                                pe.wait_ge(a_lo_made.sem, now.up(UP - 1, i) + 1)
                                pe.wait_ge(hid_made.sem, now.up(UP - 1, i) + 1)
                            else:
                                pe.wait_ge(y_made.sem, now.down(UP, i) + 1)
                            product(s, i, a_hi, a_lo).then_inc(down_summed.sem, 1)


def build(nc, io):
    def scratch(name, shape, dt=F32):
        return nc.dram_tensor(name, shape, dt, kind="Internal").ap()

    io = dict(io)
    sems = io["sems"] = []
    io["z"] = scratch("z", (S, ZW))
    io["oT"] = scratch("oT", (TILES, P, 16 * P))
    io["merged"] = scratch("merged", (S, D))
    io["sum"] = scratch("sum", (S + PAD, D))
    io["h2"] = scratch("h2", (S + PAD, D))
    io["slots"] = scratch("slots", (SLOTS, 2), I32)
    io["blocks"] = scratch("blocks", (P + 1, BLOCK_COLS), I32)
    with ExitStack() as c:
        ident = c.enter_context(nc.sbuf_tensor("ident", [P, P], F32))
        eps = c.enter_context(nc.sbuf_tensor("eps", [P, 1], F32))
        with ExitStack() as s:
            hT_hi = s.enter_context(nc.sbuf_tensor("hT_hi", [P, KD, S], F32R))
            hT_lo = s.enter_context(nc.sbuf_tensor("hT_lo", [P, KD, S], F32R))
            norm_inputs(nc, io, hT_hi, hT_lo, ident, eps)
            end_stage(nc, sems)
            project_inputs(nc, io, hT_hi, hT_lo)
            end_stage(nc, sems)
        with ExitStack() as s:
            mkT = s.enter_context(nc.sbuf_tensor("mkT", [P, MEM_H, MEM_LEN], F32))
            mv = s.enter_context(nc.sbuf_tensor("mv", [P, MEM_LEN // P, MEM_H * MEM_D], F32))
            prepare_memory(nc, io, ident, eps, mkT, mv)
            end_stage(nc, sems)
            mix_tokens(nc, io, ident, mkT, mv)
            end_stage(nc, sems)
        project_mixers(nc, io)
        end_stage(nc, sems)
        with ExitStack() as s:
            blocks = s.enter_context(nc.sbuf_tensor("blocks_row", [1, (P + 1) * BLOCK_COLS], I32))
            raw = s.enter_context(nc.sbuf_tensor("e_raw", [P, KD, C], F32))
            finish_mixing(nc, io, ident, blocks, raw)
            end_stage(nc, sems)
            run_experts(nc, io, ident, blocks, raw)


_INS = ["x", "mem", "mix_norm_w", "mem_norm_w", "w_in", "swa_q_norm_w", "swa_k_norm_w", "swa_sinks", "ret_norm_w",
        "w_mem_kv", "mem_q_norm_w", "mem_k_norm_w", "w_br_swa", "w_br_ret", "w_br_mem", "w_out", "ffn_norm_w",
        "w_router", "b_router", "w_up", "b_up", "w_down", "b_down"]
_MATRICES = {"x", "mem", "w_in", "w_mem_kv", "w_br_swa", "w_br_ret", "w_br_mem", "w_out", "w_router", "w_up", "b_up",
             "w_down", "b_down"}


def kernel(**inputs):
    import numpy as _np
    import concourse.bacc as _bacc
    from concourse import mybir as _mybir
    from concourse.bass_utils import run_bass_kernel_spmd as _run

    nc = _bacc.Bacc("TRN2", target_bir_lowering=False, num_devices=1)
    arrays, io = {}, {}
    given = {name: _np.ascontiguousarray(inputs[name]) for name in _INS}
    for name in _MATRICES:
        given[name] = given[name][0]
    given.update(mixer_constants())
    for name, a in given.items():
        arrays[f"in_{name}"] = a
        io[name] = nc.dram_tensor(f"in_{name}", a.shape, _mybir.dt.from_np(a.dtype), kind="ExternalInput").ap()
    io["out"] = nc.dram_tensor("out_0", (S, D), _mybir.dt.float32, kind="ExternalOutput").ap()
    build(nc, io)
    r = _run(nc, [arrays], core_ids=[0])
    return r.results[0]["out_0"].reshape(1, S, D)
```
